# Optimizing a Trainium2 kernel written in Bass

```python
import jax, jax.numpy as jnp
from jax import lax
import numpy as np
import math

D_MODEL = 1024
BATCH = 1
SEQ = 512
DEPTH = 2

HGRN_HEADS = 4
HGRN_KEY = 128
HGRN_VAL = 128
HGRN_KW = HGRN_HEADS * HGRN_KEY
HGRN_VW = HGRN_HEADS * HGRN_VAL
HGRN_CHUNK = 64
POOL_WINDOWS = (2, 4, 8, 16)
POOL_GROUP = 128
POOL_WIDTH = POOL_GROUP * len(POOL_WINDOWS)
FOX_HEADS = 16
FOX_HEAD_DIM = 64
FOX_WIDTH = FOX_HEADS * FOX_HEAD_DIM
FOX_BLOCK = 128
EVEN_IN = 2 * HGRN_KW + 2 * HGRN_VW + 2 * POOL_WIDTH
EVEN_MIX = HGRN_VW + POOL_WIDTH
ODD_IN = 4 * FOX_WIDTH + FOX_HEADS
N_EVEN = (DEPTH + 1) // 2
N_ODD = DEPTH // 2
EPS = 1e-6


def rms_norm(x, g):
    xf = x.astype(jnp.float32)
    y = xf * lax.rsqrt(jnp.mean(xf * xf, axis=-1, keepdims=True) + EPS)
    return (y * g.astype(jnp.float32)).astype(x.dtype)

def hgrn2_chunked(q, k, v, logf):
    b_, s_, h_, kd = q.shape
    vd = v.shape[-1]
    nc = s_ // HGRN_CHUNK

    def to_chunks(t):
        return t.reshape(b_, nc, HGRN_CHUNK, h_, t.shape[-1]).transpose(1, 0, 3, 2, 4)

    causal = jnp.tril(jnp.ones((HGRN_CHUNK, HGRN_CHUNK), dtype=bool))

    def step(state, inp):
        qc, kc, vc, gc = inp
        cum = jnp.cumsum(gc, axis=2)
        diff = cum[:, :, :, None, :] - cum[:, :, None, :, :]
        decay = jnp.where(causal[:, :, None], jnp.exp(jnp.minimum(diff, 0.0)), 0.0)
        scores = jnp.einsum('bhtk,bhsk,bhtsk->bhts', qc, kc, decay)
        out = (jnp.einsum('bhts,bhsv->bhtv', scores, vc)
               + jnp.einsum('bhtk,bhkv->bhtv', qc * jnp.exp(cum), state))
        last = cum[:, :, -1:, :]
        state = (jnp.exp(last[:, :, 0, :])[..., None] * state
                 + jnp.einsum('bhsk,bhsv->bhkv', kc * jnp.exp(last - cum), vc))
        return state, out

    s0 = jnp.zeros((b_, h_, kd, vd), jnp.float32)
    _, out = lax.scan(step, s0, (to_chunks(q), to_chunks(k), to_chunks(v), to_chunks(logf)))
    return out.transpose(1, 0, 3, 2, 4).reshape(b_, s_, h_, vd)

def multiscale_pool(u):
    b_, s_, _ = u.shape
    groups = u.reshape(b_, s_, len(POOL_WINDOWS), POOL_GROUP)
    csum = jnp.cumsum(groups, axis=1)
    csum = jnp.concatenate([jnp.zeros_like(csum[:, :1]), csum], axis=1)
    pos = jnp.arange(s_)
    outs = []
    for gi, w in enumerate(POOL_WINDOWS):
        cg = csum[:, :, gi]
        lagged = jnp.concatenate([jnp.zeros((b_, w - 1, POOL_GROUP), cg.dtype), cg[:, :s_ - w + 1]], axis=1)
        count = jnp.minimum(pos + 1, w).astype(cg.dtype)[None, :, None]
        outs.append((cg[:, 1:] - lagged) / count - groups[:, :, gi])
    return jnp.stack(outs, axis=2)

def even_mixer(h, w_in, lower, onorm_g, pool_w, pool_scale, w_out):
    b_, s_, _ = h.shape
    proj = (h @ w_in).astype(jnp.float32)
    cuts = [HGRN_KW, 2 * HGRN_KW, 2 * HGRN_KW + HGRN_VW, 2 * HGRN_KW + 2 * HGRN_VW,
            2 * HGRN_KW + 2 * HGRN_VW + POOL_WIDTH]
    q, f, i, g_a, u, g_b = jnp.split(proj, cuts, axis=-1)
    lb = lower.astype(jnp.float32)
    forget = lb + (1.0 - lb) * jax.nn.sigmoid(f)
    logf = jnp.log(forget)
    key = 1.0 - forget
    kh = lambda t: t.reshape(b_, s_, HGRN_HEADS, HGRN_KEY)
    o_a = hgrn2_chunked(kh(q), kh(key), i.reshape(b_, s_, HGRN_HEADS, HGRN_VAL), kh(logf))
    o_a = rms_norm(o_a, onorm_g.reshape(HGRN_HEADS, HGRN_VAL)).reshape(b_, s_, HGRN_VW) * jax.nn.silu(g_a)
    pooled = multiscale_pool(u)
    o_b = jnp.einsum('bsgc,gcd->bsgd', pooled, pool_w.astype(jnp.float32)).reshape(b_, s_, POOL_WIDTH)
    o_b = o_b * pool_scale.astype(jnp.float32) * jax.nn.silu(g_b)
    mixed = jnp.concatenate([o_a, o_b], axis=-1).astype(h.dtype)
    return mixed @ w_out

def odd_mixer(h, w_in, b_f, qnorm_g, knorm_g, w_out):
    b_, s_, _ = h.shape
    proj = (h @ w_in).astype(jnp.float32)
    q, k, v, g, fl = jnp.split(proj, [FOX_WIDTH, 2 * FOX_WIDTH, 3 * FOX_WIDTH, 4 * FOX_WIDTH], axis=-1)
    hd = lambda t: t.reshape(b_, s_, FOX_HEADS, FOX_HEAD_DIM)
    q = rms_norm(hd(q), qnorm_g).transpose(0, 2, 1, 3)
    k = rms_norm(hd(k), knorm_g).transpose(0, 2, 1, 3)
    v = hd(v).transpose(0, 2, 1, 3)
    logf = jax.nn.log_sigmoid(fl + b_f.astype(jnp.float32))
    cumf = jnp.cumsum(logf, axis=1).transpose(0, 2, 1)
    scale = FOX_HEAD_DIM ** -0.5
    outs = []
    for blk in range(s_ // FOX_BLOCK):
        q0 = blk * FOX_BLOCK
        q1 = q0 + FOX_BLOCK
        logits = (jnp.einsum('bhqd,bhkd->bhqk', q[:, :, q0:q1], k[:, :, :q1]) * scale
                  + cumf[:, :, q0:q1, None] - cumf[:, :, None, :q1])
        mask = jnp.arange(q0, q1)[:, None] >= jnp.arange(q1)[None, :]
        probs = jax.nn.softmax(jnp.where(mask, logits, -jnp.inf), axis=-1)
        outs.append(jnp.einsum('bhqk,bhkd->bhqd', probs, v[:, :, :q1]))
    o = jnp.concatenate(outs, axis=2).transpose(0, 2, 1, 3).reshape(b_, s_, FOX_WIDTH)
    o = o * jax.nn.silu(g)
    return o.astype(h.dtype) @ w_out

def first_inputs(seed: int = 0) -> dict:
    key = jax.random.key(seed)
    ks = jax.random.split(key, 16)
    nrm = jax.random.normal
    f32 = jnp.float32
    return {
        'x': nrm(ks[0], (BATCH, SEQ, D_MODEL), f32),
        'c': nrm(ks[1], (BATCH, D_MODEL), f32),
        'norm_g': 1.0 + 0.05 * nrm(ks[2], (DEPTH, D_MODEL), f32),
        'ada_w': 0.5 * D_MODEL ** -0.5 * nrm(ks[3], (DEPTH, D_MODEL, 3 * D_MODEL), f32),
        'ada_b': 0.02 * nrm(ks[4], (DEPTH, 3 * D_MODEL), f32),
        'hgrn_lb': 0.1 * nrm(ks[5], (DEPTH + 1, HGRN_KW), f32),
        'even_w_in': D_MODEL ** -0.5 * nrm(ks[6], (N_EVEN, D_MODEL, EVEN_IN), f32),
        'hgrn_onorm_g': 1.0 + 0.05 * nrm(ks[7], (N_EVEN, HGRN_VW), f32),
        'pool_w': POOL_GROUP ** -0.5 * nrm(ks[8], (N_EVEN, len(POOL_WINDOWS), POOL_GROUP, POOL_GROUP), f32),
        'pool_scale': 1.0 + 0.05 * nrm(ks[9], (N_EVEN, POOL_WIDTH), f32),
        'even_w_out': EVEN_MIX ** -0.5 * nrm(ks[10], (N_EVEN, EVEN_MIX, D_MODEL), f32),
        'odd_w_in': D_MODEL ** -0.5 * nrm(ks[11], (N_ODD, D_MODEL, ODD_IN), f32),
        'fox_b_f': jax.random.uniform(ks[12], (N_ODD, FOX_HEADS), f32, 1.0, 4.0),
        'fox_qnorm_g': 1.0 + 0.05 * nrm(ks[13], (N_ODD, FOX_HEAD_DIM), f32),
        'fox_knorm_g': 1.0 + 0.05 * nrm(ks[14], (N_ODD, FOX_HEAD_DIM), f32),
        'odd_w_out': FOX_WIDTH ** -0.5 * nrm(ks[15], (N_ODD, FOX_WIDTH, D_MODEL), f32),
    }

def first_block(x, c, norm_g, ada_w, ada_b, hgrn_lb, even_w_in, hgrn_onorm_g, pool_w, pool_scale,
              even_w_out, odd_w_in, fox_b_f, fox_qnorm_g, fox_knorm_g, odd_w_out):
    lower = jnp.cumsum(jax.nn.softmax(hgrn_lb.astype(jnp.float32), axis=0), axis=0)
    cond = jax.nn.silu(c)
    for l in range(DEPTH):
        mod = cond @ ada_w[l] + ada_b[l]
        shift, scale, gate = jnp.split(mod, 3, axis=-1)
        h = rms_norm(x, norm_g[l]) * (1.0 + scale[:, None, :]) + shift[:, None, :]
        j = l // 2
        if l % 2 == 0:
            y = even_mixer(h, even_w_in[j], lower[l], hgrn_onorm_g[j], pool_w[j], pool_scale[j], even_w_out[j])
        else:
            y = odd_mixer(h, odd_w_in[j], fox_b_f[j], fox_qnorm_g[j], fox_knorm_g[j], odd_w_out[j])
        x = x + gate[:, None, :] * y
    return x


N_MIXERS = 3
CHUNK = 64
D_FF = 2816
LN_EPS = 1e-5
NORM_EPS = 1e-6
DN_ALPHA = (2 * DEPTH) ** 0.25
DN_BETA = (8 * DEPTH) ** -0.25

GLA_HEADS = 4
GLA_DK = D_MODEL // (2 * GLA_HEADS)
GLA_DV = D_MODEL // GLA_HEADS
GLA_KEY = GLA_HEADS * GLA_DK
GLA_VAL = GLA_HEADS * GLA_DV
GLA_RANK = 16
GLA_TAU = 16.0
GLA_SPLITS = (GLA_KEY, GLA_KEY, GLA_VAL, GLA_VAL, GLA_RANK)

RET_HEADS = 4
RET_DK = D_MODEL // RET_HEADS
RET_DV = 2 * D_MODEL // RET_HEADS
RET_KEY = RET_HEADS * RET_DK
RET_VAL = RET_HEADS * RET_DV
RET_SPLITS = (RET_KEY, RET_KEY, RET_VAL, RET_VAL)
ROPE_BASE = 10000.0

SSD_INNER = 2 * D_MODEL
SSD_HEADDIM = 64
SSD_HEADS = SSD_INNER // SSD_HEADDIM
SSD_GROUPS = 4
SSD_HPG = SSD_HEADS // SSD_GROUPS
SSD_STATE = 128
SSD_CONV = 4
SSD_CONV_DIM = SSD_INNER + 2 * SSD_GROUPS * SSD_STATE
SSD_SPLITS = (SSD_INNER, SSD_CONV_DIM, SSD_HEADS)

N_LAYERS_A = len(range(0, DEPTH, N_MIXERS))
N_LAYERS_B = len(range(1, DEPTH, N_MIXERS))
N_LAYERS_C = len(range(2, DEPTH, N_MIXERS))


def split_cols(t, sizes):
    return jnp.split(t, np.cumsum(sizes)[:-1].tolist(), axis=-1)

def layer_norm(x, g, b):
    xf = x.astype(jnp.float32)
    mu = xf.mean(-1, keepdims=True)
    var = jnp.square(xf - mu).mean(-1, keepdims=True)
    return ((xf - mu) * lax.rsqrt(var + LN_EPS)).astype(x.dtype) * g + b

def rms_norm_2(x, g):
    xf = x.astype(jnp.float32)
    ms = jnp.square(xf).mean(-1, keepdims=True)
    return (xf * lax.rsqrt(ms + NORM_EPS)).astype(x.dtype) * g

def head_group_norm(x, g):
    xf = x.astype(jnp.float32)
    mu = xf.mean(-1, keepdims=True)
    var = jnp.square(xf - mu).mean(-1, keepdims=True)
    return ((xf - mu) * lax.rsqrt(var + NORM_EPS)).astype(x.dtype) * g

def swiglu(x, w_in, w_out):
    gate, up = jnp.split(x @ w_in, 2, axis=-1)
    return (jax.nn.silu(gate) * up) @ w_out

def to_chunks(t):
    b, l = t.shape[:2]
    t = t.reshape((b, l // CHUNK, CHUNK) + t.shape[2:])
    return jnp.moveaxis(t, 1, 0)

def from_chunks(t):
    t = jnp.moveaxis(t, 0, 1)
    return t.reshape((t.shape[0], t.shape[1] * t.shape[2]) + t.shape[3:])

def rotary(t):
    l, dh = t.shape[1], t.shape[-1]
    inv = ROPE_BASE ** (-jnp.arange(0, dh, 2, dtype=jnp.float32) / dh)
    ang = jnp.arange(l, dtype=jnp.float32)[:, None] * inv[None, :]
    cos = jnp.cos(ang)[None, :, None, :].astype(t.dtype)
    sin = jnp.sin(ang)[None, :, None, :].astype(t.dtype)
    t1, t2 = jnp.split(t, 2, axis=-1)
    return jnp.concatenate([t1 * cos - t2 * sin, t1 * sin + t2 * cos], axis=-1)

def gla_chunked(q, k, v, log_a):
    bsz = q.shape[0]
    mask = jnp.tril(jnp.ones((CHUNK, CHUNK), dtype=bool))

    def step(state, inp):
        qc, kc, vc, ac = inp
        cum = jnp.cumsum(ac, axis=1)
        tot = cum[:, -1]
        q_dec = qc * jnp.exp(cum)
        k_inv = kc * jnp.exp(-cum)
        k_end = kc * jnp.exp(tot[:, None] - cum)
        s = jnp.where(mask, jnp.einsum('bihd,bjhd->bhij', q_dec, k_inv), 0.0)
        o = jnp.einsum('bhij,bjhv->bihv', s, vc) + jnp.einsum('bihd,bhdv->bihv', q_dec, state)
        state = jnp.exp(tot)[..., None] * state + jnp.einsum('bjhd,bjhv->bhdv', k_end, vc)
        return state, o

    state0 = jnp.zeros((bsz, GLA_HEADS, GLA_DK, GLA_DV), jnp.float32)
    _, o = lax.scan(step, state0, (to_chunks(q), to_chunks(k), to_chunks(v), to_chunks(log_a)))
    return from_chunks(o).astype(v.dtype)

def gla_mixer(x, w_in, w_gate, b_gate, norm_g, w_out):
    bsz, l, _ = x.shape
    q, k, v, r, g_low = split_cols(x @ w_in, GLA_SPLITS)
    q = q.reshape(bsz, l, GLA_HEADS, GLA_DK) * GLA_DK ** -0.5
    k = k.reshape(bsz, l, GLA_HEADS, GLA_DK)
    v = v.reshape(bsz, l, GLA_HEADS, GLA_DV)
    log_a = jax.nn.log_sigmoid((g_low @ w_gate + b_gate).astype(jnp.float32)) / GLA_TAU
    log_a = log_a.reshape(bsz, l, GLA_HEADS, GLA_DK)
    o = rms_norm_2(gla_chunked(q, k, v, log_a), norm_g)
    return (o.reshape(bsz, l, GLA_VAL) * jax.nn.silu(r)) @ w_out

def retention_chunked(q, k, v):
    bsz = q.shape[0]
    log_g = jnp.log(1.0 - 2.0 ** (-5.0 - jnp.arange(RET_HEADS, dtype=jnp.float32)))
    idx = jnp.arange(CHUNK, dtype=jnp.float32)
    mask = jnp.tril(jnp.ones((CHUNK, CHUNK), dtype=bool))
    decay_intra = jnp.where(mask[None], jnp.exp((idx[:, None] - idx[None, :])[None] * log_g[:, None, None]), 0.0)
    decay_q = jnp.exp((idx + 1.0)[:, None] * log_g[None, :])[None, :, :, None]
    decay_k = jnp.exp((CHUNK - 1.0 - idx)[:, None] * log_g[None, :])[None, :, :, None]
    decay_chunk = jnp.exp(CHUNK * log_g)[None, :, None, None]

    def step(state, inp):
        qc, kc, vc = inp
        s = jnp.einsum('bihd,bjhd->bhij', qc, kc) * decay_intra
        o = jnp.einsum('bhij,bjhv->bihv', s, vc) + jnp.einsum('bihd,bhdv->bihv', qc, state) * decay_q
        state = decay_chunk * state + jnp.einsum('bjhd,bjhv->bhdv', kc * decay_k, vc)
        return state, o

    state0 = jnp.zeros((bsz, RET_HEADS, RET_DK, RET_DV), jnp.float32)
    _, o = lax.scan(step, state0, (to_chunks(q), to_chunks(k), to_chunks(v)))
    return from_chunks(o).astype(v.dtype)

def retention_mixer(x, w_in, norm_g, w_out):
    bsz, l, _ = x.shape
    q, k, v, g = split_cols(x @ w_in, RET_SPLITS)
    q = rotary(q.reshape(bsz, l, RET_HEADS, RET_DK))
    k = rotary(k.reshape(bsz, l, RET_HEADS, RET_DK)) * RET_DK ** -0.5
    v = v.reshape(bsz, l, RET_HEADS, RET_DV)
    o = head_group_norm(retention_chunked(q, k, v), norm_g)
    return (o.reshape(bsz, l, RET_VAL) * jax.nn.silu(g)) @ w_out

def causal_dwconv(t, w, b):
    ch = t.shape[-1]
    y = lax.conv_general_dilated(t, w[:, None, :].astype(t.dtype), window_strides=(1,),
                                 padding=[(SSD_CONV - 1, 0)],
                                 dimension_numbers=('NWC', 'WIO', 'NWC'),
                                 feature_group_count=ch)
    return y + b

def ssd_chunked(xs, dt, a, bm, cm):
    bsz = xs.shape[0]
    mask = jnp.tril(jnp.ones((CHUNK, CHUNK), dtype=bool))[None, :, :, None, None]

    def step(state, inp):
        xc, dtc, bc, cc = inp
        cum = jnp.cumsum(dtc * a, axis=1)
        seg = jnp.exp(jnp.where(mask, cum[:, :, None] - cum[:, None, :], -jnp.inf))
        cb = jnp.einsum('bign,bjgn->bijg', cc, bc)
        w = seg * cb[..., None] * dtc[:, None]
        y = jnp.einsum('bijge,bjgep->bigep', w, xc)
        y = y + jnp.einsum('bign,bgepn->bigep', cc, state) * jnp.exp(cum)[..., None]
        to_end = jnp.exp(cum[:, -1:] - cum) * dtc
        state = jnp.exp(cum[:, -1])[..., None, None] * state + jnp.einsum('bjgn,bjge,bjgep->bgepn', bc, to_end, xc)
        return state, y

    state0 = jnp.zeros((bsz, SSD_GROUPS, SSD_HPG, SSD_HEADDIM, SSD_STATE), jnp.float32)
    _, y = lax.scan(step, state0, (to_chunks(xs), to_chunks(dt), to_chunks(bm), to_chunks(cm)))
    return from_chunks(y).astype(xs.dtype)

def ssd_mixer(x, w_in, conv_w, conv_b, dt_bias, a_log, d_skip, norm_g, w_out):
    bsz, l, _ = x.shape
    z, xbc, dt_raw = split_cols(x @ w_in, SSD_SPLITS)
    xbc = jax.nn.silu(causal_dwconv(xbc, conv_w, conv_b))
    xs, bm, cm = split_cols(xbc, (SSD_INNER, SSD_GROUPS * SSD_STATE, SSD_GROUPS * SSD_STATE))
    xs = xs.reshape(bsz, l, SSD_GROUPS, SSD_HPG, SSD_HEADDIM)
    bm = bm.reshape(bsz, l, SSD_GROUPS, SSD_STATE)
    cm = cm.reshape(bsz, l, SSD_GROUPS, SSD_STATE)
    dt = jax.nn.softplus((dt_raw + dt_bias).astype(jnp.float32)).reshape(bsz, l, SSD_GROUPS, SSD_HPG)
    a = -jnp.exp(a_log.astype(jnp.float32)).reshape(SSD_GROUPS, SSD_HPG)
    y = ssd_chunked(xs, dt, a, bm, cm) + xs * d_skip.reshape(SSD_GROUPS, SSD_HPG)[..., None]
    y = y.reshape(bsz, l, SSD_INNER) * jax.nn.silu(z)
    y = rms_norm_2(y.reshape(bsz, l, SSD_GROUPS, SSD_INNER // SSD_GROUPS), norm_g.reshape(SSD_GROUPS, -1))
    return y.reshape(bsz, l, SSD_INNER) @ w_out

def _col_scale(sizes, scaled):
    return jnp.concatenate([jnp.full((s,), DN_BETA if i in scaled else 1.0, jnp.float32)
                            for i, s in enumerate(sizes)])

def second_inputs(seed: int = 0) -> dict:
    key = jax.random.key(seed)
    ks = list(jax.random.split(key, 24))

    def nrm(i, shape, scale):
        return jax.random.normal(ks[i], shape, jnp.float32) * scale

    x = nrm(0, (BATCH, SEQ, D_MODEL), 1.0)
    ffn_w_in = nrm(1, (DEPTH, 2, D_MODEL, 2 * D_FF), DN_BETA * D_MODEL ** -0.5)
    ffn_w_out = nrm(2, (DEPTH, 2, D_FF, D_MODEL), DN_BETA * D_FF ** -0.5)
    ln_g = 1.0 + nrm(3, (DEPTH, 3, D_MODEL), 0.02)
    ln_b = nrm(4, (DEPTH, 3, D_MODEL), 0.02)
    gla_w_in = nrm(5, (N_LAYERS_A, D_MODEL, sum(GLA_SPLITS)), D_MODEL ** -0.5) * _col_scale(GLA_SPLITS, (2,))
    gla_w_gate = nrm(6, (N_LAYERS_A, GLA_RANK, GLA_KEY), GLA_RANK ** -0.5)
    gla_b_gate = nrm(7, (N_LAYERS_A, GLA_KEY), 0.1)
    gla_norm_g = 1.0 + nrm(8, (N_LAYERS_A, GLA_DV), 0.02)
    gla_w_out = nrm(9, (N_LAYERS_A, GLA_VAL, D_MODEL), DN_BETA * GLA_VAL ** -0.5)
    ret_w_in = nrm(10, (N_LAYERS_B, D_MODEL, sum(RET_SPLITS)), D_MODEL ** -0.5) * _col_scale(RET_SPLITS, (2,))
    ret_norm_g = 1.0 + nrm(11, (N_LAYERS_B, RET_DV), 0.02)
    ret_w_out = nrm(12, (N_LAYERS_B, RET_VAL, D_MODEL), DN_BETA * RET_VAL ** -0.5)
    ssd_cols = (SSD_INNER, SSD_INNER, SSD_CONV_DIM - SSD_INNER, SSD_HEADS)
    ssd_w_in = nrm(13, (N_LAYERS_C, D_MODEL, sum(SSD_SPLITS)), D_MODEL ** -0.5) * _col_scale(ssd_cols, (1,))
    ssd_conv_w = nrm(14, (N_LAYERS_C, SSD_CONV, SSD_CONV_DIM), SSD_CONV ** -0.5)
    ssd_conv_b = nrm(15, (N_LAYERS_C, SSD_CONV_DIM), 0.02)
    dt0 = jnp.exp(jax.random.uniform(ks[16], (N_LAYERS_C, SSD_HEADS), jnp.float32,
                                     math.log(1e-3), math.log(1e-1)))
    ssd_dt_bias = dt0 + jnp.log(-jnp.expm1(-dt0))
    ssd_a_log = jnp.log(jax.random.uniform(ks[17], (N_LAYERS_C, SSD_HEADS), jnp.float32, 1.0, 16.0))
    ssd_d = 1.0 + nrm(18, (N_LAYERS_C, SSD_HEADS), 0.02)
    ssd_norm_g = 1.0 + nrm(19, (N_LAYERS_C, SSD_INNER), 0.02)
    ssd_w_out = nrm(20, (N_LAYERS_C, SSD_INNER, D_MODEL), DN_BETA * SSD_INNER ** -0.5)
    return {'x': x, 'ffn_w_in': ffn_w_in, 'ffn_w_out': ffn_w_out, 'ln_g': ln_g, 'ln_b': ln_b,
            'gla_w_in': gla_w_in, 'gla_w_gate': gla_w_gate, 'gla_b_gate': gla_b_gate,
            'gla_norm_g': gla_norm_g, 'gla_w_out': gla_w_out,
            'ret_w_in': ret_w_in, 'ret_norm_g': ret_norm_g, 'ret_w_out': ret_w_out,
            'ssd_w_in': ssd_w_in, 'ssd_conv_w': ssd_conv_w, 'ssd_conv_b': ssd_conv_b,
            'ssd_dt_bias': ssd_dt_bias, 'ssd_a_log': ssd_a_log, 'ssd_d': ssd_d,
            'ssd_norm_g': ssd_norm_g, 'ssd_w_out': ssd_w_out}

def second_block(x, ffn_w_in, ffn_w_out, ln_g, ln_b,
              gla_w_in, gla_w_gate, gla_b_gate, gla_norm_g, gla_w_out,
              ret_w_in, ret_norm_g, ret_w_out,
              ssd_w_in, ssd_conv_w, ssd_conv_b, ssd_dt_bias, ssd_a_log, ssd_d, ssd_norm_g, ssd_w_out):
    h = x
    for i in range(DEPTH):
        h = layer_norm(DN_ALPHA * h + 0.5 * swiglu(h, ffn_w_in[i, 0], ffn_w_out[i, 0]), ln_g[i, 0], ln_b[i, 0])
        kind, j = i % N_MIXERS, i // N_MIXERS
        if kind == 0:
            m = gla_mixer(h, gla_w_in[j], gla_w_gate[j], gla_b_gate[j], gla_norm_g[j], gla_w_out[j])
        elif kind == 1:
            m = retention_mixer(h, ret_w_in[j], ret_norm_g[j], ret_w_out[j])
        else:
            m = ssd_mixer(h, ssd_w_in[j], ssd_conv_w[j], ssd_conv_b[j], ssd_dt_bias[j],
                          ssd_a_log[j], ssd_d[j], ssd_norm_g[j], ssd_w_out[j])
        h = layer_norm(DN_ALPHA * h + m, ln_g[i, 1], ln_b[i, 1])
        h = layer_norm(DN_ALPHA * h + 0.5 * swiglu(h, ffn_w_in[i, 1], ffn_w_out[i, 1]), ln_g[i, 2], ln_b[i, 2])
    return h


def setup_inputs(seed=0):
    out = dict(first_inputs(seed))
    for name, value in second_inputs(seed + 1).items():
        if name != "x":
            out[name + "_2"] = value
    return out


def reference(
    x, c, norm_g, ada_w, ada_b, hgrn_lb, even_w_in, hgrn_onorm_g, pool_w, pool_scale,
    even_w_out, odd_w_in, fox_b_f, fox_qnorm_g, fox_knorm_g, odd_w_out, ffn_w_in_2, ffn_w_out_2,
    ln_g_2, ln_b_2, gla_w_in_2, gla_w_gate_2, gla_b_gate_2, gla_norm_g_2, gla_w_out_2,
    ret_w_in_2, ret_norm_g_2, ret_w_out_2, ssd_w_in_2, ssd_conv_w_2, ssd_conv_b_2,
    ssd_dt_bias_2, ssd_a_log_2, ssd_d_2, ssd_norm_g_2, ssd_w_out_2,
):
    x = first_block(
        x, c, norm_g, ada_w, ada_b, hgrn_lb, even_w_in, hgrn_onorm_g, pool_w, pool_scale,
        even_w_out, odd_w_in, fox_b_f, fox_qnorm_g, fox_knorm_g, odd_w_out,
    )
    return second_block(
        x, ffn_w_in_2, ffn_w_out_2, ln_g_2, ln_b_2, gla_w_in_2, gla_w_gate_2, gla_b_gate_2,
        gla_norm_g_2, gla_w_out_2, ret_w_in_2, ret_norm_g_2, ret_w_out_2, ssd_w_in_2,
        ssd_conv_w_2, ssd_conv_b_2, ssd_dt_bias_2, ssd_a_log_2, ssd_d_2, ssd_norm_g_2,
        ssd_w_out_2,
    )


_drawn_inputs = setup_inputs


def setup_inputs(seed=0):
    import zlib

    import numpy as np

    out = dict(_drawn_inputs(seed))
    spreads = {}
    factors = {'hgrn_lb': 6.727,
     'hgrn_onorm_g': 6.816,
     'pool_scale': 7.462,
     'fox_qnorm_g': 8.0,
     'fox_knorm_g': 8.0,
     'gla_b_gate_2': 6.227,
     'gla_norm_g_2': 8.0,
     'ret_norm_g_2': 8.0}
    for name, (base, spread) in spreads.items():
        noise = np.random.default_rng([zlib.crc32(name.encode()), seed]).standard_normal(out[name].shape)
        drawn = base * np.exp(spread * noise) if base else spread * noise
        out[name] = __import__('jax').numpy.asarray(drawn.astype(out[name].dtype))
    for name, factor in factors.items():
        out[name] = (out[name] * factor).astype(out[name].dtype)
    return out
```

```python
from collections import defaultdict
from contextlib import ExitStack, contextmanager

import numpy as np
import concourse.bass as bass
from concourse import mybir

F32 = mybir.dt.float32
F32R = mybir.dt.float32r
I32 = mybir.dt.int32
ALU = mybir.AluOpType
ACT = mybir.ActivationFunctionType
AX = mybir.AxisListType.X

P = 128
T = 512
NT = T // P
D = 1024
KD = D // P
PIECE = 2048
SLOTS = 3
DFF = 2816
NH = 4
FOX_H = 16
DH = 64
EPS = 1e-6
LN_EPS = 1e-5
ALPHA = 4.0 ** 0.25
NEG = -1e30
CREDIT = 512
LEVELS = (1, 2, 4, 8, 16, 32, 64)


def _columns():
    at, out = 0, {}
    for name, n in (("ident", P), ("ones", P), ("block_ones", P), ("level", P * len(LEVELS)),
                    ("chunk_causal", P), ("causal_add", P), ("reset128", T), ("reset64", T),
                    ("pool_on", 16), ("pool_w", 4), ("pool_head", 64)):
        out[name] = (at, n)
        at += n
    return out, at


COLS, NCOLS = _columns()


def constant_tables():
    c = np.zeros((P, NCOLS), np.float32)

    def put(name, a):
        c[:, COLS[name][0]:COLS[name][0] + COLS[name][1]] = a

    i = np.arange(P)
    put("ident", np.eye(P))
    put("ones", 1.0)
    put("block_ones", (i[:, None] // DH) == (i[None, :] // DH))
    s, t = i[:, None], i[None, :]
    put("level", np.concatenate([((s // (2 * h)) == (t // (2 * h))) & (s % (2 * h) < h) & (t % (2 * h) >= h)
                                 for h in LEVELS], axis=1))
    put("chunk_causal", (s // 64 == t // 64) & (t >= s))
    put("causal_add", np.where(t > s, NEG, 0.0))
    tok = np.arange(T)
    put("reset128", (tok % 128 != 0)[None, :])
    put("reset64", (tok % 64 != 0)[None, :])
    wins = (2, 4, 8, 16)
    put("pool_on", np.array([[w >= 2 ** (k + 1) for k in range(4)] for w in wins]).reshape(1, 16))
    put("pool_w", np.array([[1.0 / w for w in wins]]))
    put("pool_head", np.array([[w / min(n + 1, w) for n in range(16)] for w in wins]).reshape(1, 64))
    sel = np.zeros((FOX_H, FOX_H, P), np.float32)
    for h in range(FOX_H):
        sel[h, h, :] = 1.0
    dh = D // 4
    inv = (10000.0 ** (-np.arange(0, dh, 2, dtype=np.float32) / np.float32(dh))).astype(np.float32)
    ang = inv[:, None] * np.arange(T, dtype=np.float32)[None, :]
    rope = np.stack([np.cos(ang), np.sin(ang)], axis=1).astype(np.float32)
    lg = np.log(1.0 - 2.0 ** (-5.0 - np.arange(NH)))
    lag = tok[None, None, :] - i[:, None, None]
    decay = np.where(lag >= 0, np.exp(np.maximum(lag, 0) * lg[None, :, None]), 0.0) * dh ** -0.5
    return {"consts": c, "sel": sel.reshape(FOX_H, FOX_H * P), "rope": rope,
            "ret_decay": decay.astype(np.float32)}


class Token:

    def __init__(self, prog, value, loop):
        self.prog, self.value, self.loop = prog, value, loop


class Progress:

    def __init__(self, k, name, eng, inc=1, credit=0):
        self.k, self.name, self.eng, self.inc = k, name, eng, inc
        self.sem = k.sem("s_" + name)
        self.n = credit
        self.seen = {}
        k.progs.append(self)

    def wait(self, *tokens):
        for t in tokens:
            if isinstance(t, str):
                self.k.wait_noted(self, t)
            elif isinstance(t, (list, tuple)):
                self.wait(*t)
            elif t is not None:
                self.k.wait_token(self, t)


class Kernel:
    def __init__(self, nc, ctx, counts):
        self.nc, self.ctx, self.counts = nc, ctx, counts
        self.loop, self.progs, self.noted, self.found = None, [], {}, {}

    def sem(self, name):
        return self.ctx.enter_context(self.nc.semaphore(name))

    def wait_token(self, me, t):
        L = self.loop
        if L is not None and t.loop is L:
            key = (t.prog.name, L.name)
            if me.seen.get(key, -1) < t.value:
                me.seen[key] = t.value
                me.eng.wait_ge(t.prog.sem, L.i * L.per(t.prog) + t.value if L.per(t.prog) else t.value)
            return
        value = t.value if t.loop is None else t.value + (t.loop.n - 1) * t.loop.per(t.prog)
        if me.seen.get(t.prog.name, -1) < value:
            if L is None:
                me.seen[t.prog.name] = value
            me.eng.wait_ge(t.prog.sem, value)

    def wait_noted(self, me, name):
        L, got = self.loop, self.noted.get(name, [])
        if L is None or (got and got[0].loop is L):
            for t in got:
                self.wait_token(me, t)
            return
        for t in got:
            self.wait_token_before(me, t)
        for prog, off in L.last.get(name, []):
            p = self.prog(prog)
            if (me.seen.get((prog, L.name), -1)) >= 0:
                continue
            key = (prog, L.name, "last")
            if me.seen.get(key, -1) < off:
                me.seen[key] = off
                value = L.start[prog] + off - L.per(p)
                assert value > 0 or L.dry, (name, prog, value)
                me.eng.wait_ge(p.sem, L.i * L.per(p) + max(value, 1))

    def wait_token_before(self, me, t):
        value = t.value if t.loop is None else t.value + (t.loop.n - 1) * t.loop.per(t.prog)
        if me.seen.get(t.prog.name, -1) < value:
            L = self.loop
            if L.dry:
                L.hoist.append((me.name, t.prog.name, value))
            else:
                raise AssertionError("a wait of the first round was not met before the loop")

    def prog(self, name):
        return next(p for p in self.progs if p.name == name)

    @contextmanager
    def rounds(self, name, n, pieces):
        L = Loop(self, name, n, pieces)
        for me, prog, value in self.counts.get(name, {}).get("hoist", []):
            m = self.prog(me)
            if m.seen.get(prog, -1) < value:
                m.seen[prog] = value
                m.eng.wait_ge(self.prog(prog).sem, value)
        with self.nc.Fori(0, n) as i:
            L.i = i
            self.loop = L
            yield i
            self.loop = None
        L.end()
        self.weights.end_loop(n, pieces)


class Loop:
    def __init__(self, k, name, n, pieces):
        self.k, self.name, self.n, self.pieces = k, name, n, pieces
        known = k.counts.get(name)
        self.dry = known is None
        self.pers = {} if self.dry else known["per"]
        self.last = {} if self.dry else known["last"]
        self.start = defaultdict(int, {p.name: p.n for p in k.progs})
        self.hoist = []

    def per(self, prog):
        return self.pers.get(prog.name, 0)

    def end(self):
        per = {p.name: p.n - self.start[p.name] for p in self.k.progs}
        last = {a: [(t.prog.name, t.value - self.start[t.prog.name]) for t in b]
                for a, b in self.k.noted.items() if b and b[0].loop is self}
        if not self.dry:
            assert per == self.pers and last == self.last, self.name
        self.k.found[self.name] = {"per": per, "last": last, "hoist": self.hoist}
        self.pers = per
        for p in self.k.progs:
            p.n = self.start[p.name] + self.n * per[p.name]


class Weights:

    def __init__(self, k, raw, hi, lo):
        self.k, self.raw, self.hi, self.lo = k, raw, hi, lo
        self.loaded = [k.sem(f"s_loaded{s}") for s in range(SLOTS)]
        self.rounded = [k.sem(f"s_rounded{s}") for s in range(SLOTS)]
        self.split = [k.sem(f"s_split{s}") for s in range(SLOTS)]
        for s in range(SLOTS):
            k.nc.vector.sem_inc(self.split[s], 1)
        self.n = {what: [0] * SLOTS for what in ("load", "convert", "use")}

    def number(self, what, s, k=1, plus=0):
        L, n = self.k.loop, self.n[what][s]
        if L is None:
            return n * k + plus
        return L.i * (L.pieces.count(s) * k) + (n * k + plus)

    def end_loop(self, n, pieces):
        for what in self.n:
            for s in range(SLOTS):
                self.n[what][s] += (n - 1) * pieces.count(s)

    def load(self, s, halves):
        self.n["load"][s] += 1
        sp = self.k.nc.sync
        sp.wait_ge(self.split[s], self.number("load", s))
        for dst, src in halves:
            sp.dma_start(dst, src).then_inc(self.loaded[s], 16)

    def convert(self, s):
        self.n["convert"][s] += 1
        k, nc = self.k, self.k.nc
        nc.scalar.wait_ge(self.loaded[s], self.number("convert", s, k=32))
        k.prog("act").wait(f"used{s}")
        nc.scalar.activation(self.hi[:, s, :], self.raw[:, s, :], ACT.Copy).then_inc(self.rounded[s], 1)
        nc.vector.wait_ge(self.rounded[s], self.number("convert", s))
        nc.vector.tensor_tensor(self.lo[:, s, :], self.raw[:, s, :], self.hi[:, s, :].bitcast(F32),
                                ALU.subtract).then_inc(self.split[s], 1)

    def use(self, s):
        self.n["use"][s] += 1
        self.k.nc.tensor.wait_ge(self.split[s], self.number("use", s, plus=1))


def build(nc, a, counts):
    with ExitStack() as ctx:
        k = Kernel(nc, ctx, counts)
        emit(nc, ctx, k, a)
        return k.found


def emit(nc, ctx, k, a):
    def sb(name, shape, dt=F32, c=ctx):
        return c.enter_context(nc.sbuf_tensor(name, shape, dt))

    bank = [ctx.enter_context(nc.psum_tensor(f"bank{b}", [P, T], F32)) for b in range(8)]
    acc = sb("acc", [P, NT, D])
    h_hi, h_lo = sb("h_hi", [P, KD, T], F32R), sb("h_lo", [P, KD, T], F32R)
    w_raw = sb("w_raw", [P, SLOTS, PIECE])
    w_hi, w_lo = sb("w_hi", [P, SLOTS, PIECE], F32R), sb("w_lo", [P, SLOTS, PIECE], F32R)
    oh_hi, oh_lo = sb("oh_hi", [P, 2, T], F32R), sb("oh_lo", [P, 2, T], F32R)
    consts = sb("consts", [P, NCOLS])
    vcol = sb("vcol", [P, 2, P])
    eps = sb("eps", [P, 3])
    zero8, spare = sb("zero8", [P, KD]), sb("spare", [P, 1])
    col8 = sb("col8", [P, 2, KD])
    val = sb("val", [P, 2, T])
    stat = sb("stat", [P, NT, 24])

    def const(name, lo=0, n=None):
        at, size = COLS[name]
        return consts[:, at + lo:at + lo + (size - lo if n is None else n)]

    ident, ones = const("ident"), const("ones")

    PE = Progress(k, "pe", nc.tensor, credit=CREDIT)
    SC = Progress(k, "act", nc.scalar, credit=CREDIT)
    VE = Progress(k, "dve", nc.vector, credit=CREDIT)
    PO = Progress(k, "pool", nc.gpsimd, credit=CREDIT)
    SP = Progress(k, "sp", nc.sync)
    for e in (PE, SC, VE, PO):
        e.eng.sem_inc(e.sem, CREDIT)
    W = k.weights = Weights(k, w_raw, w_hi, w_lo)

    def do(e, ins, note=None):
        ins.then_inc(e.sem, e.inc)
        e.n += e.inc
        t = Token(e, e.n, k.loop)
        if note:
            k.noted[note] = [t]
        return t

    def note(name, *tokens):
        k.noted[name] = [t for t in tokens if t is not None]

    queues = {}

    def dma(name, out, in_, eng=None):
        if name not in queues:
            queues[name] = Progress(k, "dma_" + name, eng or nc.gpsimd, inc=16)
        q = queues[name]
        return do(q, q.eng.dma_start(out, in_))

    def act(out, in_, func, *waits, **kw):
        SC.wait(*waits)
        return do(SC, nc.scalar.activation(out, in_, func, **kw))

    def tt(out, x, y, op, *waits, e=VE):
        e.wait(*waits)
        return do(e, e.eng.tensor_tensor(out, x, y, op))

    def ts(out, x, s1, s2, op0, op1, *waits, e=VE):
        e.wait(*waits)
        if s2 is None:
            return do(e, e.eng.tensor_scalar(out, x, s1, None, op0))
        return do(e, e.eng.tensor_scalar(out, x, s1, s2, op0, op1))

    def stt(out, x, s, y, op0, op1, *waits):
        VE.wait(*waits)
        return do(VE, nc.vector.scalar_tensor_tensor(out, x, s, y, op0, op1))

    def recip(out, x, *waits):
        VE.wait(*waits)
        return do(VE, nc.vector.reciprocal(out, x))

    def enter_scratch():
        for e in (SC, VE, PO, PE):
            e.wait("scratch")

    def wait_apart(*tokens):
        VE.wait(*tokens, "spare")
        do(VE, nc.vector.memset(spare[:], 0.0), "spare")

    mult, add, sub = ALU.mult, ALU.add, ALU.subtract

    def three(out, ws, wl, xs, xl, first, last):
        nc.tensor.matmul(out, ws, xs, start=first, stop=False)
        nc.tensor.matmul(out, ws, xl, start=False, stop=False)
        return nc.tensor.matmul(out, wl, xs, start=False, stop=last)

    def project(s, c, b, last=True):
        PE.wait(f"bank{b}", "h")
        for kk in range(KD):
            w = slice(kk * 256 + c * P, kk * 256 + (c + 1) * P)
            ins = three(bank[b][:], w_hi[:, s, w], w_lo[:, s, w], h_hi[:, kk, :], h_lo[:, kk, :],
                        kk == 0, kk == KD - 1)
        if last:
            return do(PE, ins, f"used{s}")
        return do(PE, ins)

    def project_tokens(s, banks, c0=0, n=256, last=True):
        per = T // n
        done = []
        for t in range(NT):
            b = banks[t // per]
            if t % per == 0:
                PE.wait(f"bank{b}", "h")
            o = bank[b][:, (t % per) * n:(t % per + 1) * n]
            for kk in range(KD):
                w = slice(kk * 256 + c0, kk * 256 + c0 + n)
                x = slice(t * P, (t + 1) * P)
                nc.tensor.matmul(o, h_hi[:, kk, x], w_hi[:, s, w], start=kk == 0, stop=False)
                nc.tensor.matmul(o, h_lo[:, kk, x], w_hi[:, s, w], start=False, stop=False)
                ins = nc.tensor.matmul(o, h_hi[:, kk, x], w_lo[:, s, w], start=False, stop=kk == KD - 1)
            if t == NT - 1 and last:
                done.append(do(PE, ins, f"used{s}"))
            elif t % per == per - 1:
                done.append(do(PE, ins))
        return done

    def split_oh(c, value, *waits, hi=oh_hi, lo=oh_lo, free="oh"):
        t1 = act(hi[:, c, :], value, ACT.Copy, free, *waits)
        t2 = tt(lo[:, c, :], value, hi[:, c, :].bitcast(F32), sub, t1)
        return t2

    def out_step(s, ready, scale=1.0, gate=None, order=(0, 1), hi=oh_hi, lo=oh_lo, free="oh"):
        outs = [(t, n) for t in range(NT) for n in range(2)]

        def part(j, c, first, last):
            t, n = outs[j]
            b = 4 + j % 4
            x, w = slice(t * P, (t + 1) * P), slice(c * D + n * T, c * D + (n + 1) * T)
            nc.tensor.matmul(bank[b][:], hi[:, c, x], w_hi[:, s, w], start=first, stop=False)
            nc.tensor.matmul(bank[b][:], lo[:, c, x], w_hi[:, s, w], start=False, stop=False)
            return nc.tensor.matmul(bank[b][:], hi[:, c, x], w_lo[:, s, w], start=False, stop=last)

        def evacuate(j, done):
            t, n = outs[j]
            b = 4 + j % 4
            dst = acc[:, t, n * T:(n + 1) * T]
            if gate is None:
                e = stt(dst, bank[b][:], scale, dst, mult, add, done, "acc")
                note(f"bank{b}", e)
            else:
                g = val[:, j % 2, :]
                e = tt(g, bank[b][:], gate[:, n * T:(n + 1) * T], mult, done, f"val{j % 2}")
                note(f"bank{b}", e)
                e = tt(dst, dst, g, add, e, "acc")
                note(f"val{j % 2}", e)
            return e

        PE.wait(ready[0])
        for j in range(4):
            PE.wait(f"bank{4 + j}")
            part(j, order[0], True, False)
        PE.wait(ready[1])
        last = None
        for j in range(8):
            if j >= 4:
                PE.wait(f"bank{4 + j % 4}")
                part(j, order[0], True, False)
            ins = part(j, order[1], False, True)
            if j == 7:
                done = do(PE, ins, f"used{s}")
                note(free, done)
            else:
                done = do(PE, ins)
            last = evacuate(j, done)
        note("acc", last)

    def wview(s, n=256):
        return w_raw[:, s, :].rearrange("p (k n) -> p k n", n=n)

    def load_columns(s, m, cols):
        v = m.rearrange("(k p) n -> p k n", p=P)
        W.load(s, [(wview(s)[:, :, c * P:(c + 1) * P], v[:, :, bass.ds(cols[c], P)]) for c in range(2)])

    def load_wide(s, m, col):
        v = m.rearrange("(k p) n -> p k n", p=P)
        W.load(s, [(wview(s)[:, c * 4:c * 4 + 4, :], v[:, c * 4:c * 4 + 4, bass.ds(col, 256)]) for c in range(2)])

    def load_rows(s, m, rows):
        W.load(s, [(w_raw[:, s, c * D:(c + 1) * D], m[bass.ds(rows[c], P), :]) for c in range(2)])

    def sigmoid_part(tmp, x, *waits):
        t = act(tmp, x, ACT.Exp, *waits, scale=-1.0)
        t = ts(tmp, tmp, 1.0, None, add, None, t)
        return recip(tmp, tmp, t)

    t_consts = dma("consts", consts[:], a["consts"])
    t_x = dma("x", acc[:], a["x"].rearrange("b (t p) d -> p (b t) d", p=P))
    k.noted["acc"] = [t_x]

    vrow = val[:, 0, 0:2 * P].rearrange("p (g n) -> p g n", n=P)
    po_t = do(PO, nc.gpsimd.memset(vrow, 0.0))
    do(PO, nc.gpsimd.memset(eps[:, 0:1], EPS))
    do(PO, nc.gpsimd.memset(eps[:, 1:2], LN_EPS))
    do(PO, nc.gpsimd.memset(zero8[:], 0.0))
    t_eps = do(PO, nc.gpsimd.memset(eps[:, 2:3], 1.0))
    for e in (SC, VE, PE):
        e.wait(t_consts, t_eps)
    vec, at = {}, 0
    PO.wait(po_t)
    for name, src, n in (
            ("c", a["c"].rearrange("b (j p) -> (b j) p", p=P), 8),
            ("ada_b", a["ada_b"].rearrange("l (j p) -> (l j) p", p=P), 48),
            ("norm_g", a["norm_g"].rearrange("l (j p) -> (l j) p", p=P), 16),
            ("lb", a["hgrn_lb"].rearrange("l (j p) -> (l j) p", p=P), 12),
            ("onorm", a["hgrn_onorm_g"].rearrange("l (j p) -> (l j) p", p=P), 4),
            ("pool_scale", a["pool_scale"].rearrange("l (j p) -> (l j) p", p=P), 4),
            ("b_gate", a["gla_b_gate_2"].rearrange("l (j p) -> (l j) p", p=P), 4),
            ("gla_g", a["gla_norm_g_2"].rearrange("l (j p) -> (l j) p", p=P), 2)):
        t_v = dma("vec", vrow[at:at + n, 0, :], src)
        vec[name] = at
        at += n
    for name, src in (("qnorm", a["fox_qnorm_g"]), ("knorm", a["fox_knorm_g"])):
        for half in range(2):
            t_v = dma("vec", vrow[at:at + 1, 0, half * DH:(half + 1) * DH], src)
        vec[name] = at
        at += 1
    assert at <= P
    t_v = dma("vec", vrow[0:48, 1, :], a["ln_g_2"].rearrange("l m (j p) -> (l m j) p", p=P))
    t_v = dma("vec", vrow[48:96, 1, :], a["ln_b_2"].rearrange("l m (j p) -> (l m j) p", p=P))
    fb = sb("fox_b", [FOX_H, 1])
    t_fb = dma("vec", fb[:], a["fox_b_f"].rearrange("a h -> h a"))
    PE.wait(t_fb)
    for g in range(2):
        t_tr = do(PE, nc.tensor.transpose(bank[0][:, g * P:(g + 1) * P], vrow[:, g, :], ident))
    SC.wait(t_tr)
    t_vc = act(vcol[:].rearrange("p g n -> p (g n)"), bank[0][:, 0:2 * P], ACT.Copy)
    note("bank0", t_vc)

    def vc(name, j, n=1, g=0):
        return vcol[:, g, bass.ds(vec[name] + j, n)]

    lbt = sb("lbt", [P, 12])
    lb, oml = sb("lb", [P, 4]), sb("oml", [P, 4])
    x = [vcol[:, 0, vec["lb"] + 4 * r:vec["lb"] + 4 * r + 4] for r in range(3)]
    t = tt(lb[:], x[0], x[1], ALU.max, t_vc)
    t = tt(lb[:], lb[:], x[2], ALU.max, t)
    for r in range(3):
        t = tt(lbt[:, 4 * r:4 * r + 4], x[r], lb[:], sub, t)
    t = act(lbt[:], lbt[:], ACT.Exp, t)
    t = tt(lb[:], lbt[:, 0:4], lbt[:, 4:8], add, t)
    t = tt(lb[:], lb[:], lbt[:, 8:12], add, t)
    t = recip(lb[:], lb[:], t)
    t = tt(lb[:], lb[:], lbt[:, 0:4], mult, t)
    t_lb = ts(oml[:], lb[:], -1.0, 1.0, mult, add, t)

    cond = sb("cond", [P, 8])
    sg = sb("sg", [P, 8])
    t = sigmoid_part(sg[:], vc("c", 0, 8))
    t_cond = tt(cond[:], vc("c", 0, 8), sg[:], mult, t)

    mod = sb("mod", [P, 2, 24])
    first = ctx.enter_context(ExitStack())
    gate = sb("gate", [P, D], c=first)
    AR = 3
    ada_buf = ctx.enter_context(ExitStack())
    ada_raw = sb("ada_raw", [P, AR, 1024], c=ada_buf)
    ada_loaded = [k.sem(f"s_ada_loaded{r}") for r in range(AR)]

    def ada_group(l, i, base, b):
        w = a["ada_w"][l].rearrange("(k p) n -> p k n", p=P)
        PE.wait(f"bank{b}", t_cond)
        for j in range(6):
            r, n = j % AR, base + j // AR + 1
            SP.wait(f"ada{r}")
            nc.sync.dma_start(ada_raw[:, r, :].rearrange("p (k n) -> p k n", n=P),
                              w[:, :, bass.ds(i * 768 + j * P, P)]).then_inc(ada_loaded[r], 16)
            nc.tensor.wait_ge(ada_loaded[r], i * 32 + 16 * n)
            for kk in range(KD):
                ins = nc.tensor.matmul(bank[b][:, j:j + 1], ada_raw[:, r, kk * P:(kk + 1) * P],
                                       cond[:, kk:kk + 1], start=kk == 0, stop=kk == KD - 1)
            t = do(PE, ins, f"ada{r}")
        t = tt(mod[:, l, bass.ds(i * 6, 6)], bank[b][:, 0:6], vc("ada_b", l * 24 + i * 6, 6), add, t)
        note(f"bank{b}", t)
        note("mod", t)

    even_w, odd_w = a["even_w_in"][0], a["odd_w_in"][0]

    with k.rounds("ada0", 4, []) as i:
        ada_group(0, i, 0, 7)


    def modulated_norm(l, ctx2):
        xn = sb(f"xn{l}", [P, NT, D], c=ctx2)
        t = ts(col8[:, 0, :], mod[:, l, 8:16], 1.0, None, add, None, "mod", "col8")
        t_s = tt(col8[:, 0, :], col8[:, 0, :], vc("norm_g", l * 8, 8), mult, t)
        for j in range(KD):
            t = ts(val[:, j % 2, 0:P], ident, mod[:, l, 16 + j:17 + j], None, mult, None,
                   "mod", f"val{j % 2}")
            PE.wait(t, f"bank{j // 4}")
            tp = do(PE, nc.tensor.matmul(bank[j // 4][:, (j % 4) * P:(j % 4 + 1) * P], ones,
                                         val[:, j % 2, 0:P], start=True, stop=True))
            note(f"val{j % 2}", tp)
            if j % 4 == 3:
                t = act(gate[:, (j // 4) * T:(j // 4 + 1) * T], bank[j // 4][:], ACT.Copy, tp)
                note(f"bank{j // 4}", t)
        note("gate", t)
        ssq = stat[:, :, 0]
        for tt_ in range(NT):
            t = act(xn[:, tt_, :], acc[:, tt_, :], ACT.Square, "acc", accum_out=stat[:, tt_, 0:1])
        t = act(stat[:, :, 1], ssq, ACT.Ln, t, scale=1.0 / D, bias=eps[:, 0:1])
        t = act(stat[:, :, 1], stat[:, :, 1], ACT.Exp, t, scale=-0.5)
        for q in range(NT):
            t = ts(xn[:, q, :], acc[:, q, :], stat[:, q, 1:2], None, mult, None, t)
        to_features(xn, col8[:, 0, :], mod[:, l, 0:8], t, t_s)

    def to_features(src, g, b, *waits):
        PE.wait(*waits)
        for j in range(8):
            PE.wait(f"bank{j}")
        for t in range(NT):
            for j in range(KD):
                done = do(PE, nc.tensor.transpose(bank[j][:, t * P:(t + 1) * P],
                                                  src[:, t, j * P:(j + 1) * P], ident))
        for j in range(KD):
            v = val[:, j % 2, :]
            if j % 2 == 0:
                t = act(v, bank[j][:], ACT.Identity, done, f"val{j % 2}", scale=g[:, j:j + 1], bias=b[:, j:j + 1])
            else:
                t = ts(v, bank[j][:], g[:, j:j + 1], b[:, j:j + 1], mult, add, done, f"val{j % 2}")
            note(f"bank{j}", t)
            t = act(h_hi[:, j, :], v, ACT.Copy, t, "h_free")
            t = tt(h_lo[:, j, :], v, h_hi[:, j, :].bitcast(F32), sub, t)
            note(f"val{j % 2}", t)
        note("h", t)
        note("transposed", done)

    with ExitStack() as c2:
        modulated_norm(0, c2)
    note("scratch", *k.noted["transposed"])

    def cross_tiles(q0, kend, edge, ex, ST, vw, b0, b1, *waits):
        t1 = ts(ex[:, 0, :], q0[:, 2 * P:3 * P], edge[:, 1:2], None, mult, None, *waits)
        t2 = ts(ex[:, 1, :], q0[:, 3 * P:4 * P], edge[:, 2:3], None, mult, None)
        t3 = ts(ex[:, 2, :], ex[:, 1, :], edge[:, 1:2], None, mult, None, t2)
        PE.wait(t3, f"bank{b0}", f"bank{b1}")
        for n, (b, o, j, rhs) in enumerate(((b0, 0, 0, q0[:, P:2 * P]), (b0, 1, 0, ex[:, 0, :]), (b0, 2, 0, ex[:, 2, :]),
                             (b1, 0, 1, q0[:, 2 * P:3 * P]), (b1, 1, 1, ex[:, 1, :]),
                             (b1, 2, 2, q0[:, 3 * P:4 * P]))):
            t = do(PE, nc.tensor.matmul(bank[b][:, o * P:(o + 1) * P], kend[:, j * P:(j + 1) * P],
                                        rhs, start=True, stop=True))
        note("cross", t)
        u1 = act(ST[:, P:T], bank[b0][:, 0:3 * P], ACT.Copy, t, "pv")
        u2 = act(ST[:, 640 + P:640 + 3 * P], bank[b1][:, 0:2 * P], ACT.Copy)
        u3 = act(ST[:, 1280 + P:1280 + 2 * P], bank[b1][:, 2 * P:3 * P], ACT.Copy)
        note(f"bank{b0}", u1)
        note(f"bank{b1}", u3)
        return u3

    def masked_diag(ST, mask, kk, qq, b, *waits):
        PE.wait(f"bank{b}", *waits)
        for j in range(NT):
            t = do(PE, nc.tensor.matmul(bank[b][:, j * P:(j + 1) * P], kk[:, j * P:(j + 1) * P],
                                        qq[:, j * P:(j + 1) * P], start=True, stop=True))
        diag = ST.rearrange("p (j x) -> p j x", x=640)[:, :, 0:P]
        m = mask.bitcast(I32).unsqueeze(1).broadcast_to((P, NT, P))
        wait_apart(t, "diag")
        u = do(VE, nc.vector.copy_predicated(diag, m, bank[b][:].rearrange("p (j x) -> p j x", x=P)))
        note(f"bank{b}", u)
        note("diag", u)
        return t, u

    def head_values(b, v, c, ST, *waits):
        PE.wait(f"bank{b}", *waits)
        for j in range(NT):
            ins = nc.tensor.matmul(bank[b][:, j * P:T], v[:, j, c * P:(c + 1) * P],
                                   ST[:, j * 640:j * 640 + T - j * P], start=j == 0, stop=j == NT - 1)
        return do(PE, ins)

    def tile_view(x, n=P):
        return x.rearrange("p (j n) -> p j n", n=n)

    with ExitStack() as c2:
        enter_scratch()
        s_q, s_key, s_cum = (sb(n, [P, T], c=c2) for n in ("e_q", "e_key", "e_cum"))
        s_v = sb("e_v", [P, NT, P], c=c2)
        s_ga = sb("e_ga", [P, T], c=c2)
        s_u = sb("e_u", [P, 2, 16 + T], c=c2)
        s_d, s_E = sb("e_d", [P, 2, T], c=c2), sb("e_E", [P, 2, T], c=c2)
        s_qs, s_ks = sb("e_qs", [P, 2, T], c=c2), sb("e_ks", [P, 2, T], c=c2)
        s_q0, s_kend = sb("e_q0", [P, T], c=c2), sb("e_kend", [P, T], c=c2)
        s_gb = s_ks[:, 0, :]
        s_f = s_kend
        s_ex, s_edge = sb("e_ex", [P, 3, P], c=c2), sb("e_edge", [P, NT], c=c2)
        ST = sb("e_ST", [P, NT * 640], c=c2)
        s_sq, s_rs = s_qs[:, 1, :], s_ks[:, 1, :]
        s_pw = sb("e_pw", [P, P], c=c2)
        do(PO, nc.gpsimd.memset(ST[:], 0.0))
        t_z = do(PO, nc.gpsimd.memset(s_u[:], 0.0))
        SC.wait(t_z); VE.wait(t_z)

        def even_body(i):
            load_columns(0, even_w, (i * P, i * P + 512))
            load_columns(1, even_w, (i * P + 1024, i * P + 1536))
            load_columns(2, even_w, (i * P + 2048, i * P + 2560))
            PO.wait("e_pw")
            t_pw = dma("pool_w", s_pw[:], a["pool_w"][0][bass.ds(i, 1)].rearrange("g c d -> (g c) d"))
            load_rows(1, a["even_w_out"][0], (i * P, i * P + 512))
            W.convert(1)
            W.use(0)
            tq = project(0, 0, 0, last=False)
            tf = project(0, 1, 1)
            t = sigmoid_part(s_f[:], bank[1][:], tf, "cross")
            note("bank1", t)
            t = ts(s_f[:], s_f[:], oml[:, bass.ds(i, 1)], lb[:, bass.ds(i, 1)], mult, add, t)
            t_key = ts(s_key[:], s_f[:], -1.0, 1.0, mult, add, t, "e_key")
            t_q = act(s_q[:], bank[0][:], ACT.Copy, tq, "e_q")
            note("bank0", t_q)
            t = act(s_f[:], s_f[:], ACT.Ln, t_key)
            VE.wait(t)
            t_cum = do(VE, nc.vector.tensor_tensor_scan(s_cum[:], const("reset128"), s_f[:], 0.0, mult, add))
            W.convert(2)
            W.use(1)
            (tv,) = project_tokens(1, [2], 0, P, last=False)
            tga = project(1, 1, 3)
            t_v = act(s_v[:].rearrange("p t n -> p (t n)"), bank[2][:], ACT.Copy, tv, "e_v")
            note("bank2", t_v)
            t = sigmoid_part(s_ga[:], bank[3][:], tga, "e_ga")
            t_ga = tt(s_ga[:], s_ga[:], bank[3][:], mult, t)
            note("bank3", t_ga)
            W.convert(1)
            cum4 = tile_view(s_cum[:])
            t_E = act(s_E[:, 0, :], s_cum[:], ACT.Exp, t_cum, "e_E0")
            t_q0 = tt(s_q0[:], s_q[:], s_E[:, 0, :], mult, t_E, t_q, "cross")
            t_ed = act(s_edge[:], cum4[:, :, P - 1], ACT.Exp)
            t = tt(tile_view(s_d[:, 0, :]), cum4[:, :, P - 1:P].broadcast_to((P, NT, P)), cum4, sub, "e_d0")
            t = act(s_d[:, 0, :], s_d[:, 0, :], ACT.Exp, t)
            t_kend = tt(s_kend[:], s_key[:], s_d[:, 0, :], mult, t)
            note("e_d0", t_kend)
            note("e_E0", t_kend)
            W.use(2)
            tu = project(2, 0, 0, last=False)
            tgb = project(2, 1, 1)
            t_cr = cross_tiles(s_q0, s_kend, s_edge, s_ex, ST[:], s_v, 4, 5, t_kend, t_ed)
            _, u = masked_diag(ST[:], ident, s_key[:], s_q[:], 6, t_cr)
            for n, h in enumerate(LEVELS):
                z = n % 2
                nb = T // (2 * h)
                c3 = s_cum[:].rearrange("p (b n) -> p b n", n=2 * h)
                d3 = s_d[:, z, :].rearrange("p (b n) -> p b n", n=2 * h)
                E3 = s_E[:, z, :].rearrange("p (b n) -> p b n", n=2 * h)
                mid = c3[:, :, h - 1:h].broadcast_to((P, nb, 2 * h))
                t = tt(d3, c3, mid, sub, f"e_d{z}")
                t = act(E3[:, :, 0:h], d3[:, :, 0:h], ACT.Exp, t, f"e_E{z}", scale=-1.0)
                t = act(E3[:, :, h:2 * h], d3[:, :, h:2 * h], ACT.Exp)
                note(f"e_d{z}", t)
                tq_ = tt(s_qs[:, z, :], s_q[:], s_E[:, z, :], mult, t, f"e_qs{z}")
                tk_ = tt(s_ks[:, z, :], s_key[:], s_E[:, z, :], mult)
                note(f"e_E{z}", tk_)
                tp, u = masked_diag(ST[:], const("level", n * P, P), s_ks[:, z, :], s_qs[:, z, :], 6 + z, tk_)
                note(f"e_qs{z}", tp)
            note("e_key", tp)
            note("e_q", tp)
            t = act(s_u[:, 0, 16:16 + T], bank[0][:], ACT.Copy, tu, "e_u")
            t_u = act(s_E[:, 0, :], bank[0][:], ACT.Copy, "e_E0")
            note("bank0", t_u)
            t_gb = sigmoid_part(s_gb, bank[1][:], tgb, "e_qs0")
            t_gb = tt(s_gb, s_gb, bank[1][:], mult, t_gb)
            note("bank1", t_gb)
            VE.wait(t_u)
            for n in range(4):
                sh = 2 ** n
                src, dst = s_u[:, n % 2, :], s_u[:, (n + 1) % 2, :]
                t = stt(dst[:, 16:16 + T], src[:, 16 - sh:16 - sh + T],
                        const("pool_on")[:, bass.ds(i * 4 + n, 1)], src[:, 16:16 + T], mult, add, t)
            pooled = s_u[:, 0, 16:16 + T]
            t = tt(s_u[:, 0, 16:32], s_u[:, 0, 16:32], const("pool_head")[:, bass.ds(i * 16, 16)], mult, t)
            t = stt(s_qs[:, 0, :], pooled, const("pool_w")[:, bass.ds(i, 1)], s_E[:, 0, :], mult, sub, t)
            note("e_E0", t)
            note("e_u", t)
            PE.wait(t, "bank0", t_pw, t_pw)
            t = do(PE, nc.tensor.matmul(bank[0][:], s_pw[:], s_qs[:, 0, :], start=True, stop=True))
            note("e_pw", t)
            t = stt(s_gb, bank[0][:], vc("pool_scale", i), s_gb, mult, mult, t)
            note("bank0", t)
            r1 = split_oh(1, s_gb, t)
            note("e_qs0", r1)
            tp = head_values(2, s_v[:], 0, ST[:], u, t_v, t_cr)
            note("pv", tp)
            note("e_v", tp)
            t = act(s_sq, bank[2][:], ACT.Square, tp, "e_qs1")
            PE.wait(t, "bank3")
            t = do(PE, nc.tensor.matmul(bank[3][:], ones, s_sq, start=True, stop=True))
            t = act(s_rs, bank[3][:], ACT.Ln, t, scale=1.0 / P, bias=eps[:, 0:1])
            note("bank3", t)
            t = act(s_rs, s_rs, ACT.Exp, t, scale=-0.5)
            t = stt(s_rs, bank[2][:], vc("onorm", i), s_rs, mult, mult, t)
            note("bank2", t)
            t = tt(s_ga[:], s_ga[:], s_rs, mult, t)
            note("e_qs1", t)
            r0 = split_oh(0, s_ga[:], t)
            note("e_ga", r0)
            ada_group(1, i, 8, 7)
            W.convert(0)
            W.use(1)
            out_step(1, (r1, r0), gate=gate[:], order=(1, 0))

        W.convert(0)
        with k.rounds("even", NH, [0, 1, 2, 1]) as i:
            even_body(i)
    note("scratch", *k.noted["acc"])

    ada_buf.close()

    def narrow(m, col, b, ctx2, name):
        raw = sb(name + "_raw", [P, KD, 16], c=ctx2)
        hi, lo = sb(name + "_hi", [P, KD, P], F32R, ctx2), sb(name + "_lo", [P, KD, P], F32R, ctx2)
        t0 = dma(name, raw[:], m.rearrange("(k p) n -> p k n", p=P)[:, :, col:col + 16])
        t1 = do(PO, nc.gpsimd.memset(hi[:].bitcast(F32), 0.0))
        t2 = do(PO, nc.gpsimd.memset(lo[:].bitcast(F32), 0.0))
        t3 = act(hi[:, :, 0:16], raw[:], ACT.Copy, t0, t2)
        t4 = tt(lo[:, :, 0:16], raw[:], hi[:, :, 0:16].bitcast(F32), sub, t3)
        PE.wait(t4, "h", f"bank{b}")
        for kk in range(KD):
            ins = three(bank[b][:], hi[:, kk, :], lo[:, kk, :], h_hi[:, kk, :], h_lo[:, kk, :],
                        kk == 0, kk == KD - 1)
        return do(PE, ins)

    def log_sigmoid(out, tmp, xb, *waits):
        t = act(tmp, xb, ACT.Abs, *waits)
        t = act(tmp, tmp, ACT.Exp, t, scale=-1.0)
        t = act(tmp, tmp, ACT.Ln, t, bias=eps[0:tmp.shape[0], 2:3])
        return stt(out, xb, 0.0, tmp, ALU.min, sub, t)

    with ExitStack() as c2:
        enter_scratch()
        modulated_norm(1, c2)
        note("scratch", *k.noted["transposed"])

    odd_w = a["odd_w_in"][0]
    with ExitStack() as c2:
        enter_scratch()
        ncum = sb("o_ncum", [P, FOX_H, T], c=c2)
        with ExitStack() as c3:
            t = narrow(odd_w, 4096, 0, c3, "fl")
            R = slice(0, FOX_H)
            xb, tmp, lf = (sb(n, [FOX_H, T], c=c3) for n in ("fl_x", "fl_t", "fl_l"))
            sel = sb("fl_sel", [FOX_H, FOX_H * P], c=c3)
            t_sel = dma("sel", sel[:], a["sel"])
            t = act(xb[:], bank[0][R, :], ACT.Identity, t, bias=fb[:, 0:1])
            note("bank0", t)
            t = log_sigmoid(lf[:], tmp[:], xb[:], t)
            t1 = do(PO, nc.gpsimd.memset(tmp[:], 1.0)) if PO.wait(t) is None else None
            VE.wait(t1, t)
            t = do(VE, nc.vector.tensor_tensor_scan(xb[:], tmp[:], lf[:], 0.0, mult, add))
            PE.wait(t, t_sel)
            for h in range(FOX_H):
                b = h % 4
                PE.wait(f"bank{b}")
                t = do(PE, nc.tensor.matmul(bank[b][:], sel[:, h * P:(h + 1) * P], xb[:], start=True, stop=True))
                t = act(ncum[:, h, :], bank[b][:], ACT.Copy, t, scale=-1.0)
                note(f"bank{b}", t)
            t_ncum = t
            note("scratch", t)
        enter_scratch()
        VE.wait(t_ncum)
        gq8 = sb("o_gq8", [P, 1], c=c2)
        t_gq = ts(gq8[:], vc("qnorm", 0), DH ** -0.5, None, mult, None)
        o_qn, o_kn = sb("o_qn", [P, 2, T], c=c2), sb("o_kn", [P, 2, T], c=c2)
        o_v, o_g = sb("o_v", [P, NT, 256], c=c2), sb("o_g", [P, NT, 256], c=c2)
        o_S, o_PT = sb("o_S", [P, 3, T], c=c2), sb("o_PT", [P, 2, T], c=c2)
        o_sq, o_rs = o_S, o_PT
        o_m, o_l = sb("o_m", [P, 16], c=c2), sb("o_l", [P, 16], c=c2)

        def head_norm(dst, g, src, b, *waits):
            tb = []
            for c in range(2):
                t = act(o_sq[:, c, :], bank[src + c][:], ACT.Square, waits[c], f"o_S{c}")
                PE.wait(t, f"bank{b + c}")
                tb.append(do(PE, nc.tensor.matmul(bank[b + c][:], const("block_ones"), o_sq[:, c, :],
                                                  start=True, stop=True)))
            note("o_S0", *tb)
            note("o_S1", *tb)
            for c in range(2):
                t = act(o_rs[:, c, :], bank[b + c][:], ACT.Ln, tb[c], f"o_PT{c}", scale=1.0 / DH, bias=eps[:, 0:1])
                note(f"bank{b + c}", t)
                t = act(o_rs[:, c, :], o_rs[:, c, :], ACT.Exp, t, scale=-0.5)
                t = stt(dst[:, c, :], bank[src + c][:], g, o_rs[:, c, :], mult, mult, t, "o_qk")
                note(f"bank{src + c}", t)
                note(f"o_PT{c}", t)
            return t

        def odd_body(i):
            for s, col in ((0, 0), (1, 1024), (2, 2048), (0, 3072)):
                load_wide(s, odd_w, i * 256 + col)
            load_rows(1, a["odd_w_out"][0], (i * 256, i * 256 + P))
            W.convert(1)
            W.use(0)
            tq0, tq1 = project(0, 0, 0, last=False), project(0, 1, 1)
            W.convert(2)
            W.use(1)
            tk0, tk1 = project(1, 0, 2, last=False), project(1, 1, 3)
            t_qn = head_norm(o_qn, gq8[:, 0:1], 0, 4, tq0, tq1)
            W.convert(0)
            W.use(2)
            tv = project_tokens(2, (6, 7))
            t_kn = head_norm(o_kn, vc("knorm", 0), 2, 4, tk0, tk1)
            for c in range(2):
                t_v = act(o_v[:, 2 * c:2 * c + 2, :].rearrange("p t n -> p (t n)"), bank[6 + c][:], ACT.Copy,
                          tv[c], "o_v")
                note(f"bank{6 + c}", t_v)
            W.convert(1)
            W.use(0)
            tg = project_tokens(0, (0, 1))
            for c in range(2):
                g = o_g[:, 2 * c:2 * c + 2, :].rearrange("p t n -> p (t n)")
                t = sigmoid_part(g, bank[c][:], tg[c], "o_g")
                t_g = tt(g, g, bank[c][:], mult, t)
                note(f"bank{c}", t_g)

            def scores(n):
                t, hh = n // 4, n % 4
                w, z, b = (t + 1) * P, n % 3, 4 + n % 2
                rows = slice((hh % 2) * DH, (hh % 2 + 1) * DH)
                PE.wait(f"bank{b}", t_qn, t_kn)
                x = do(PE, nc.tensor.matmul(bank[b][:, 0:w], o_qn[rows, hh // 2, t * P:w],
                                            o_kn[rows, hh // 2, 0:w], start=True, stop=True))
                S = o_S[:, z, 0:w]
                bias = ncum[:, bass.ds(i * 4 + hh, 1), 0:w].rearrange("p a w -> p (a w)")
                y = tt(S, bank[b][:, 0:w], bias, add, x, f"o_S{z}")
                note(f"bank{b}", y)
                y = tt(o_S[:, z, t * P:w], o_S[:, z, t * P:w], const("causal_add"), add, y)
                VE.wait(y)
                y = do(VE, nc.vector.tensor_reduce(o_m[:, n:n + 1], S, AX, ALU.max))
                y = ts(o_m[:, n:n + 1], o_m[:, n:n + 1], -1.0, None, mult, None, y)
                return act(S, S, ACT.Exp, y, bias=o_m[:, n:n + 1], accum_out=o_l[:, n:n + 1])

            def values(n, e):
                t, hh = n // 4, n % 4
                w, z, y, b = (t + 1) * P, n % 3, n % 2, 6 + n % 2
                PE.wait(e, f"bank{b}")
                for j in range(t + 1):
                    x = do(PE, nc.tensor.transpose(bank[b][:, j * P:(j + 1) * P],
                                                   o_S[:, z, j * P:(j + 1) * P], ident))
                note(f"o_S{z}", x)
                if n % 2:
                    x = act(o_PT[:, y, 0:w], bank[b][:, 0:w], ACT.Copy, x, f"o_PT{y}")
                else:
                    VE.wait(x, f"o_PT{y}")
                    x = do(VE, nc.vector.tensor_copy(o_PT[:, y, 0:w], bank[b][:, 0:w]))
                note(f"bank{b}", x)
                PE.wait(x, t_v)
                if hh == 0:
                    PE.wait(f"bank{t}")
                for j in range(t + 1):
                    ins = nc.tensor.matmul(bank[t][:, hh * DH:(hh + 1) * DH], o_PT[:, y, j * P:(j + 1) * P],
                                           o_v[:, j, hh * DH:(hh + 1) * DH], start=j == 0, stop=j == t)
                x = do(PE, ins, f"o_PT{y}")
                if hh == 3:
                    o3 = bank[t][:, 0:256].rearrange("p (h d) -> p h d", d=DH)
                    r = recip(o_l[:, t * 4:t * 4 + 4], o_l[:, t * 4:t * 4 + 4], e)
                    r3 = o_l[:, t * 4:t * 4 + 4].unsqueeze(2).broadcast_to((P, 4, DH))
                    g3 = o_g[:, t, :].rearrange("p (h d) -> p h d", d=DH)
                    q = tt(g3, g3, r3, mult, r, t_g)
                    q = tt(g3, o3, g3, mult, x, q)
                    note(f"bank{t}", q)
                    return q

            ahead, ready = [], []
            for n in range(16 + 2):
                if n < 16:
                    ahead.append(scores(n))
                if n >= 2:
                    ready.append(values(n - 2, ahead[n - 2]))
            note("o_qk", k.noted["o_PT1"][0])
            note("o_v", k.noted["o_PT1"][0])
            PE.wait("bank4", "bank5", ready[-1])
            for c in range(2):
                for t in range(NT):
                    x = do(PE, nc.tensor.transpose(bank[4 + c][:, t * P:(t + 1) * P],
                                                   o_g[:, t, c * P:(c + 1) * P], ident))
                r = split_oh(c, bank[4 + c][:], x)
                note(f"bank{4 + c}", r)
                if c == 0:
                    r0 = r
            note("o_g", x)
            W.convert(0)
            W.use(1)
            out_step(1, (r0, r), gate=gate[:])

        with k.rounds("odd", 4, [0, 1, 2, 0, 1]) as i:
            odd_body(i)
        note("scratch", *k.noted["acc"])
    first.close()

    enter_scratch()
    to_features(acc, const("ones"), zero8, "acc")
    for q in range(NT):
        t = ts(acc[:, q, :], acc[:, q, :], ALPHA, None, mult, None, "transposed")
    note("acc", t)
    lng, lnb = sb("lng", [P, D]), sb("lnb", [P, D])

    def ffn(l, w, last=False):
        with ExitStack() as c2:
            enter_scratch()
            f_s, f_h = sb(f"f_s{l}{w}", [P, 2, T], c=c2), sb(f"f_h{l}{w}", [P, 2, T], c=c2)
            ffn_rounds(f_s, f_h, l, w, last)
            note("scratch", *k.noted["acc"])

    def ffn_rounds(f_s, f_h, l, w, last):
        w_in, w_out = a["ffn_w_in_2"][l, w], a["ffn_w_out_2"][l, w]

        def hidden(s):
            tg, tu = project(s, 0, 2 * s, last=False), project(s, 1, 2 * s + 1)
            t = act(f_s[:, s, :], bank[2 * s][:], ACT.Silu, tg, f"f_h{s}")
            note(f"bank{2 * s}", t)
            t = tt(f_h[:, s, :], f_s[:, s, :], bank[2 * s + 1][:], mult, t, tu)
            note(f"bank{2 * s + 1}", t)
            r = split_oh(s, f_h[:, s, :], t)
            note(f"f_h{s}", r)
            return r

        def body(i, more=True):
            load_columns(0, w_in, (i * 256, i * 256 + DFF))
            load_columns(1, w_in, (i * 256 + P, i * 256 + P + DFF))
            load_rows(2, w_out, (i * 256, i * 256 + P))
            W.convert(1)
            W.convert(2)
            W.use(0)
            r0 = hidden(0)
            if more:
                W.convert(0)
            W.use(1)
            r1 = hidden(1)
            W.use(2)
            out_step(2, (r0, r1), scale=0.5)

        n = DFF // 256
        nc.scalar.preload_act_table(ACT.Silu)
        with k.rounds(f"ffn{l}{w}", n - last, [0, 1, 2]) as i:
            body(i)
        if last:
            body(n - 1, more=False)

    def layer_norm(l, m, final=False):
        at = (l * 3 + m) * KD
        PO.wait("ln_vec")
        dma("ln_vec", lng[:], a["ln_g_2"][l, m].partition_broadcast(P))
        t_vec = dma("ln_vec", lnb[:], a["ln_b_2"][l, m].partition_broadcast(P))
        VE.wait("acc")
        for q in range(NT):
            for n in range(2):
                t = do(VE, nc.vector.bn_stats(stat[:, q, 6 * n:6 * n + 6], acc[:, q, n * T:(n + 1) * T]))
        VE.wait(t)
        for q in range(NT):
            t = do(VE, nc.vector.bn_aggr(stat[:, q, 12:14], stat[:, q, 0:12]))
        t = act(stat[:, :, 14], stat[:, :, 13], ACT.Sqrt, t, bias=eps[:, 1:2])
        t = recip(stat[:, :, 14], stat[:, :, 14], t)
        for q in range(NT):
            t = ts(acc[:, q, :], acc[:, q, :], stat[:, q, 12:13], stat[:, q, 14:15], sub, mult, t)
        if not final:
            to_features(acc, vcol[:, 1, at:at + 8], vcol[:, 1, 48 + at:56 + at], t)
            t = k.noted["transposed"][0]
        scale = 1.0 if final else ALPHA
        for q in range(NT):
            g = stt(acc[:, q, :], acc[:, q, :], scale, lng[:], mult, mult, t, t_vec)
            g = stt(acc[:, q, :], lnb[:], scale, acc[:, q, :], mult, add, g)
            if final:
                SP.wait(g)
                t_out = dma("out", a["out"].rearrange("b (t p) d -> t p (b d)", p=P)[q], acc[:, q, :], nc.sync)
        note("acc", g)
        note("ln_vec", g)
        if final:
            SP.wait(t_out)

    def gla():
        m = a["gla_w_in_2"][0]
        with ExitStack() as c2:
            enter_scratch()
            low = sb("g_low", [16, T], c=c2)
            with ExitStack() as c3:
                t = narrow(m, 3072, 0, c3, "gl")
                t_low = act(low[:], bank[0][0:16, :], ACT.Copy, t)
                note("bank0", t_low)
                note("scratch", t_low)
            enter_scratch()
            g_wg = sb("g_wg", [16, P], c=c2)
            g_q, g_k, g_x, g_l, g_c64, g_c128 = (sb("g_" + n, [P, T], c=c2)
                                                for n in ("q", "k", "x", "l", "c64", "c128"))
            g_v, g_r = sb("g_v", [P, NT, 256], c=c2), sb("g_r", [P, 2, T], c=c2)
            g_E, g_d = sb("g_E", [P, 3, T], c=c2), sb("g_d", [P, 2, T], c=c2)
            g_qd, g_kinv, g_k64, g_q0, g_kend = (sb("g_" + n, [P, T], c=c2)
                                                for n in ("qd", "kinv", "k64", "q0", "kend"))
            g_ex, g_edge = sb("g_ex", [P, 3, P], c=c2), sb("g_edge", [P, NT], c=c2)
            ST = sb("g_ST", [P, NT * 640], c=c2)
            g_sq, g_rs = g_d, g_x
            t_z = do(PO, nc.gpsimd.memset(ST[:], 0.0))
            SC.wait(t_z); VE.wait(t_z); PE.wait(t_low)
            nc.scalar.preload_act_table_set("natural_log_exp_and_others")

            def body(i):
                load_columns(0, m, (i * P, i * P + 512))
                load_wide(1, m, i * 256 + 1024)
                load_wide(2, m, i * 256 + 2048)
                load_rows(1, a["gla_w_out_2"][0], (i * 256, i * 256 + P))
                PO.wait("g_wg")
                t_wg = dma("w_gate", g_wg[:], a["gla_w_gate_2"][0][:, bass.ds(i * P, P)])
                PE.wait(t_wg, "bank2")
                t = do(PE, nc.tensor.matmul(bank[2][:], g_wg[:], low[:], start=True, stop=True), "g_wg")
                t = act(g_x[:], bank[2][:], ACT.Identity, t, "g_x", bias=vc("b_gate", i))
                note("bank2", t)
                t = log_sigmoid(g_l[:], g_E[:, 0, :], g_x[:], t, "g_E")
                note("g_x", t)
                VE.wait(t, "g_c")
                do(VE, nc.vector.tensor_tensor_scan(g_c64[:], const("reset64"), g_l[:], 0.0, mult, add))
                t_c = do(VE, nc.vector.tensor_tensor_scan(g_c128[:], const("reset128"), g_l[:], 0.0, mult, add))
                W.convert(1)
                W.use(0)
                tq, tk = project(0, 0, 0, last=False), project(0, 1, 1)
                t_q = act(g_q[:], bank[0][:], ACT.Copy, tq, "g_q", scale=P ** -0.5)
                note("bank0", t_q)
                t_k = act(g_k[:], bank[1][:], ACT.Copy, tk, "g_k")
                note("bank1", t_k)
                W.convert(2)
                W.use(1)
                tv = project_tokens(1, (4, 5))
                s16 = 1.0 / 16.0
                te = act(g_E[:, 0, :], g_c64[:], ACT.Exp, t_c, scale=s16)
                t_qd = tt(g_qd[:], g_q[:], g_E[:, 0, :], mult, te, t_q, "g_diag")
                te = act(g_E[:, 1, :], g_c64[:], ACT.Exp, scale=-s16)
                t_ki = tt(g_kinv[:], g_k[:], g_E[:, 1, :], mult, te, t_k)
                te = act(g_E[:, 2, :], g_c128[:], ACT.Exp, scale=s16)
                t_q0 = tt(g_q0[:], g_q[:], g_E[:, 2, :], mult, te, "cross")
                c8, c4 = tile_view(g_c64[:], 64), tile_view(g_c128[:])
                t = tt(tile_view(g_d[:, 0, :], 64), c8[:, :, 63:64].broadcast_to((P, 8, 64)), c8, sub, "g_sq")
                t = act(g_d[:, 0, :], g_d[:, 0, :], ACT.Exp, t, scale=s16)
                t_k64 = tt(g_k64[:], g_k[:], g_d[:, 0, :], mult, t)
                t = tt(tile_view(g_d[:, 1, :]), c4[:, :, P - 1:P].broadcast_to((P, NT, P)), c4, sub)
                t = act(g_d[:, 1, :], g_d[:, 1, :], ACT.Exp, t, scale=s16)
                t_ed = act(g_edge[:], c4[:, :, P - 1], ACT.Exp, scale=s16)
                note("g_c", t_ed)
                t_kend = tt(g_kend[:], g_k[:], g_d[:, 1, :], mult, t)
                note("g_E", t_kend)
                note("g_q", t_kend)
                note("g_k", t_kend)
                for c in range(2):
                    t_v = act(g_v[:, 2 * c:2 * c + 2, :].rearrange("p t n -> p (t n)"), bank[4 + c][:],
                              ACT.Copy, tv[c], "pv")
                    note(f"bank{4 + c}", t_v)
                W.convert(1)
                W.use(2)
                tr = [project(2, 0, 2, last=False), project(2, 1, 3)]
                cross_tiles(g_q0, g_kend, g_edge, g_ex, ST[:], g_v, 4, 5, t_kend, t_ed)
                masked_diag(ST[:], const("chunk_causal"), g_kinv[:], g_qd[:], 6, t_ki)
                tp, u = masked_diag(ST[:], const("level", 6 * P, P), g_k64[:], g_qd[:], 7, t_k64)
                note("g_diag", tp)
                for c in range(2):
                    t = sigmoid_part(g_r[:, c, :], bank[2 + c][:], tr[c], "g_r")
                    t_r = tt(g_r[:, c, :], g_r[:, c, :], bank[2 + c][:], mult, t)
                    note(f"bank{2 + c}", t_r)
                tsq = []
                PE.wait(t_v, *k.noted["bank5"], *k.noted["bank4"])
                for c in range(2):
                    tp = head_values(6 + c, g_v[:], c, ST[:], u)
                    tsq.append(act(g_sq[:, c, :], bank[6 + c][:], ACT.Square, tp, "g_E", "g_sq"))
                note("pv", tp)
                PE.wait("bank0")
                for c in range(2):
                    PE.wait(tsq[c])
                    ins = nc.tensor.matmul(bank[0][:], ones, g_sq[:, c, :], start=c == 0, stop=c == 1)
                t = do(PE, ins, "g_sq")
                t = act(g_rs[:], bank[0][:], ACT.Ln, t, scale=1.0 / 256, bias=eps[:, 0:1])
                note("bank0", t)
                t = act(g_rs[:], g_rs[:], ACT.Exp, t, scale=-0.5)
                r = []
                for c in range(2):
                    u = stt(g_sq[:, c, :], bank[6 + c][:], vc("gla_g", c), g_rs[:], mult, mult, t, "g_sq")
                    note(f"bank{6 + c}", u)
                    u = tt(g_r[:, c, :], g_r[:, c, :], g_sq[:, c, :], mult, u)
                    r.append(split_oh(c, g_r[:, c, :], u))
                note("g_x", u)
                note("g_sq", u)
                note("g_r", r[1])
                W.convert(0)
                W.use(1)
                out_step(1, r)

            with k.rounds("gla", NH, [0, 1, 2, 1]) as i:
                body(i)
            note("scratch", *k.noted["acc"])

    def retention():
        m = a["ret_w_in_2"][0]
        with ExitStack() as c2:
            enter_scratch()
            rope, dec = sb("r_rope", [P, 2, T], c=c2), sb("r_dec", [P, NH, T], c=c2)
            t1 = dma("rope", rope[:], a["rope"])
            t2 = dma("decay", dec[:], a["ret_decay"])
            ng = sb("r_ng", [P, T], c=c2)
            t3 = dma("ret_g", ng[:], a["ret_norm_g_2"][0].partition_broadcast(P))
            VE.wait(t1, t2, t3)
            qr, kr = sb("r_q", [P, 2, T], c=c2), sb("r_k", [P, 2, T], c=c2)
            r_t = val
            r_v, r_g = sb("r_v", [P, NT, T], c=c2), sb("r_g", [P, NT, T], c=c2)
            ST = sb("r_ST", [P, NT, T], c=c2)
            o2_hi, o2_lo = sb("o2_hi", [P, 2, T], F32R, c2), sb("o2_lo", [P, 2, T], F32R, c2)
            cos, sin = rope[:, 0, :], rope[:, 1, :]
            nc.scalar.preload_act_table_set("natural_log_exp_and_others")

            def rotate(dst, b, tks, *waits):
                x1, x2 = bank[b][:], bank[b + 1][:]
                t = tt(dst[:, 0, :], x1, cos, mult, *tks, *waits)
                u = tt(r_t[:, 0, :], x2, sin, mult)
                t = tt(dst[:, 0, :], dst[:, 0, :], r_t[:, 0, :], sub, u)
                t = tt(dst[:, 1, :], x1, sin, mult)
                note(f"bank{b}", t)
                u = tt(r_t[:, 1, :], x2, cos, mult)
                note(f"bank{b + 1}", u)
                return tt(dst[:, 1, :], dst[:, 1, :], r_t[:, 1, :], add, u)

            def body(i):
                for s, col in ((0, i * 256), (1, i * 256 + 1024), (2, i * 512 + 2048), (0, i * 512 + 2304),
                               (1, i * 512 + 4096), (2, i * 512 + 4352)):
                    load_wide(s, m, col)
                for s in range(2):
                    load_rows(s, a["ret_w_out_2"][0], (i * 512 + s * 256, i * 512 + s * 256 + P))
                W.convert(1)
                W.use(0)
                tq = [project(0, 0, 0, last=False), project(0, 1, 1)]
                t_q = rotate(qr, 0, tq, "r_qk")
                W.convert(2)
                W.use(1)
                tk = [project(1, 0, 2, last=False), project(1, 1, 3)]
                t_k = rotate(kr, 2, tk)
                for half in range(2):
                    W.convert(half)
                    W.use((2, 0)[half])
                    tv = project_tokens((2, 0)[half], (4 + 2 * half, 5 + 2 * half))
                    for c in range(2):
                        b = 4 + 2 * half + c
                        t_v = act(r_v[:, 2 * c:2 * c + 2, half * 256:half * 256 + 256],
                                  bank[b][:].rearrange("p (t n) -> p t n", n=256), ACT.Copy, tv[c], "pv")
                        note(f"bank{b}", t_v)
                for half in range(2):
                    W.convert((2, 0)[half])
                    W.use((1, 2)[half])
                    tg = project_tokens((1, 2)[half], (0 + 2 * half, 1 + 2 * half))
                    for c in range(2):
                        b = 2 * half + c
                        g = r_g[:, 2 * c:2 * c + 2, half * 256:half * 256 + 256]
                        x = bank[b][:].rearrange("p (t n) -> p t n", n=256)
                        t = sigmoid_part(g, x, tg[c], "r_g")
                        t_g = tt(g, g, x, mult, t)
                        note(f"bank{b}", t_g)
                for j in range(NT):
                    PE.wait(f"bank{4 + j}", t_q, t_k)
                    w = T - j * P
                    for c in range(2):
                        ins = nc.tensor.matmul(bank[4 + j][:, 0:w], kr[:, c, j * P:(j + 1) * P],
                                               qr[:, c, j * P:T], start=c == 0, stop=c == 1)
                    t = do(PE, ins)
                    t_S = tt(ST[:, j, 0:w], bank[4 + j][:, 0:w],
                             dec[:, bass.ds(i, 1), 0:w].rearrange("p a w -> p (a w)"), mult, t, "pv")
                    note(f"bank{4 + j}", t_S)
                note("r_qk", t)
                PE.wait(t_S, t_v)
                for q in range(NT):
                    PE.wait(f"bank{q}")
                    for j in range(q + 1):
                        ins = nc.tensor.matmul(bank[q][:], ST[:, j, (q - j) * P:(q - j + 1) * P], r_v[:, j, :],
                                               start=j == 0, stop=j == q)
                    tp = do(PE, ins)
                    VE.wait(tp)
                    t = do(VE, nc.vector.bn_stats(stat[:, q, 0:6], bank[q][:]))
                    wait_apart(t)
                    t = do(VE, nc.vector.bn_aggr(stat[:, q, 12:14], stat[:, q, 0:6]))
                    t = act(stat[:, q, 14:15], stat[:, q, 13:14], ACT.Ln, t, bias=eps[:, 0:1])
                    t = act(stat[:, q, 14:15], stat[:, q, 14:15], ACT.Exp, t, scale=-0.5)
                    t = ts(r_t[:, q % 2, :], bank[q][:], stat[:, q, 12:13], stat[:, q, 14:15], sub, mult, t)
                    note(f"bank{q}", t)
                    t = tt(r_t[:, q % 2, :], r_t[:, q % 2, :], ng[:], mult, t)
                    t = tt(r_g[:, q, :], r_g[:, q, :], r_t[:, q % 2, :], mult, t)
                note("pv", tp)
                PE.wait(t)
                r = []
                for c in range(4):
                    PE.wait(f"bank{4 + c}")
                    for q in range(NT):
                        x = do(PE, nc.tensor.transpose(bank[4 + c][:, q * P:(q + 1) * P],
                                                       r_g[:, q, c * P:(c + 1) * P], ident))
                    own = {} if c < 2 else {"hi": o2_hi, "lo": o2_lo, "free": "o2"}
                    r.append(split_oh(c % 2, bank[4 + c][:], x, **own))
                    note(f"bank{4 + c}", r[-1])
                note("r_g", x)
                W.convert(1)
                W.use(0)
                out_step(0, r[0:2])
                W.convert(0)
                W.use(1)
                out_step(1, r[2:4], hi=o2_hi, lo=o2_lo, free="o2")

            with k.rounds("ret", NH, [0, 1, 2, 0, 1, 2, 0, 1]) as i:
                body(i)
            note("scratch", *k.noted["acc"])

    ffn(0, 0)
    layer_norm(0, 0)
    gla()
    layer_norm(0, 1)
    ffn(0, 1)
    layer_norm(0, 2)
    ffn(1, 0)
    layer_norm(1, 0)
    retention()
    layer_norm(1, 1)
    ffn(1, 1, last=True)
    layer_norm(1, 2, final=True)


_INS = ["x", "c", "norm_g", "ada_w", "ada_b", "hgrn_lb", "even_w_in", "hgrn_onorm_g", "pool_w", "pool_scale",
        "even_w_out", "odd_w_in", "fox_b_f", "fox_qnorm_g", "fox_knorm_g", "odd_w_out", "ffn_w_in_2",
        "ffn_w_out_2", "ln_g_2", "ln_b_2", "gla_w_in_2", "gla_w_gate_2", "gla_b_gate_2", "gla_norm_g_2",
        "gla_w_out_2", "ret_w_in_2", "ret_norm_g_2", "ret_w_out_2"]


def kernel(**inputs):
    import numpy as _np
    import concourse.bacc as _bacc
    from concourse import mybir as _mybir
    from concourse.bass_utils import run_bass_kernel_spmd as _run

    arrays = {n: _np.ascontiguousarray(inputs[n]) for n in _INS}
    arrays.update(constant_tables())
    counts = {}
    for _ in range(2):
        nc = _bacc.Bacc("TRN2", target_bir_lowering=False, num_devices=1)
        dt = _mybir.dt.float32
        a = {n: nc.dram_tensor(f"in_{n}", v.shape, dt, kind="ExternalInput").ap() for n, v in arrays.items()}
        a["out"] = nc.dram_tensor("out", (1, T, D), dt, kind="ExternalOutput").ap()
        counts = build(nc, a, counts)
    r = _run(nc, [{f"in_{n}": v for n, v in arrays.items()}], core_ids=[0])
    return r.results[0]["out"]
```

```python
from collections import defaultdict
from contextlib import ExitStack, contextmanager

import numpy as np
import concourse.bass as bass
from concourse import mybir

F32 = mybir.dt.float32
F32R = mybir.dt.float32r
I32 = mybir.dt.int32
ALU = mybir.AluOpType
ACT = mybir.ActivationFunctionType
AX = mybir.AxisListType.X

P = 128
T = 512
NT = T // P
D = 1024
KD = D // P
PIECE = 2048
SLOTS = 3
DFF = 2816
NH = 4
FOX_H = 16
DH = 64
EPS = 1e-6
LN_EPS = 1e-5
ALPHA = 4.0 ** 0.25
NEG = -1e30
CREDIT = 512
LEVELS = (1, 2, 4, 8, 16, 32, 64)


def _columns():
    at, out = 0, {}
    for name, n in (("ident", P), ("ones", P), ("block_ones", P), ("level", P * len(LEVELS)),
                    ("chunk_causal", P), ("causal_add", P), ("reset128", T), ("reset64", T),
                    ("pool_on", 16), ("pool_w", 4), ("pool_head", 64)):
        out[name] = (at, n)
        at += n
    return out, at


COLS, NCOLS = _columns()


def constant_tables():
    c = np.zeros((P, NCOLS), np.float32)

    def put(name, a):
        c[:, COLS[name][0]:COLS[name][0] + COLS[name][1]] = a

    i = np.arange(P)
    put("ident", np.eye(P))
    put("ones", 1.0)
    put("block_ones", (i[:, None] // DH) == (i[None, :] // DH))
    s, t = i[:, None], i[None, :]
    put("level", np.concatenate([((s // (2 * h)) == (t // (2 * h))) & (s % (2 * h) < h) & (t % (2 * h) >= h)
                                 for h in LEVELS], axis=1))
    put("chunk_causal", (s // 64 == t // 64) & (t >= s))
    put("causal_add", np.where(t > s, NEG, 0.0))
    tok = np.arange(T)
    put("reset128", (tok % 128 != 0)[None, :])
    put("reset64", (tok % 64 != 0)[None, :])
    wins = (2, 4, 8, 16)
    put("pool_on", np.array([[w >= 2 ** (k + 1) for k in range(4)] for w in wins]).reshape(1, 16))
    put("pool_w", np.array([[1.0 / w for w in wins]]))
    put("pool_head", np.array([[w / min(n + 1, w) for n in range(16)] for w in wins]).reshape(1, 64))
    dh = D // 4
    inv = (10000.0 ** (-np.arange(0, dh, 2, dtype=np.float32) / np.float32(dh))).astype(np.float32)
    ang = inv[:, None] * np.arange(T, dtype=np.float32)[None, :]
    rope = np.stack([np.cos(ang), np.sin(ang)], axis=1).astype(np.float32)
    lg = np.log(1.0 - 2.0 ** (-5.0 - np.arange(NH)))
    lag = tok[None, None, :] - i[:, None, None]
    decay = np.where(lag >= 0, np.exp(np.maximum(lag, 0) * lg[None, :, None]), 0.0) * dh ** -0.5
    return {"consts": c, "rope": rope,
            "ret_decay": decay.astype(np.float32)}


class Token:

    def __init__(self, prog, value, loop):
        self.prog, self.value, self.loop = prog, value, loop


class Progress:

    def __init__(self, k, name, eng, inc=1, credit=0):
        self.k, self.name, self.eng, self.inc = k, name, eng, inc
        self.sem = k.sem("s_" + name)
        self.n = credit
        self.seen = {}
        k.progs.append(self)

    def wait(self, *tokens):
        for t in tokens:
            if isinstance(t, str):
                self.k.wait_noted(self, t)
            elif isinstance(t, (list, tuple)):
                self.wait(*t)
            elif t is not None:
                self.k.wait_token(self, t)


class Kernel:
    def __init__(self, nc, ctx, counts):
        self.nc, self.ctx, self.counts = nc, ctx, counts
        self.loop, self.progs, self.noted, self.found = None, [], {}, {}

    def sem(self, name):
        return self.ctx.enter_context(self.nc.semaphore(name))

    def wait_token(self, me, t):
        L = self.loop
        if L is not None and t.loop is L:
            key = (t.prog.name, L.name)
            if me.seen.get(key, -1) < t.value:
                me.seen[key] = t.value
                me.eng.wait_ge(t.prog.sem, L.i * L.per(t.prog) + t.value if L.per(t.prog) else t.value)
            return
        value = t.value if t.loop is None else t.value + (t.loop.n - 1) * t.loop.per(t.prog)
        key = t.prog.name if L is None else (t.prog.name, L.name, "before")
        if max(me.seen.get(t.prog.name, -1), me.seen.get(key, -1)) < value:
            me.seen[key] = value
            me.eng.wait_ge(t.prog.sem, value)

    def wait_noted(self, me, name):
        L, got = self.loop, self.noted.get(name, [])
        if L is None or (got and got[0].loop is L):
            for t in got:
                self.wait_token(me, t)
            return
        for t in got:
            self.wait_token(me, t)
        for prog, off in L.last.get(name, []):
            p = self.prog(prog)
            if (me.seen.get((prog, L.name), -1)) >= 0:
                continue
            key = (prog, L.name, "last")
            if me.seen.get(key, -1) < off:
                me.seen[key] = off
                value = L.start[prog] + off - L.per(p)
                assert value > 0 or L.dry, (name, prog, value)
                me.eng.wait_ge(p.sem, L.i * L.per(p) + max(value, 1))

    def prog(self, name):
        return next(p for p in self.progs if p.name == name)

    @contextmanager
    def rounds(self, name, n, pieces):
        L = Loop(self, name, n, pieces)
        with self.nc.Fori(0, n) as i:
            L.i = i
            self.loop = L
            yield i
            self.loop = None
        L.end()
        self.weights.end_loop(n, pieces)


class Loop:
    def __init__(self, k, name, n, pieces):
        self.k, self.name, self.n, self.pieces = k, name, n, pieces
        known = k.counts.get(name)
        self.dry = known is None
        self.pers = {} if self.dry else known["per"]
        self.last = {} if self.dry else known["last"]
        self.start = defaultdict(int, {p.name: p.n for p in k.progs})

    def per(self, prog):
        return self.pers.get(prog.name, 0)

    def end(self):
        per = {p.name: p.n - self.start[p.name] for p in self.k.progs}
        last = {a: [(t.prog.name, t.value - self.start[t.prog.name]) for t in b]
                for a, b in self.k.noted.items() if b and b[0].loop is self}
        if not self.dry:
            assert per == self.pers and last == self.last, self.name
        self.k.found[self.name] = {"per": per, "last": last}
        self.pers = per
        for p in self.k.progs:
            p.n = self.start[p.name] + self.n * per[p.name]


class Weights:

    def __init__(self, k, raw, hi, lo):
        self.k, self.raw, self.hi, self.lo = k, raw, hi, lo
        self.loaded = [k.sem(f"s_loaded{s}") for s in range(SLOTS)]
        self.rounded = [k.sem(f"s_rounded{s}") for s in range(SLOTS)]
        self.split = [k.sem(f"s_split{s}") for s in range(SLOTS)]
        for s in range(SLOTS):
            k.nc.vector.sem_inc(self.split[s], 1)
        self.n = {what: [0] * SLOTS for what in ("load", "convert", "use")}

    def number(self, what, s, k=1, plus=0):
        L, n = self.k.loop, self.n[what][s]
        if L is None:
            return n * k + plus
        return L.i * (L.pieces.count(s) * k) + (n * k + plus)

    def end_loop(self, n, pieces):
        for what in self.n:
            for s in range(SLOTS):
                self.n[what][s] += (n - 1) * pieces.count(s)

    def load(self, s, halves):
        self.n["load"][s] += 1
        sp = self.k.nc.sync
        sp.wait_ge(self.split[s], self.number("load", s))
        for dst, src in halves:
            sp.dma_start(dst, src).then_inc(self.loaded[s], 16)

    def convert(self, s, gate=None):
        self.n["convert"][s] += 1
        k, nc = self.k, self.k.nc
        if gate is None:
            nc.scalar.wait_ge(self.loaded[s], self.number("convert", s, k=32))
        else:
            nc.gpsimd.wait_ge(self.loaded[s], self.number("convert", s, k=32))
            po = k.prog("pool")
            po.wait("gate")
            raw = self.raw[:, s, :].rearrange("p (c n) -> p c n", n=D)
            ins = nc.gpsimd.tensor_tensor(raw, raw, gate.unsqueeze(1).broadcast_to((P, 2, D)), ALU.mult)
            ins.then_inc(po.sem, 1)
            po.n += 1
            k.prog("act").wait(Token(po, po.n, k.loop))
        k.prog("act").wait(f"used{s}")
        nc.scalar.activation(self.hi[:, s, :], self.raw[:, s, :], ACT.Copy).then_inc(self.rounded[s], 1)
        nc.vector.wait_ge(self.rounded[s], self.number("convert", s))
        nc.vector.tensor_tensor(self.lo[:, s, :], self.raw[:, s, :], self.hi[:, s, :].bitcast(F32),
                                ALU.subtract).then_inc(self.split[s], 1)

    def use(self, s):
        self.n["use"][s] += 1
        self.k.nc.tensor.wait_ge(self.split[s], self.number("use", s, plus=1))


def build(nc, a, counts):
    with ExitStack() as ctx:
        k = Kernel(nc, ctx, counts)
        emit(nc, ctx, k, a)
        return k.found


def emit(nc, ctx, k, a):
    def sb(name, shape, dt=F32, c=ctx):
        return c.enter_context(nc.sbuf_tensor(name, shape, dt))

    psum = ctx.enter_context(nc.psum_tensor("psum", [P, 8, T], F32))
    bank = [psum[:, b, :] for b in range(8)]
    acc = sb("acc", [P, NT, D])
    h_hi, h_lo = sb("h_hi", [P, KD, T], F32R), sb("h_lo", [P, KD, T], F32R)
    w_raw = sb("w_raw", [P, SLOTS, PIECE])
    w_hi, w_lo = sb("w_hi", [P, SLOTS, PIECE], F32R), sb("w_lo", [P, SLOTS, PIECE], F32R)
    oh_hi, oh_lo = sb("oh_hi", [P, 2, T], F32R), sb("oh_lo", [P, 2, T], F32R)
    consts = sb("consts", [P, NCOLS])
    vcol = sb("vcol", [P, 2, P])
    eps = sb("eps", [P, 3])
    alpha = sb("alpha", [P, 1])
    zero8, spare = sb("zero8", [P, KD]), sb("spare", [P, 1])
    col8 = sb("col8", [P, 2, KD])
    val = sb("val", [P, 4, T])
    stat = sb("stat", [P, NT, 24])

    def const(name, lo=0, n=None):
        at, size = COLS[name]
        return consts[:, at + lo:at + lo + (size - lo if n is None else n)]

    ident, ones = const("ident"), const("ones")

    PE = Progress(k, "pe", nc.tensor, credit=CREDIT)
    SC = Progress(k, "act", nc.scalar, credit=CREDIT)
    VE = Progress(k, "dve", nc.vector, credit=CREDIT)
    PO = Progress(k, "pool", nc.gpsimd, credit=CREDIT)
    SP = Progress(k, "sp", nc.sync)
    for e in (PE, SC, VE, PO):
        e.eng.sem_inc(e.sem, CREDIT)
    W = k.weights = Weights(k, w_raw, w_hi, w_lo)

    def do(e, ins, note=None):
        ins.then_inc(e.sem, e.inc)
        e.n += e.inc
        t = Token(e, e.n, k.loop)
        if note:
            k.noted[note] = [t]
        return t

    def note(name, *tokens):
        k.noted[name] = [t for t in tokens if t is not None]

    queues = {}

    def dma(name, out, in_, eng=None):
        if name not in queues:
            queues[name] = Progress(k, "dma_" + name, eng or nc.gpsimd, inc=16)
        q = queues[name]
        return do(q, q.eng.dma_start(out, in_))

    def act(out, in_, func, *waits, **kw):
        SC.wait(*waits)
        return do(SC, nc.scalar.activation(out, in_, func, **kw))

    def tt(out, x, y, op, *waits, e=VE):
        e.wait(*waits)
        return do(e, e.eng.tensor_tensor(out, x, y, op))

    def ts(out, x, s1, s2, op0, op1, *waits, e=VE):
        e.wait(*waits)
        if s2 is None:
            return do(e, e.eng.tensor_scalar(out, x, s1, None, op0))
        return do(e, e.eng.tensor_scalar(out, x, s1, s2, op0, op1))

    def stt(out, x, s, y, op0, op1, *waits):
        VE.wait(*waits)
        return do(VE, nc.vector.scalar_tensor_tensor(out, x, s, y, op0, op1))

    def recip(out, x, *waits):
        VE.wait(*waits)
        return do(VE, nc.vector.reciprocal(out, x))

    def enter_scratch():
        for e in (SC, VE, PO):
            e.wait("scratch")

    def wait_apart(*tokens):
        VE.wait(*tokens, "spare")
        do(VE, nc.vector.memset(spare[:], 0.0), "spare")

    mult, add, sub = ALU.mult, ALU.add, ALU.subtract

    def three(out, ws, wl, xs, xl, first, last):
        nc.tensor.matmul(out, ws, xs, start=first, stop=False)
        nc.tensor.matmul(out, ws, xl, start=False, stop=False)
        return nc.tensor.matmul(out, wl, xs, start=False, stop=last)

    def project(s, c, b, last=True):
        PE.wait(f"bank{b}", "h7")
        for kk in range(KD):
            w = slice(kk * 256 + c * P, kk * 256 + (c + 1) * P)
            ins = three(bank[b][:], w_hi[:, s, w], w_lo[:, s, w], h_hi[:, kk, :], h_lo[:, kk, :],
                        kk == 0, kk == KD - 1)
        if last:
            return do(PE, ins, f"used{s}")
        return do(PE, ins)

    def project_steps(s, b0, b1):
        PE.wait(f"bank{b0}", f"bank{b1}")
        for kk in range(KD):
            PE.wait(f"h{kk}")
            for c, b in enumerate((b0, b1)):
                w = slice(kk * 256 + c * P, kk * 256 + (c + 1) * P)
                ins = three(bank[b][:], w_hi[:, s, w], w_lo[:, s, w], h_hi[:, kk, :], h_lo[:, kk, :],
                            kk == 0, kk == KD - 1)
            if kk < KD - 1:
                yield
        done = do(PE, ins, f"used{s}")
        k.noted["project"] = [done]
        yield

    def project_pair(s, b0, b1):
        for _ in project_steps(s, b0, b1):
            pass
        return k.noted["project"][0]

    def project_tokens(s, banks, c0=0, n=256, last=True):
        per = T // n
        done = []
        for t in range(NT):
            b = banks[t // per]
            if t % per == 0:
                PE.wait(f"bank{b}", "h7")
            o = bank[b][:, (t % per) * n:(t % per + 1) * n]
            for kk in range(KD):
                w = slice(kk * 256 + c0, kk * 256 + c0 + n)
                x = slice(t * P, (t + 1) * P)
                nc.tensor.matmul(o, h_hi[:, kk, x], w_hi[:, s, w], start=kk == 0, stop=False)
                nc.tensor.matmul(o, h_lo[:, kk, x], w_hi[:, s, w], start=False, stop=False)
                ins = nc.tensor.matmul(o, h_hi[:, kk, x], w_lo[:, s, w], start=False, stop=kk == KD - 1)
            if t == NT - 1 and last:
                done.append(do(PE, ins, f"used{s}"))
            elif t % per == per - 1:
                done.append(do(PE, ins))
        return done

    def split_oh(c, value, *waits, hi=oh_hi, lo=oh_lo, free="oh"):
        t1 = act(hi[:, c, :], value, ACT.Copy, free, *waits)
        t2 = tt(lo[:, c, :], value, hi[:, c, :].bitcast(F32), sub, t1)
        return t2

    def out_step(s, ready, scale=1.0, order=(0, 1), hi=oh_hi, lo=oh_lo, free="oh", then=None):
        outs = [(t, n) for t in range(NT) for n in range(2)]

        def part(j, c, first, last):
            t, n = outs[j]
            b = 4 + j % 4
            x, w = slice(t * P, (t + 1) * P), slice(c * D + n * T, c * D + (n + 1) * T)
            nc.tensor.matmul(bank[b][:], hi[:, c, x], w_hi[:, s, w], start=first, stop=False)
            nc.tensor.matmul(bank[b][:], lo[:, c, x], w_hi[:, s, w], start=False, stop=False)
            return nc.tensor.matmul(bank[b][:], hi[:, c, x], w_lo[:, s, w], start=False, stop=last)

        def evacuate(j, done):
            t, n = outs[j]
            b = 4 + j % 4
            dst = acc[:, t, n * T:(n + 1) * T]
            e = stt(dst, bank[b][:], scale, dst, mult, add, done, "acc")
            note(f"bank{b}", e)
            return e

        if then:
            nc.scalar.preload_act_table_set("natural_log_exp_and_others")
        PE.wait(ready[0])
        for j in range(4):
            PE.wait(f"bank{4 + j}")
            part(j, order[0], True, False)
        PE.wait(ready[1])
        last = None
        for j in range(8):
            if j >= 4:
                PE.wait(f"bank{4 + j % 4}")
                part(j, order[0], True, False)
            ins = part(j, order[1], False, True)
            if j == 7:
                done = do(PE, ins, f"used{s}")
                note(free, done)
            else:
                done = do(PE, ins)
            last = evacuate(j, done)
            if then and j % 2 == 1:
                then.tile(j // 2, last)
        note("acc", last)
        if then:
            then.features()

    def wview(s, n=256):
        return w_raw[:, s, :].rearrange("p (k n) -> p k n", n=n)

    def load_columns(s, m, cols):
        v = m.rearrange("(k p) n -> p k n", p=P)
        W.load(s, [(wview(s)[:, :, c * P:(c + 1) * P], v[:, :, bass.ds(cols[c], P)]) for c in range(2)])

    def load_wide(s, m, col):
        v = m.rearrange("(k p) n -> p k n", p=P)
        W.load(s, [(wview(s)[:, c * 4:c * 4 + 4, :], v[:, c * 4:c * 4 + 4, bass.ds(col, 256)]) for c in range(2)])

    def load_rows(s, m, rows):
        W.load(s, [(w_raw[:, s, c * D:(c + 1) * D], m[bass.ds(rows[c], P), :]) for c in range(2)])

    def sigmoid_part(tmp, x, *waits):
        t = act(tmp, x, ACT.Exp, *waits, scale=-1.0)
        t = ts(tmp, tmp, 1.0, None, add, None, t)
        return recip(tmp, tmp, t)

    t_x = dma("x", acc[:], a["x"].rearrange("b (t p) d -> p (b t) d", p=P))
    k.noted["acc"] = [t_x]

    vrow = val[:, 0, 0:2 * P].rearrange("p (g n) -> p g n", n=P)
    ve_t = do(VE, nc.vector.memset(vrow, 0.0))
    do(PO, nc.gpsimd.memset(eps[:, 0:1], EPS))
    do(PO, nc.gpsimd.memset(eps[:, 1:2], LN_EPS))
    do(PO, nc.gpsimd.memset(zero8[:], 0.0))
    do(PO, nc.gpsimd.memset(alpha[:], ALPHA))
    t_eps = do(PO, nc.gpsimd.memset(eps[:, 2:3], 1.0))
    for e in (SC, VE, PE):
        e.wait(t_eps)
    vec, at = {}, 0
    SP.wait(ve_t)
    for name, src, n in (
            ("c", a["c"].rearrange("b (j p) -> (b j) p", p=P), 8),
            ("ada_b", a["ada_b"].rearrange("l (j p) -> (l j) p", p=P), 48),
            ("norm_g", a["norm_g"].rearrange("l (j p) -> (l j) p", p=P), 16),
            ("lb", a["hgrn_lb"].rearrange("l (j p) -> (l j) p", p=P), 12),
            ("onorm", a["hgrn_onorm_g"].rearrange("l (j p) -> (l j) p", p=P), 4),
            ("pool_scale", a["pool_scale"].rearrange("l (j p) -> (l j) p", p=P), 4),
            ("b_gate", a["gla_b_gate_2"].rearrange("l (j p) -> (l j) p", p=P), 4),
            ("gla_g", a["gla_norm_g_2"].rearrange("l (j p) -> (l j) p", p=P), 2)):
        t_v = dma("vec", vrow[at:at + n, 0, :], src, nc.sync)
        vec[name] = at
        at += n
    for name, src in (("qnorm", a["fox_qnorm_g"]), ("knorm", a["fox_knorm_g"])):
        for half in range(2):
            t_v = dma("vec", vrow[at:at + 1, 0, half * DH:(half + 1) * DH], src, nc.sync)
        vec[name] = at
        at += 1
    assert at <= P
    t_v = dma("vec", vrow[0:48, 1, :], a["ln_g_2"].rearrange("l m (j p) -> (l m j) p", p=P), nc.sync)
    t_v = dma("vec", vrow[48:96, 1, :], a["ln_b_2"].rearrange("l m (j p) -> (l m j) p", p=P), nc.sync)
    fb = sb("fox_b", [FOX_H, 1])
    t_fb = dma("vec", fb[:], a["fox_b_f"].rearrange("a h -> h a"), nc.sync)
    narrow_raw = sb("narrow_raw", [P, 2, KD, 16])
    for n, m in enumerate((a["odd_w_in"][0][:, 4096:4112], a["gla_w_in_2"][0][:, 3072:3088])):
        t_narrow = dma("narrow", narrow_raw[:, n, :, :], m.rearrange("(k p) n -> p k n", p=P), nc.sync)
    t_consts = dma("consts", consts[:], a["consts"], nc.scalar)
    for e in (SC, VE, PE):
        e.wait(t_fb, t_consts)
    for g in range(2):
        t_tr = do(PE, nc.tensor.transpose(bank[0][:, g * P:(g + 1) * P], vrow[:, g, :], ident))
    SC.wait(t_tr)
    t_vc = act(vcol[:].rearrange("p g n -> p (g n)"), bank[0][:, 0:2 * P], ACT.Copy)
    note("bank0", t_vc)

    def vc(name, j, n=1, g=0):
        return vcol[:, g, bass.ds(vec[name] + j, n)]

    lbt = sb("lbt", [P, 12])
    lb, oml = sb("lb", [P, 4]), sb("oml", [P, 4])
    x = [vcol[:, 0, vec["lb"] + 4 * r:vec["lb"] + 4 * r + 4] for r in range(3)]
    t = tt(lb[:], x[0], x[1], ALU.max, t_vc)
    t = tt(lb[:], lb[:], x[2], ALU.max, t)
    for r in range(3):
        t = tt(lbt[:, 4 * r:4 * r + 4], x[r], lb[:], sub, t)
    t = act(lbt[:], lbt[:], ACT.Exp, t)
    t = tt(lb[:], lbt[:, 0:4], lbt[:, 4:8], add, t)
    t = tt(lb[:], lb[:], lbt[:, 8:12], add, t)
    t = recip(lb[:], lb[:], t)
    t = tt(lb[:], lb[:], lbt[:, 0:4], mult, t)
    t_lb = ts(oml[:], lb[:], -1.0, 1.0, mult, add, t)

    cond = sb("cond", [P, 8])
    sg = sb("sg", [P, 8])
    t = sigmoid_part(sg[:], vc("c", 0, 8))
    t_cond = tt(cond[:], vc("c", 0, 8), sg[:], mult, t)

    mod = sb("mod", [P, 2, 24])
    first = ctx.enter_context(ExitStack())
    gate = sb("gate", [P, D], c=first)
    AR = 3
    ada_buf = ctx.enter_context(ExitStack())
    ada_loaded = [k.sem(f"s_ada_loaded{r}") for r in range(AR)]

    ada_sum = val[:, 2:4, :].rearrange("p a (j n) -> p (a j) n", n=P)

    def ada_load(i, j):
        r = j % AR
        SP.wait(f"ada{r}")
        nc.sync.dma_start(ada_raw[:, r, :].rearrange("p (k n) -> p k n", n=P),
                          a["ada_w"][1].rearrange("(k p) n -> p k n", p=P)[:, :, bass.ds(i * 768 + j * P, P)]
                          ).then_inc(ada_loaded[r], 16)

    def ada_piece(i, j):
        r = j % AR
        nc.gpsimd.wait_ge(ada_loaded[r], i * 32 + 16 * (j // AR + 1))
        w = ada_raw[:, r, :]
        t = tt(w.rearrange("p (k n) -> p k n", n=P), w.rearrange("p (k n) -> p k n", n=P),
               cond[:].unsqueeze(2).broadcast_to((P, KD, P)), mult, "ada_sum", e=PO)
        t = tt(w[:, 0:512], w[:, 0:512], w[:, 512:1024], add, t, e=PO)
        t = tt(w[:, 0:256], w[:, 0:256], w[:, 256:512], add, t, e=PO)
        t = tt(ada_sum[:, j, :], w[:, 0:P], w[:, P:2 * P], add, t, e=PO)
        note(f"ada{r}", t)
        if j + AR < 6:
            ada_load(i, j + AR)
        return t

    def ada_columns(i, b, ready):
        PE.wait(ready, f"bank{b}")
        for j in range(6):
            ins = nc.tensor.matmul(bank[b][:, j:j + 1], ada_sum[:, j, :], ones[:, 0:1], start=True, stop=True)
        t = do(PE, ins, "ada_sum")
        t = tt(mod[:, 1, bass.ds(i * 6, 6)], bank[b][:, 0:6], vc("ada_b", 24 + i * 6, 6), add, t)
        note(f"bank{b}", t)
        note("mod", t)

    even_w, odd_w = a["even_w_in"][0], a["odd_w_in"][0]

    diag4 = val[:, 3, :].rearrange("p (t n) -> p t n", n=P)

    class Boundary:

        def __init__(self, gain, shift, by_diag=False):
            self.gain, self.shift, self.by_diag = gain, shift, by_diag
            self.ready = [None] * NT

        def tile(self, t, ready):
            self.ready[t] = ready

        def features(self):
            lo4, hi4 = range(4), range(4, KD)
            order = ((0, lo4), (1, lo4), (0, hi4), (1, hi4), (2, lo4), (2, hi4), (3, lo4), (3, hi4))
            for t, chunks in order:
                PE.wait(self.ready[t])
                rhs = diag4[:, t, :] if self.by_diag else ident
                for j in chunks:
                    if t == 0:
                        PE.wait(f"bank{j}")
                    o, x = bank[j][:, t * P:(t + 1) * P], acc[:, t, j * P:(j + 1) * P]
                    if self.by_diag:
                        ins = nc.tensor.matmul(o, x, rhs, start=True, stop=True)
                    else:
                        ins = nc.tensor.transpose(o, x, rhs)
                done = do(PE, ins)
                if t == 3 and chunks is lo4:
                    done4 = done
            note("transposed", done)
            if self.by_diag:
                note("val3", done)
            g, b = self.gain, self.shift

            def parts(j):
                d = done4 if j < 4 else done
                x, v = bank[j][:], val[:, j % 4, :]
                if j % 2 == 0:
                    hi = act(h_hi[:, j, :], x, ACT.Identity, d, scale=g[:, j:j + 1], bias=b[:, j:j + 1])
                    f = act(v, x, ACT.Identity, f"val{j % 4}", scale=g[:, j:j + 1], bias=b[:, j:j + 1])
                else:
                    f = ts(v, x, g[:, j:j + 1], b[:, j:j + 1], mult, add, d, f"val{j % 4}")
                    hi = act(h_hi[:, j, :], v, ACT.Copy, f)
                note(f"bank{j}", f)
                return hi, f

            made = [parts(0)]
            for j in range(KD):
                if j + 1 < KD:
                    made.append(parts(j + 1))
                hi, f = made[j]
                t = tt(h_lo[:, j, :], val[:, j % 4, :], h_hi[:, j, :].bitcast(F32), sub, hi, f)
                note(f"val{j % 4}", t)
                note(f"h{j}", t)
            self.rest()

        def rest(self):
            pass

    class Modulated(Boundary):

        def __init__(self, l):
            t = ts(col8[:, 0, :], mod[:, l, 8:16], 1.0, None, add, None, "mod", "col8")
            self.cols = tt(col8[:, 0, :], col8[:, 0, :], vc("norm_g", l * 8, 8), mult, t)
            SC.wait(self.cols)
            super().__init__(col8[:, 0, :], mod[:, l, 0:8], by_diag=True)

        def tile(self, t, ready):
            x = stat[:, t, 0:1]
            r = act(val[:, 0:2, :], acc[:, t, :].rearrange("p (a b) -> p a b", a=2), ACT.Square, ready,
                    "val0", "val1", accum_out=x)
            note("val0", r)
            note("val1", r)
            r = act(x, x, ACT.Ln, r, scale=1.0 / D, bias=eps[:, 0:1])
            r = act(x, x, ACT.Exp, r, scale=-0.5)
            self.ready[t] = ts(diag4[:, t, :], ident, x, None, mult, None, r, "transposed")

    def spread_gate(l):
        v = val[:, 0:2, :].rearrange("p a (j n) -> p (a j) n", n=P)
        t = tt(v, ident.unsqueeze(1).broadcast_to((P, KD, P)),
               mod[:, l, 16:24].unsqueeze(2).broadcast_to((P, KD, P)), mult, "mod", "val0", "val1", "val2", "val3")
        for c in range(2):
            PE.wait(t, f"bank{c}")
            tp = do(PE, nc.tensor.matmul(bank[c][:], ones, val[:, c, :], start=True, stop=True))
            note(f"val{c}", tp)
            t_g = act(gate[:, c * T:(c + 1) * T], bank[c][:], ACT.Copy, tp, "gate")
            note(f"bank{c}", t_g)
        note("gate", t_g)

    with ExitStack() as c2:
        NP = 3 * D // 256
        RING = 5
        first_w, first_sum = sb("ada_first", [P, RING, KD * 256], c=c2), sb("first_sum", [P, RING, 256], c=c2)
        w0 = a["ada_w"][0].rearrange("(k p) n -> p k n", p=P)

        def fetch(n):
            SP.wait(f"ada_free{n % RING}")
            note(f"arrived{n}", dma(f"ada_first{n % RING}", first_w[:, n % RING, :].rearrange("p (k n) -> p k n", n=256),
                                    w0[:, :, n * 256:(n + 1) * 256], nc.sync))

        for n in range(RING):
            fetch(n)

        def first_columns(n0, n1, b):
            for n in range(n0, n1):
                x, w = first_sum[:, n % RING, :], first_w[:, n % RING, :]
                VE.wait(f"arrived{n}", f"first_sum{n % RING}")
                t = ts(x, w[:, 0:256], cond[:, 0:1], None, mult, None, t_cond)
                for kk in range(1, KD):
                    t = stt(x, w[:, kk * 256:(kk + 1) * 256], cond[:, kk:kk + 1], x, mult, add, t)
                note(f"ada_free{n % RING}", t)
                if n + RING < NP:
                    fetch(n + RING)
                PE.wait(t, f"bank{b}")
                for c in range(2):
                    ins = nc.tensor.matmul(bank[b][:, 2 * n + c:2 * n + c + 1], x[:, c * P:(c + 1) * P],
                                           ones[:, 0:1], start=True, stop=True)
                t = do(PE, ins, f"first_sum{n % RING}")
            cols = slice(2 * n0, 2 * n1)
            t = tt(mod[:, 0, cols], bank[b][:, cols], vc("ada_b", 2 * n0, 2 * (n1 - n0)), add, t)
            note(f"bank{b}", t)
            note("mod", t)
            return t

        for e in (SC, VE, PE):
            e.wait(t_x)
        first_columns(0, 2 * NP // 3, 7)
        start = Modulated(0)
        for t in range(NT):
            start.tile(t, None)
        start.features()
        first_columns(2 * NP // 3, NP, 0)
        spread_gate(0)
    note("scratch", *k.noted["h7"], *k.noted["gate"])

    ada_raw = sb("ada_raw", [P, AR, 1024], c=ada_buf)
    PO.wait(t_cond)

    def cross_tiles(q0, kend, edge, ex, ST, vw, b0, b1, *waits):
        t1 = ts(ex[:, 0, :], q0[:, 2 * P:3 * P], edge[:, 1:2], None, mult, None, *waits)
        t2 = ts(ex[:, 1, :], q0[:, 3 * P:4 * P], edge[:, 2:3], None, mult, None)
        t3 = ts(ex[:, 2, :], ex[:, 1, :], edge[:, 1:2], None, mult, None, t2)
        PE.wait(t3, f"bank{b0}", f"bank{b1}")
        for n, (b, o, j, rhs) in enumerate(((b0, 0, 0, q0[:, P:2 * P]), (b0, 1, 0, ex[:, 0, :]), (b0, 2, 0, ex[:, 2, :]),
                             (b1, 0, 1, q0[:, 2 * P:3 * P]), (b1, 1, 1, ex[:, 1, :]),
                             (b1, 2, 2, q0[:, 3 * P:4 * P]))):
            t = do(PE, nc.tensor.matmul(bank[b][:, o * P:(o + 1) * P], kend[:, j * P:(j + 1) * P],
                                        rhs, start=True, stop=True))
        note("cross", t)
        u1 = act(ST[:, P:T], bank[b0][:, 0:3 * P], ACT.Copy, t, "pv")
        u2 = act(ST[:, 640 + P:640 + 3 * P], bank[b1][:, 0:2 * P], ACT.Copy)
        u3 = act(ST[:, 1280 + P:1280 + 2 * P], bank[b1][:, 2 * P:3 * P], ACT.Copy)
        note(f"bank{b0}", u1)
        note(f"bank{b1}", u3)
        return u3

    def diag_scores(kk, qq, b, *waits):
        PE.wait(f"bank{b}", *waits)
        for j in range(NT):
            t = nc.tensor.matmul(bank[b][:, j * P:(j + 1) * P], kk[:, j * P:(j + 1) * P],
                                 qq[:, j * P:(j + 1) * P], start=True, stop=True)
        return do(PE, t)

    def keep_diag(ST, mask, b, t):
        diag = ST.rearrange("p (j x) -> p j x", x=640)[:, :, 0:P]
        m = mask.bitcast(I32).unsqueeze(1).broadcast_to((P, NT, P))
        wait_apart(t, "diag")
        u = do(VE, nc.vector.copy_predicated(diag, m, bank[b][:].rearrange("p (j x) -> p j x", x=P)))
        note(f"bank{b}", u)
        note("diag", u)
        return u

    def masked_diag(ST, mask, kk, qq, b, *waits):
        t = diag_scores(kk, qq, b, *waits)
        return t, keep_diag(ST, mask, b, t)

    def head_values(b, v, c, ST, *waits):
        PE.wait(f"bank{b}", *waits)
        for j in range(NT):
            ins = nc.tensor.matmul(bank[b][:, j * P:T], v[:, j, c * P:(c + 1) * P],
                                   ST[:, j * 640:j * 640 + T - j * P], start=j == 0, stop=j == NT - 1)
        return do(PE, ins)

    def tile_view(x, n=P):
        return x.rearrange("p (j n) -> p j n", n=n)

    with ExitStack() as c2:
        enter_scratch()
        s_q, s_key, s_cum = (sb(n, [P, T], c=c2) for n in ("e_q", "e_key", "e_cum"))
        s_v = sb("e_v", [P, NT, P], c=c2)
        s_ga, s_ex = val[:, 1, :], val[:, 0, 0:3 * P].rearrange("p (a n) -> p a n", n=P)
        s_u = sb("e_u", [P, 2, 16 + T], c=c2)
        s_d, s_E = sb("e_d", [P, 2, T], c=c2), sb("e_E", [P, 2, T], c=c2)
        s_qs, s_ks = sb("e_qs", [P, 2, T], c=c2), sb("e_ks", [P, 2, T], c=c2)
        s_q0, s_kend = sb("e_q0", [P, T], c=c2), sb("e_kend", [P, T], c=c2)
        s_gb = s_ks[:, 0, :]
        s_f = s_kend
        s_edge = sb("e_edge", [P, NT], c=c2)
        ST = sb("e_ST", [P, NT * 640], c=c2)
        s_sq, s_rs = s_qs[:, 1, :], s_ks[:, 1, :]
        s_pw = val[:, 0, 3 * P:T]
        do(PO, nc.gpsimd.memset(ST[:], 0.0))
        do(PO, nc.gpsimd.memset(s_qs[:], 0.0))
        do(PO, nc.gpsimd.memset(s_ks[:], 0.0))
        t_z = do(PO, nc.gpsimd.memset(s_u[:], 0.0))
        SC.wait(t_z); VE.wait(t_z)

        def even_body(i, then=None):
            load_columns(0, even_w, (i * P, i * P + 512))
            load_columns(1, even_w, (i * P + 1024, i * P + 1536))
            load_columns(2, even_w, (i * P + 2048, i * P + 2560))
            PO.wait("e_pw")
            t_pw = dma("pool_w", s_pw, a["pool_w"][0][bass.ds(i, 1)].rearrange("g c d -> (g c) d"))
            load_rows(1, a["even_w_out"][0], (i * P, i * P + 512))
            for j in range(AR):
                ada_load(i, j)
            ada_piece(i, 0)
            ada_piece(i, 1)
            W.convert(1)
            W.use(0)
            tq = tf = project_pair(0, 0, 1)
            t = sigmoid_part(s_f[:], bank[1][:], tf, "cross")
            note("bank1", t)
            t = ts(s_f[:], s_f[:], oml[:, bass.ds(i, 1)], lb[:, bass.ds(i, 1)], mult, add, t)
            t_key = ts(s_key[:], s_f[:], -1.0, 1.0, mult, add, t, "e_key")
            t_q = act(s_q[:], bank[0][:], ACT.Copy, tq, "e_q")
            note("bank0", t_q)
            t = act(s_f[:], s_f[:], ACT.Ln, t_key)
            VE.wait(t)
            t_cum = do(VE, nc.vector.tensor_tensor_scan(s_cum[:], const("reset128"), s_f[:], 0.0, mult, add))
            W.convert(2)
            W.use(1)
            (tv,) = project_tokens(1, [2], 0, P, last=False)
            tga = project(1, 1, 3)
            t_v = act(s_v[:].rearrange("p t n -> p (t n)"), bank[2][:], ACT.Copy, tv, "e_v")
            note("bank2", t_v)
            W.convert(1, gate[:])
            cum4 = tile_view(s_cum[:])
            t_E = act(s_E[:, 0, :], s_cum[:], ACT.Exp, t_cum, "e_E0")
            t_q0 = tt(s_q0[:], s_q[:], s_E[:, 0, :], mult, t_E, t_q, "cross")
            t_ed = act(s_edge[:], cum4[:, :, P - 1], ACT.Exp)
            t = tt(tile_view(s_d[:, 0, :]), cum4[:, :, P - 1:P].broadcast_to((P, NT, P)), cum4, sub, "e_d0")
            t = act(s_d[:, 0, :], s_d[:, 0, :], ACT.Exp, t)
            t_kend = tt(s_kend[:], s_key[:], s_d[:, 0, :], mult, t)
            note("e_d0", t_kend)
            note("e_E0", t_kend)
            t_cr = cross_tiles(s_q0, s_kend, s_edge, s_ex, ST[:], s_v, 4, 5, t_kend, t_ed)

            def level_operands(n):
                h, z = LEVELS[n], n % 2
                nb = T // (2 * h)
                q3, k3, c3, d3, E3, qs3, ks3 = (x.rearrange("p (b n) -> p b n", n=2 * h) for x in (
                    s_q[:], s_key[:], s_cum[:], s_d[:, z, :], s_E[:, z, :], s_qs[:, z, :], s_ks[:, z, :]))
                lo_, hi_ = slice(0, h), slice(h, 2 * h)
                t = tt(d3, c3, c3[:, :, h - 1:h].broadcast_to((P, nb, 2 * h)), sub, f"e_d{z}", t_cum, e=PO)
                t1 = act(E3[:, :, hi_], d3[:, :, hi_], ACT.Exp, t, f"e_E{z}")
                t2 = act(E3[:, :, lo_], d3[:, :, lo_], ACT.Exp, scale=-1.0)
                note(f"e_d{z}", t2)
                tt(qs3[:, :, hi_], q3[:, :, hi_], E3[:, :, hi_], mult, t1, t_q, f"e_qs{z}")
                t = tt(ks3[:, :, lo_], k3[:, :, lo_], E3[:, :, lo_], mult, t2)
                note(f"e_E{z}", t)
                return t

            W.use(2)
            steps = project_steps(2, 0, 1)
            ready = level_operands(0)
            td = diag_scores(s_key[:], s_q[:], 6, t_key, t_q)
            next(steps)
            for n in range(len(LEVELS)):
                z = n % 2
                after = level_operands(n + 1) if n + 1 < len(LEVELS) else None
                if n in (1, 3, 4, 5):
                    t_ada = ada_piece(i, {1: 2, 3: 3, 4: 4, 5: 5}[n])
                u = keep_diag(ST[:], ident if n == 0 else const("level", (n - 1) * P, P), 6 + z, td)
                td = diag_scores(s_ks[:, z, :], s_qs[:, z, :], 7 - z, ready)
                note(f"e_qs{z}", td)
                ready = after
                next(steps)
            u = keep_diag(ST[:], const("level", (len(LEVELS) - 1) * P, P), 6 + len(LEVELS) % 2, td)
            tu = tgb = k.noted["project"][0]
            note("e_key", td)
            note("e_q", td)
            t_ga = act(s_ga, bank[3][:], ACT.Silu, tga, "e_ga")
            note("bank3", t_ga)
            t_gb = act(s_gb, bank[1][:], ACT.Silu, tgb, "e_qs0")
            note("bank1", t_gb)
            t = act(s_u[:, 0, 16:16 + T], bank[0][:], ACT.Copy, tu, "e_u")
            t_u = act(s_E[:, 0, :], bank[0][:], ACT.Copy, "e_E0")
            note("bank0", t_u)
            nc.scalar.preload_act_table_set("natural_log_exp_and_others")
            VE.wait(t_u)
            for n in range(4):
                sh = 2 ** n
                src, dst = s_u[:, n % 2, :], s_u[:, (n + 1) % 2, :]
                t = stt(dst[:, 16:16 + T], src[:, 16 - sh:16 - sh + T],
                        const("pool_on")[:, bass.ds(i * 4 + n, 1)], src[:, 16:16 + T], mult, add, t)
            pooled = s_u[:, 0, 16:16 + T]
            t = tt(s_u[:, 0, 16:32], s_u[:, 0, 16:32], const("pool_head")[:, bass.ds(i * 16, 16)], mult, t)
            t = stt(s_qs[:, 0, :], pooled, const("pool_w")[:, bass.ds(i, 1)], s_E[:, 0, :], mult, sub, t)
            note("e_E0", t)
            note("e_u", t)
            PE.wait(t, "bank0", t_pw, t_pw)
            t = do(PE, nc.tensor.matmul(bank[0][:], s_pw, s_qs[:, 0, :], start=True, stop=True))
            note("e_pw", t)
            t = stt(s_gb, bank[0][:], vc("pool_scale", i), s_gb, mult, mult, t, t_gb)
            note("bank0", t)
            r1 = split_oh(1, s_gb, t)
            note("e_qs0", r1)
            tp = head_values(2, s_v[:], 0, ST[:], u, t_v, t_cr)
            note("pv", tp)
            note("e_v", tp)
            t = act(s_sq, bank[2][:], ACT.Square, tp, "e_qs1")
            PE.wait(t, "bank3")
            t = do(PE, nc.tensor.matmul(bank[3][:], ones, s_sq, start=True, stop=True))
            t = act(s_rs, bank[3][:], ACT.Ln, t, scale=1.0 / P, bias=eps[:, 0:1])
            note("bank3", t)
            t = act(s_rs, s_rs, ACT.Exp, t, scale=-0.5)
            t = stt(s_rs, bank[2][:], vc("onorm", i), s_rs, mult, mult, t)
            note("bank2", t)
            t = tt(s_ga, s_ga, s_rs, mult, t, t_ga)
            note("e_qs1", t)
            r0 = split_oh(0, s_ga, t)
            note("e_ga", r0)
            ada_columns(i, 7, t_ada)
            W.convert(0)
            W.use(1)
            out_step(1, (r1, r0), order=(1, 0), then=then and then())

        W.convert(0)
        with k.rounds("even", NH - 1, [0, 1, 2, 1]) as i:
            even_body(i)
        even_body(NH - 1, then=lambda: Modulated(1))
        spread_gate(1)
    note("scratch", *k.noted["h7"], *k.noted["gate"])

    ada_buf.close()

    def narrow(n, b, ctx2, name):
        hi, lo = sb(name + "_hi", [P, KD, P], F32R, ctx2), sb(name + "_lo", [P, KD, P], F32R, ctx2)
        t1 = do(VE, nc.vector.memset(hi[:].bitcast(F32), 0.0))
        t2 = do(VE, nc.vector.memset(lo[:].bitcast(F32), 0.0))
        t3 = act(hi[:, :, 0:16], narrow_raw[:, n, :, :], ACT.Copy, t_narrow, t1, t2)
        t4 = tt(lo[:, :, 0:16], narrow_raw[:, n, :, :], hi[:, :, 0:16].bitcast(F32), sub, t2, t3)
        PE.wait(t4, "h7", f"bank{b}")
        for kk in range(KD):
            ins = three(bank[b][:], hi[:, kk, :], lo[:, kk, :], h_hi[:, kk, :], h_lo[:, kk, :],
                        kk == 0, kk == KD - 1)
        return do(PE, ins)

    def log_sigmoid(out, tmp, xb, *waits):
        t = act(tmp, xb, ACT.Abs, *waits)
        t = act(tmp, tmp, ACT.Exp, t, scale=-1.0)
        t = act(tmp, tmp, ACT.Ln, t, bias=eps[0:tmp.shape[0], 2:3])
        return stt(out, xb, 0.0, tmp, ALU.min, sub, t)

    with ExitStack() as c2:
        enter_scratch()
        cum = sb("o_cum", [FOX_H, T], c=c2)
        with ExitStack() as c3:
            t = narrow(0, 0, c3, "fl")
            xb, tmp, lf = (sb(n, [FOX_H, T], c=c3) for n in ("fl_x", "fl_t", "fl_l"))
            t = act(xb[:], bank[0][0:FOX_H, :], ACT.Identity, t, bias=fb[:, 0:1])
            note("bank0", t)
            t = log_sigmoid(lf[:], tmp[:], xb[:], t)
            VE.wait(t)
            t1 = do(VE, nc.vector.memset(tmp[:], 1.0))
            VE.wait(t1, t)
            t_cum = do(VE, nc.vector.tensor_tensor_scan(cum[:], tmp[:], lf[:], 0.0, mult, add))
            note("scratch", t_cum)
        enter_scratch()
        gq8 = sb("o_gq8", [P, 1], c=c2)
        t_gq = ts(gq8[:], vc("qnorm", 0), DH ** -0.5, None, mult, None)
        o_qn, o_kn = sb("o_qn", [P, 2, T], c=c2), sb("o_kn", [P, 2, T], c=c2)
        o_v, o_g = sb("o_v", [P, NT, 256], c=c2), sb("o_g", [P, NT, 256], c=c2)
        o_S, o_PT = sb("o_S", [P, 3, 2, T], c=c2), sb("o_PT", [P, 2, T], c=c2)
        o_sq, o_rs = o_S[:, 0, :, :], o_PT
        o_row, o_bias = sb("o_row", [FOX_H, 2, T], c=c2), sb("o_bias", [P, 4, T], c=c2)
        o_m, o_l = sb("o_m", [P, 16], c=c2), sb("o_l", [P, 16], c=c2)

        def head_norm(dst, g, src, b, *waits):
            tb = []
            for c in range(2):
                t = act(o_sq[:, c, :], bank[src + c][:], ACT.Square, waits[c], "o_S0")
                PE.wait(t, f"bank{b + c}")
                tb.append(do(PE, nc.tensor.matmul(bank[b + c][:], const("block_ones"), o_sq[:, c, :],
                                                  start=True, stop=True)))
            note("o_S0", *tb)
            for c in range(2):
                t = act(o_rs[:, c, :], bank[b + c][:], ACT.Ln, tb[c], f"o_PT{c}", scale=1.0 / DH, bias=eps[:, 0:1])
                note(f"bank{b + c}", t)
                t = act(o_rs[:, c, :], o_rs[:, c, :], ACT.Exp, t, scale=-0.5)
                t = stt(dst[:, c, :], bank[src + c][:], g, o_rs[:, c, :], mult, mult, t, "o_qk")
                note(f"bank{src + c}", t)
                note(f"o_PT{c}", t)
            return t

        def odd_body(i, then=None):
            for s, col in ((0, 0), (1, 1024), (2, 2048), (0, 3072)):
                load_wide(s, odd_w, i * 256 + col)
            load_rows(1, a["odd_w_out"][0], (i * 256, i * 256 + P))
            W.convert(1)
            W.use(0)
            tq = project_pair(0, 0, 1)
            W.convert(2)
            W.use(1)
            tk = project_pair(1, 2, 3)
            for hh in range(4):
                z = hh % 2
                t = ts(o_row[:, z, :], cum[:], ident[0:FOX_H, bass.ds(i * 4 + hh, 1)], -1.0, mult, mult, f"o_row{z}")
                PE.wait(t, f"bank{4 + z}")
                t = do(PE, nc.tensor.matmul(bank[4 + z][:], ones[0:FOX_H, :], o_row[:, z, :], start=True, stop=True),
                       f"o_row{z}")
                t_bias = act(o_bias[:, hh, :], bank[4 + z][:], ACT.Copy, t, "o_bias")
                note(f"bank{4 + z}", t_bias)
            t_qn = head_norm(o_qn, gq8[:, 0:1], 0, 4, tq, tq)
            W.convert(0)
            W.use(2)
            tv = project_tokens(2, (6, 7))
            t_kn = head_norm(o_kn, vc("knorm", 0), 2, 4, tk, tk)
            for c in range(2):
                t_v = act(o_v[:, 2 * c:2 * c + 2, :].rearrange("p t n -> p (t n)"), bank[6 + c][:], ACT.Copy,
                          tv[c], "o_v")
                note(f"bank{6 + c}", t_v)
            W.convert(1, gate[:])
            W.use(0)
            tg = project_tokens(0, (0, 1))
            for c in range(2):
                t_g = act(o_g[:, 2 * c:2 * c + 2, :].rearrange("p t n -> p (t n)"), bank[c][:], ACT.Silu,
                          tg[c], "o_g")
                note(f"bank{c}", t_g)
            nc.scalar.preload_act_table_set("natural_log_exp_and_others")

            def scores(n):
                t, pair = n // 2, n % 2
                w, z, b = (t + 1) * P, n % 3, 4 + 2 * (n % 2)
                PE.wait(f"bank{b}", f"bank{b + 1}", t_qn, t_kn)
                for e in range(2):
                    rows = slice(e * DH, (e + 1) * DH)
                    x = nc.tensor.matmul(bank[b + e][:, 0:w], o_qn[rows, pair, t * P:w],
                                         o_kn[rows, pair, 0:w], start=True, stop=True)
                x = do(PE, x)
                S = o_S[:, z, :, 0:w]
                y = tt(S, psum[:, b:b + 2, 0:w], o_bias[:, 2 * pair:2 * pair + 2, 0:w], add, x, f"o_S{z}", t_bias)
                note(f"bank{b}", y)
                note(f"bank{b + 1}", y)
                d = o_S[:, z, :, t * P:w]
                y = tt(d, d, const("causal_add").unsqueeze(1).broadcast_to((P, 2, P)), add, y)
                VE.wait(y)
                m = o_m[:, 2 * n:2 * n + 2]
                y = do(VE, nc.vector.tensor_reduce(m, S, AX, ALU.max))
                y = ts(m, m, -1.0, None, mult, None, y)
                for e in range(2):
                    y = act(o_S[:, z, e, 0:w], o_S[:, z, e, 0:w], ACT.Exp, y, bias=m[:, e:e + 1],
                            accum_out=o_l[:, 2 * n + e:2 * n + e + 1])
                return y

            def values(n, e_done):
                t, pair, z = n // 2, n % 2, n % 3
                w, ob = (t + 1) * P, 2 + t // 2
                PE.wait(e_done)
                xs = []
                for e in range(2):
                    PE.wait(f"bank{e}")
                    for j in range(t + 1):
                        x = nc.tensor.transpose(bank[e][:, j * P:(j + 1) * P],
                                                o_S[:, z, e, j * P:(j + 1) * P], ident)
                    xs.append(do(PE, x))
                note(f"o_S{z}", xs[1])
                for e in range(2):
                    xs[e] = act(o_PT[:, e, 0:w], bank[e][:, 0:w], ACT.Copy, xs[e], f"o_PT{e}")
                    note(f"bank{e}", xs[e])
                if pair == 0 and t % 2 == 0:
                    PE.wait(f"bank{ob}")
                for e in range(2):
                    PE.wait(xs[e], t_v)
                    col = (t % 2) * 256 + (2 * pair + e) * DH
                    for j in range(t + 1):
                        x = nc.tensor.matmul(bank[ob][:, col:col + DH], o_PT[:, e, j * P:(j + 1) * P],
                                             o_v[:, j, (2 * pair + e) * DH:(2 * pair + e + 1) * DH],
                                             start=j == 0, stop=j == t)
                    x = do(PE, x, f"o_PT{e}")
                if pair == 1:
                    o3 = bank[ob][:, (t % 2) * 256:(t % 2) * 256 + 256].rearrange("p (h d) -> p h d", d=DH)
                    l4 = o_l[:, t * 4:t * 4 + 4]
                    r = recip(l4, l4, e_done)
                    g3 = o_g[:, t, :].rearrange("p (h d) -> p h d", d=DH)
                    q = tt(g3, g3, l4.unsqueeze(2).broadcast_to((P, 4, DH)), mult, r, t_g)
                    q = tt(g3, o3, g3, mult, x, q)
                    note(f"bank{ob}", q)
                    return q

            ahead, ready = [], []
            for n in range(8 + 1):
                if n < 8:
                    ahead.append(scores(n))
                if n >= 1:
                    ready.append(values(n - 1, ahead[n - 1]))
            note("o_bias", ahead[-1])
            note("o_qk", k.noted["o_PT1"][0])
            note("o_v", k.noted["o_PT1"][0])
            PE.wait("bank4", "bank5", ready[-1])
            for c in range(2):
                for t in range(NT):
                    x = do(PE, nc.tensor.transpose(bank[4 + c][:, t * P:(t + 1) * P],
                                                   o_g[:, t, c * P:(c + 1) * P], ident))
                r = split_oh(c, bank[4 + c][:], x)
                note(f"bank{4 + c}", r)
                if c == 0:
                    r0 = r
            note("o_g", x)
            W.convert(0)
            W.use(1)
            out_step(1, (r0, r), then=then)

        class Plain(Boundary):

            def rest(self):
                PO.wait("transposed")
                note("acc", do(PO, nc.gpsimd.tensor_tensor(
                    acc[:], acc[:], alpha[:, 0:1].unsqueeze(2).broadcast_to((P, NT, D)), mult)))

        with k.rounds("odd", 3, [0, 1, 2, 0, 1]) as i:
            odd_body(i)
        odd_body(3, then=Plain(const("ones"), zero8))
        note("scratch", *k.noted["h7"])
    first.close()

    lng, lnb = sb("lng", [P, D]), sb("lnb", [P, D])

    class LayerNorm(Boundary):

        def __init__(self, l, m, final=False):
            at = (l * 3 + m) * KD
            self.final, self.out = final, []
            PO.wait("ln_vec")
            dma("ln_vec", lng[:], a["ln_g_2"][l, m].partition_broadcast(P))
            self.vec = dma("ln_vec", lnb[:], a["ln_b_2"][l, m].partition_broadcast(P))
            super().__init__(vcol[:, 1, at:at + 8], vcol[:, 1, 48 + at:56 + at])

        def begin(self):
            if not self.final:
                act(lng[:], lng[:], ACT.Copy, self.vec, scale=ALPHA)
                self.vec = act(lnb[:], lnb[:], ACT.Copy, scale=ALPHA)
            return self

        def tile(self, t, ready):
            s = stat[:, t, :]
            VE.wait(ready)
            for n in range(2):
                r = do(VE, nc.vector.bn_stats(s[:, 6 * n:6 * n + 6], acc[:, t, n * T:(n + 1) * T]))
            VE.wait(r)
            r = do(VE, nc.vector.bn_aggr(s[:, 12:14], s[:, 0:12]))
            mean, rstd, shift = s[:, 12:13], s[:, 14:15], s[:, 15:16]
            r = act(rstd, s[:, 13:14], ACT.Ln, r, bias=eps[:, 1:2])
            r = act(rstd, rstd, ACT.Exp, r, scale=-0.5)
            if not self.final:
                r = stt(shift, mean, -1.0, rstd, mult, mult, r)
                self.ready[t] = act(acc[:, t, :], acc[:, t, :], ACT.Identity, r, scale=rstd, bias=shift)
                return
            r = stt(acc[:, t, :], acc[:, t, :], mean, lng[:], sub, mult, r, self.vec)
            r = stt(acc[:, t, :], acc[:, t, :], rstd, lnb[:], mult, add, r)
            SP.wait(r)
            self.out.append(dma("out", a["out"].rearrange("b (t p) d -> t p (b d)", p=P)[t], acc[:, t, :], nc.sync))

        def features(self):
            if self.final:
                SP.wait(self.out[-1])
            else:
                super().features()

        def rest(self):
            for t in range(NT):
                g = tt(acc[:, t, :], acc[:, t, :], lng[:], mult, "transposed", self.vec, e=PO)
                g = tt(acc[:, t, :], acc[:, t, :], lnb[:], add, g, e=PO)
            note("acc", g)
            note("ln_vec", g)

    def ffn(l, w):
        with ExitStack() as c2:
            enter_scratch()
            f_s, f_h = sb(f"f_s{l}{w}", [P, 2, T], c=c2), sb(f"f_h{l}{w}", [P, 2, T], c=c2)
            ffn_rounds(f_s, f_h, l, w)
            note("scratch", *k.noted["h7"])

    def ffn_rounds(f_s, f_h, l, w):
        w_in, w_out = a["ffn_w_in_2"][l, w], a["ffn_w_out_2"][l, w]

        def hidden(s):
            tg = tu = project_pair(s, 2 * s, 2 * s + 1)
            t = act(f_s[:, s, :], bank[2 * s][:], ACT.Silu, tg, f"f_h{s}")
            note(f"bank{2 * s}", t)
            t = tt(f_h[:, s, :], f_s[:, s, :], bank[2 * s + 1][:], mult, t, tu)
            note(f"bank{2 * s + 1}", t)
            r = split_oh(s, f_h[:, s, :], t)
            note(f"f_h{s}", r)
            return r

        def body(i, more=True, then=None):
            load_columns(0, w_in, (i * 256, i * 256 + DFF))
            load_columns(1, w_in, (i * 256 + P, i * 256 + P + DFF))
            load_rows(2, w_out, (i * 256, i * 256 + P))
            W.convert(1)
            W.convert(2)
            W.use(0)
            r0 = hidden(0)
            if more:
                W.convert(0)
            W.use(1)
            r1 = hidden(1)
            W.use(2)
            out_step(2, (r0, r1), scale=0.5, then=then)

        n = DFF // 256
        final = (l, w) == (1, 1)
        nc.scalar.preload_act_table(ACT.Silu)
        then = LayerNorm(l, 2 * w, final)
        with k.rounds(f"ffn{l}{w}", n - 1, [0, 1, 2]) as i:
            body(i)
        body(n - 1, more=not final, then=then.begin())

    def gla():
        m = a["gla_w_in_2"][0]
        with ExitStack() as c2:
            enter_scratch()
            low = sb("g_low", [16, T], c=c2)
            with ExitStack() as c3:
                t = narrow(1, 0, c3, "gl")
                t_low = act(low[:], bank[0][0:16, :], ACT.Copy, t)
                note("bank0", t_low)
                note("scratch", t_low)
            enter_scratch()
            g_wg = sb("g_wg", [16, P], c=c2)
            g_q, g_k, g_x, g_l, g_c64, g_c128 = (sb("g_" + n, [P, T], c=c2)
                                                for n in ("q", "k", "x", "l", "c64", "c128"))
            g_v, g_r = sb("g_v", [P, NT, 256], c=c2), val[:, 1:3, :]
            g_E, g_d = sb("g_E", [P, 3, T], c=c2), sb("g_d", [P, 2, T], c=c2)
            g_qd, g_kinv, g_k64, g_q0, g_kend = (sb("g_" + n, [P, T], c=c2)
                                                for n in ("qd", "kinv", "k64", "q0", "kend"))
            g_ex, g_edge = val[:, 0, 0:3 * P].rearrange("p (a n) -> p a n", n=P), sb("g_edge", [P, NT], c=c2)
            ST = sb("g_ST", [P, NT * 640], c=c2)
            g_sq, g_rs = g_d, g_x
            t_z = do(PO, nc.gpsimd.memset(ST[:], 0.0))
            SC.wait(t_z); VE.wait(t_z)
            nc.scalar.preload_act_table_set("natural_log_exp_and_others")

            def body(i, then=None):
                load_columns(0, m, (i * P, i * P + 512))
                load_wide(1, m, i * 256 + 1024)
                load_wide(2, m, i * 256 + 2048)
                load_rows(1, a["gla_w_out_2"][0], (i * 256, i * 256 + P))
                PO.wait("g_wg")
                t_wg = dma("w_gate", g_wg[:], a["gla_w_gate_2"][0][:, bass.ds(i * P, P)])
                W.convert(1)
                W.use(0)
                tq = tk = project_pair(0, 0, 1)
                PE.wait(t_low, t_wg, "bank2")
                t = do(PE, nc.tensor.matmul(bank[2][:], g_wg[:], low[:], start=True, stop=True), "g_wg")
                t = act(g_x[:], bank[2][:], ACT.Identity, t, "g_x", bias=vc("b_gate", i))
                note("bank2", t)
                t = log_sigmoid(g_l[:], g_E[:, 0, :], g_x[:], t, "g_E")
                note("g_x", t)
                VE.wait(t, "g_c")
                do(VE, nc.vector.tensor_tensor_scan(g_c64[:], const("reset64"), g_l[:], 0.0, mult, add))
                t_c = do(VE, nc.vector.tensor_tensor_scan(g_c128[:], const("reset128"), g_l[:], 0.0, mult, add))
                t_q = act(g_q[:], bank[0][:], ACT.Copy, tq, "g_q", scale=P ** -0.5)
                note("bank0", t_q)
                t_k = act(g_k[:], bank[1][:], ACT.Copy, tk, "g_k")
                note("bank1", t_k)
                W.convert(2)
                W.use(1)
                tv = project_tokens(1, (4, 5))
                s16 = 1.0 / 16.0
                te = act(g_E[:, 0, :], g_c64[:], ACT.Exp, t_c, scale=s16)
                t_qd = tt(g_qd[:], g_q[:], g_E[:, 0, :], mult, te, t_q, "g_diag")
                te = act(g_E[:, 1, :], g_c64[:], ACT.Exp, scale=-s16)
                t_ki = tt(g_kinv[:], g_k[:], g_E[:, 1, :], mult, te, t_k)
                te = act(g_E[:, 2, :], g_c128[:], ACT.Exp, scale=s16)
                t_q0 = tt(g_q0[:], g_q[:], g_E[:, 2, :], mult, te, "cross")
                c8, c4 = tile_view(g_c64[:], 64), tile_view(g_c128[:])
                t = tt(tile_view(g_d[:, 0, :], 64), c8[:, :, 63:64].broadcast_to((P, 8, 64)), c8, sub, "g_sq")
                t = act(g_d[:, 0, :], g_d[:, 0, :], ACT.Exp, t, scale=s16)
                t_k64 = tt(g_k64[:], g_k[:], g_d[:, 0, :], mult, t)
                t = tt(tile_view(g_d[:, 1, :]), c4[:, :, P - 1:P].broadcast_to((P, NT, P)), c4, sub)
                t = act(g_d[:, 1, :], g_d[:, 1, :], ACT.Exp, t, scale=s16)
                t_ed = act(g_edge[:], c4[:, :, P - 1], ACT.Exp, scale=s16)
                note("g_c", t_ed)
                t_kend = tt(g_kend[:], g_k[:], g_d[:, 1, :], mult, t)
                note("g_E", t_kend)
                note("g_q", t_kend)
                note("g_k", t_kend)
                for c in range(2):
                    t_v = act(g_v[:, 2 * c:2 * c + 2, :].rearrange("p t n -> p (t n)"), bank[4 + c][:],
                              ACT.Copy, tv[c], "pv")
                    note(f"bank{4 + c}", t_v)
                W.convert(1)
                W.use(2)
                tr = project_pair(2, 2, 3)
                cross_tiles(g_q0, g_kend, g_edge, g_ex, ST[:], g_v, 4, 5, t_kend, t_ed)
                masked_diag(ST[:], const("chunk_causal"), g_kinv[:], g_qd[:], 6, t_ki)
                tp, u = masked_diag(ST[:], const("level", 6 * P, P), g_k64[:], g_qd[:], 7, t_k64)
                note("g_diag", tp)
                for c in range(2):
                    t_r = act(g_r[:, c, :], bank[2 + c][:], ACT.Silu, tr, "g_r")
                    note(f"bank{2 + c}", t_r)
                nc.scalar.preload_act_table_set("natural_log_exp_and_others")
                tsq = []
                PE.wait(t_v, *k.noted["bank5"], *k.noted["bank4"])
                for c in range(2):
                    tp = head_values(6 + c, g_v[:], c, ST[:], u)
                    tsq.append(act(g_sq[:, c, :], bank[6 + c][:], ACT.Square, tp, "g_E", "g_sq"))
                note("pv", tp)
                PE.wait("bank0")
                for c in range(2):
                    PE.wait(tsq[c])
                    ins = nc.tensor.matmul(bank[0][:], ones, g_sq[:, c, :], start=c == 0, stop=c == 1)
                t = do(PE, ins, "g_sq")
                t = act(g_rs[:], bank[0][:], ACT.Ln, t, scale=1.0 / 256, bias=eps[:, 0:1])
                note("bank0", t)
                t = act(g_rs[:], g_rs[:], ACT.Exp, t, scale=-0.5)
                r = []
                for c in range(2):
                    u = stt(g_sq[:, c, :], bank[6 + c][:], vc("gla_g", c), g_rs[:], mult, mult, t, "g_sq")
                    note(f"bank{6 + c}", u)
                    u = tt(g_r[:, c, :], g_r[:, c, :], g_sq[:, c, :], mult, u, t_r)
                    r.append(split_oh(c, g_r[:, c, :], u))
                note("g_x", u)
                note("g_sq", u)
                note("g_r", r[1])
                W.convert(0)
                W.use(1)
                out_step(1, r, then=then)

            then = LayerNorm(0, 1)
            with k.rounds("gla", NH - 1, [0, 1, 2, 1]) as i:
                body(i)
            body(NH - 1, then=then.begin())
            note("scratch", *k.noted["h7"])

    def retention():
        m = a["ret_w_in_2"][0]
        with ExitStack() as c2:
            enter_scratch()
            cos, dec = sb("r_cos", [P, T], c=c2), sb("r_dec", [P, NH, T], c=c2)
            sin, ng = val[:, 3, :], val[:, 2, :]
            dma("rope", cos[:], a["rope"][:, 0, :])
            t1 = dma("rope", sin, a["rope"][:, 1, :])
            t2 = dma("decay", dec[:], a["ret_decay"])
            t3 = dma("ret_g", ng, a["ret_norm_g_2"][0].partition_broadcast(P))
            VE.wait(t1, t2, t3)
            qr, kr = sb("r_q", [P, 2, T], c=c2), sb("r_k", [P, 2, T], c=c2)
            r_t = val
            r_v, r_g = sb("r_v", [P, NT, T], c=c2), sb("r_g", [P, NT, T], c=c2)
            ST = sb("r_ST", [P, NT, T], c=c2)
            o2_hi, o2_lo = sb("o2_hi", [P, 2, T], F32R, c2), sb("o2_lo", [P, 2, T], F32R, c2)
            nc.scalar.preload_act_table_set("natural_log_exp_and_others")

            def rotate(dst, b, tks, *waits):
                x1, x2 = bank[b][:], bank[b + 1][:]
                t = tt(dst[:, 0, :], x1, cos[:], mult, *tks, *waits)
                u = tt(r_t[:, 0, :], x2, sin, mult)
                t = tt(dst[:, 0, :], dst[:, 0, :], r_t[:, 0, :], sub, u)
                t = tt(dst[:, 1, :], x1, sin, mult)
                note(f"bank{b}", t)
                u = tt(r_t[:, 1, :], x2, cos[:], mult)
                note(f"bank{b + 1}", u)
                return tt(dst[:, 1, :], dst[:, 1, :], r_t[:, 1, :], add, u)

            def body(i, then=None):
                for s, col in ((0, i * 256), (1, i * 256 + 1024), (2, i * 512 + 2048), (0, i * 512 + 2304),
                               (1, i * 512 + 4096), (2, i * 512 + 4352)):
                    load_wide(s, m, col)
                for s in range(2):
                    load_rows(s, a["ret_w_out_2"][0], (i * 512 + s * 256, i * 512 + s * 256 + P))
                W.convert(1)
                W.use(0)
                tq = [project_pair(0, 0, 1)]
                t_q = rotate(qr, 0, tq, "r_qk")
                W.convert(2)
                W.use(1)
                tk = [project_pair(1, 2, 3)]
                t_k = rotate(kr, 2, tk)
                for half in range(2):
                    W.convert(half)
                    W.use((2, 0)[half])
                    tv = project_tokens((2, 0)[half], (4 + 2 * half, 5 + 2 * half))
                    for c in range(2):
                        b = 4 + 2 * half + c
                        t_v = act(r_v[:, 2 * c:2 * c + 2, half * 256:half * 256 + 256],
                                  bank[b][:].rearrange("p (t n) -> p t n", n=256), ACT.Copy, tv[c], "pv")
                        note(f"bank{b}", t_v)
                for half in range(2):
                    W.convert((2, 0)[half])
                    W.use((1, 2)[half])
                    tg = project_tokens((1, 2)[half], (0 + 2 * half, 1 + 2 * half))
                    for c in range(2):
                        b = 2 * half + c
                        g = r_g[:, 2 * c:2 * c + 2, half * 256:half * 256 + 256]
                        x = bank[b][:].rearrange("p (t n) -> p t n", n=256)
                        t_g = act(g, x, ACT.Silu, tg[c], "r_g")
                        note(f"bank{b}", t_g)
                nc.scalar.preload_act_table_set("natural_log_exp_and_others")
                for j in range(NT):
                    PE.wait(f"bank{4 + j}", t_q, t_k)
                    w = T - j * P
                    for c in range(2):
                        ins = nc.tensor.matmul(bank[4 + j][:, 0:w], kr[:, c, j * P:(j + 1) * P],
                                               qr[:, c, j * P:T], start=c == 0, stop=c == 1)
                    t = do(PE, ins)
                    t_S = tt(ST[:, j, 0:w], bank[4 + j][:, 0:w],
                             dec[:, bass.ds(i, 1), 0:w].rearrange("p a w -> p (a w)"), mult, t, "pv")
                    note(f"bank{4 + j}", t_S)
                note("r_qk", t)
                PE.wait(t_S, t_v)
                for q in range(NT):
                    PE.wait(f"bank{q}")
                    for j in range(q + 1):
                        ins = nc.tensor.matmul(bank[q][:], ST[:, j, (q - j) * P:(q - j + 1) * P], r_v[:, j, :],
                                               start=j == 0, stop=j == q)
                    tp = do(PE, ins)
                    VE.wait(tp)
                    t = do(VE, nc.vector.bn_stats(stat[:, q, 0:6], bank[q][:]))
                    wait_apart(t)
                    t = do(VE, nc.vector.bn_aggr(stat[:, q, 12:14], stat[:, q, 0:6]))
                    t = act(stat[:, q, 14:15], stat[:, q, 13:14], ACT.Ln, t, bias=eps[:, 0:1])
                    t = act(stat[:, q, 14:15], stat[:, q, 14:15], ACT.Exp, t, scale=-0.5)
                    t = ts(r_t[:, q % 2, :], bank[q][:], stat[:, q, 12:13], stat[:, q, 14:15], sub, mult, t)
                    note(f"bank{q}", t)
                    t = tt(r_t[:, q % 2, :], r_t[:, q % 2, :], ng, mult, t)
                    t = tt(r_g[:, q, :], r_g[:, q, :], r_t[:, q % 2, :], mult, t, t_g)
                note("pv", tp)
                PE.wait(t)
                r = []
                for c in range(4):
                    PE.wait(f"bank{4 + c}")
                    for q in range(NT):
                        x = do(PE, nc.tensor.transpose(bank[4 + c][:, q * P:(q + 1) * P],
                                                       r_g[:, q, c * P:(c + 1) * P], ident))
                    own = {} if c < 2 else {"hi": o2_hi, "lo": o2_lo, "free": "o2"}
                    r.append(split_oh(c % 2, bank[4 + c][:], x, **own))
                    note(f"bank{4 + c}", r[-1])
                note("r_g", x)
                W.convert(1)
                W.use(0)
                out_step(0, r[0:2])
                W.convert(0)
                W.use(1)
                out_step(1, r[2:4], hi=o2_hi, lo=o2_lo, free="o2", then=then)

            then = LayerNorm(1, 1)
            with k.rounds("ret", NH - 1, [0, 1, 2, 0, 1, 2, 0, 1]) as i:
                body(i)
            body(NH - 1, then=then.begin())
            note("scratch", *k.noted["h7"])

    ffn(0, 0)
    gla()
    ffn(0, 1)
    ffn(1, 0)
    retention()
    ffn(1, 1)


_INS = ["x", "c", "norm_g", "ada_w", "ada_b", "hgrn_lb", "even_w_in", "hgrn_onorm_g", "pool_w", "pool_scale",
        "even_w_out", "odd_w_in", "fox_b_f", "fox_qnorm_g", "fox_knorm_g", "odd_w_out", "ffn_w_in_2",
        "ffn_w_out_2", "ln_g_2", "ln_b_2", "gla_w_in_2", "gla_w_gate_2", "gla_b_gate_2", "gla_norm_g_2",
        "gla_w_out_2", "ret_w_in_2", "ret_norm_g_2", "ret_w_out_2"]


def kernel(**inputs):
    import numpy as _np
    import concourse.bacc as _bacc
    from concourse import mybir as _mybir
    from concourse.bass_utils import run_bass_kernel_spmd as _run

    arrays = {n: _np.ascontiguousarray(inputs[n]) for n in _INS}
    arrays.update(constant_tables())
    counts = {}
    for _ in range(2):
        nc = _bacc.Bacc("TRN2", target_bir_lowering=False, num_devices=1)
        dt = _mybir.dt.float32
        a = {n: nc.dram_tensor(f"in_{n}", v.shape, dt, kind="ExternalInput").ap() for n, v in arrays.items()}
        a["out"] = nc.dram_tensor("out", (1, T, D), dt, kind="ExternalOutput").ap()
        counts = build(nc, a, counts)
    r = _run(nc, [{f"in_{n}": v for n, v in arrays.items()}], core_ids=[0])
    return r.results[0]["out"]
```

```python
from collections import defaultdict
from contextlib import ExitStack, contextmanager

import numpy as np
import concourse.bass as bass
from concourse import mybir

F32 = mybir.dt.float32
F32R = mybir.dt.float32r
I32 = mybir.dt.int32
ALU = mybir.AluOpType
ACT = mybir.ActivationFunctionType
AX = mybir.AxisListType.X

P = 128
T = 512
NT = T // P
D = 1024
KD = D // P
PIECE = 2048
SLOTS = 3
DFF = 2816
NH = 4
FOX_H = 16
DH = 64
EPS = 1e-6
LN_EPS = 1e-5
ALPHA = 4.0 ** 0.25
NEG = -1e30
CREDIT = 512
LEVELS = (1, 2, 4, 8, 16, 32, 64)


def _columns():
    at, out = 0, {}
    for name, n in (("ident", P), ("ones", P), ("block_ones", P), ("level", P * len(LEVELS)),
                    ("chunk_causal", P), ("causal_add", P), ("reset128", T), ("reset64", T),
                    ("pool_on", 16), ("pool_w", 4), ("pool_head", 64)):
        out[name] = (at, n)
        at += n
    return out, at


COLS, NCOLS = _columns()


def constant_tables():
    c = np.zeros((P, NCOLS), np.float32)

    def put(name, a):
        c[:, COLS[name][0]:COLS[name][0] + COLS[name][1]] = a

    i = np.arange(P)
    put("ident", np.eye(P))
    put("ones", 1.0)
    put("block_ones", (i[:, None] // DH) == (i[None, :] // DH))
    s, t = i[:, None], i[None, :]
    put("level", np.concatenate([((s // (2 * h)) == (t // (2 * h))) & (s % (2 * h) < h) & (t % (2 * h) >= h)
                                 for h in LEVELS], axis=1))
    put("chunk_causal", (s // 64 == t // 64) & (t >= s))
    put("causal_add", np.where(t > s, NEG, 0.0))
    tok = np.arange(T)
    put("reset128", (tok % 128 != 0)[None, :])
    put("reset64", (tok % 64 != 0)[None, :])
    wins = (2, 4, 8, 16)
    put("pool_on", np.array([[w >= 2 ** (k + 1) for k in range(4)] for w in wins]).reshape(1, 16))
    put("pool_w", np.array([[1.0 / w for w in wins]]))
    put("pool_head", np.array([[w / min(n + 1, w) for n in range(16)] for w in wins]).reshape(1, 64))
    dh = D // 4
    inv = (10000.0 ** (-np.arange(0, dh, 2, dtype=np.float32) / np.float32(dh))).astype(np.float32)
    ang = inv[:, None] * np.arange(T, dtype=np.float32)[None, :]
    rope = np.stack([np.cos(ang), np.sin(ang)], axis=1).astype(np.float32)
    lg = np.log(1.0 - 2.0 ** (-5.0 - np.arange(NH)))
    lag = tok[None, None, :] - i[:, None, None]
    decay = np.where(lag >= 0, np.exp(np.maximum(lag, 0) * lg[None, :, None]), 0.0) * dh ** -0.5
    return {"consts": c, "rope": rope,
            "ret_decay": decay.astype(np.float32)}


class Token:

    def __init__(self, prog, value, loop):
        self.prog, self.value, self.loop = prog, value, loop


class Progress:

    def __init__(self, k, name, eng, inc=1, credit=0):
        self.k, self.name, self.eng, self.inc = k, name, eng, inc
        self.sem = k.sem("s_" + name)
        self.n = credit
        self.seen = {}
        k.progs.append(self)

    def wait(self, *tokens):
        for t in tokens:
            if isinstance(t, str):
                self.k.wait_noted(self, t)
            elif isinstance(t, (list, tuple)):
                self.wait(*t)
            elif t is not None:
                self.k.wait_token(self, t)


class Kernel:
    def __init__(self, nc, ctx, counts):
        self.nc, self.ctx, self.counts = nc, ctx, counts
        self.loop, self.progs, self.noted, self.found = None, [], {}, {}

    def sem(self, name):
        return self.ctx.enter_context(self.nc.semaphore(name))

    def wait_token(self, me, t):
        L = self.loop
        if L is not None and t.loop is L:
            key = (t.prog.name, L.name)
            if me.seen.get(key, -1) < t.value:
                me.seen[key] = t.value
                me.eng.wait_ge(t.prog.sem, L.i * L.per(t.prog) + t.value if L.per(t.prog) else t.value)
            return
        value = t.value if t.loop is None else t.value + (t.loop.n - 1) * t.loop.per(t.prog)
        key = t.prog.name if L is None else (t.prog.name, L.name, "before")
        if max(me.seen.get(t.prog.name, -1), me.seen.get(key, -1)) < value:
            me.seen[key] = value
            me.eng.wait_ge(t.prog.sem, value)

    def wait_noted(self, me, name):
        L, got = self.loop, self.noted.get(name, [])
        if L is None or (got and got[0].loop is L):
            for t in got:
                self.wait_token(me, t)
            return
        for t in got:
            self.wait_token(me, t)
        for prog, off in L.last.get(name, []):
            p = self.prog(prog)
            if (me.seen.get((prog, L.name), -1)) >= 0:
                continue
            key = (prog, L.name, "last")
            if me.seen.get(key, -1) < off:
                me.seen[key] = off
                value = L.start[prog] + off - L.per(p)
                assert value > 0 or L.dry, (name, prog, value)
                me.eng.wait_ge(p.sem, L.i * L.per(p) + max(value, 1))

    def prog(self, name):
        return next(p for p in self.progs if p.name == name)

    @contextmanager
    def rounds(self, name, n, pieces):
        L = Loop(self, name, n, pieces)
        with self.nc.Fori(0, n) as i:
            L.i = i
            self.loop = L
            yield i
            self.loop = None
        L.end()
        self.weights.end_loop(n, pieces)


class Loop:
    def __init__(self, k, name, n, pieces):
        self.k, self.name, self.n, self.pieces = k, name, n, pieces
        known = k.counts.get(name)
        self.dry = known is None
        self.pers = {} if self.dry else known["per"]
        self.last = {} if self.dry else known["last"]
        self.start = defaultdict(int, {p.name: p.n for p in k.progs})

    def per(self, prog):
        return self.pers.get(prog.name, 0)

    def end(self):
        per = {p.name: p.n - self.start[p.name] for p in self.k.progs}
        last = {a: [(t.prog.name, t.value - self.start[t.prog.name]) for t in b]
                for a, b in self.k.noted.items() if b and b[0].loop is self}
        if not self.dry:
            assert per == self.pers and last == self.last, self.name
        self.k.found[self.name] = {"per": per, "last": last}
        self.pers = per
        for p in self.k.progs:
            p.n = self.start[p.name] + self.n * per[p.name]


class Weights:

    def __init__(self, k, raw, hi, lo):
        self.k, self.raw, self.hi, self.lo = k, raw, hi, lo
        self.loaded = [k.sem(f"s_loaded{s}") for s in range(SLOTS)]
        self.rounded = [k.sem(f"s_rounded{s}") for s in range(SLOTS)]
        self.split = [k.sem(f"s_split{s}") for s in range(SLOTS)]
        for s in range(SLOTS):
            k.nc.vector.sem_inc(self.split[s], 1)
        self.n = {what: [0] * SLOTS for what in ("load", "convert", "use")}

    def number(self, what, s, k=1, plus=0):
        L, n = self.k.loop, self.n[what][s]
        if L is None:
            return n * k + plus
        return L.i * (L.pieces.count(s) * k) + (n * k + plus)

    def end_loop(self, n, pieces):
        for what in self.n:
            for s in range(SLOTS):
                self.n[what][s] += (n - 1) * pieces.count(s)

    def load(self, s, halves):
        self.n["load"][s] += 1
        sp = self.k.nc.sync
        sp.wait_ge(self.split[s], self.number("load", s))
        for dst, src in halves:
            sp.dma_start(dst, src).then_inc(self.loaded[s], 16)

    def convert(self, s, gate=None):
        self.n["convert"][s] += 1
        k, nc = self.k, self.k.nc
        if gate is None:
            nc.scalar.wait_ge(self.loaded[s], self.number("convert", s, k=32))
        else:
            nc.gpsimd.wait_ge(self.loaded[s], self.number("convert", s, k=32))
            po = k.prog("pool")
            po.wait("gate")
            raw = self.raw[:, s, :].rearrange("p (c n) -> p c n", n=D)
            ins = nc.gpsimd.tensor_tensor(raw, raw, gate.unsqueeze(1).broadcast_to((P, 2, D)), ALU.mult)
            ins.then_inc(po.sem, 1)
            po.n += 1
            k.prog("act").wait(Token(po, po.n, k.loop))
        k.prog("act").wait(f"used{s}")
        nc.scalar.activation(self.hi[:, s, :], self.raw[:, s, :], ACT.Copy).then_inc(self.rounded[s], 1)
        nc.vector.wait_ge(self.rounded[s], self.number("convert", s))
        nc.vector.tensor_tensor(self.lo[:, s, :], self.raw[:, s, :], self.hi[:, s, :].bitcast(F32),
                                ALU.subtract).then_inc(self.split[s], 1)

    def use(self, s):
        self.n["use"][s] += 1
        self.k.nc.tensor.wait_ge(self.split[s], self.number("use", s, plus=1))


def build(nc, a, counts):
    with ExitStack() as ctx:
        k = Kernel(nc, ctx, counts)
        emit(nc, ctx, k, a)
        return k.found


def emit(nc, ctx, k, a):
    def sb(name, shape, dt=F32, c=ctx):
        return c.enter_context(nc.sbuf_tensor(name, shape, dt))

    psum = ctx.enter_context(nc.psum_tensor("psum", [P, 8, T], F32))
    bank = [psum[:, b, :] for b in range(8)]
    acc = sb("acc", [P, NT, D])
    h_hi, h_lo = sb("h_hi", [P, KD, T], F32R), sb("h_lo", [P, KD, T], F32R)
    w_raw = sb("w_raw", [P, SLOTS, PIECE])
    w_hi, w_lo = sb("w_hi", [P, SLOTS, PIECE], F32R), sb("w_lo", [P, SLOTS, PIECE], F32R)
    oh_hi, oh_lo = sb("oh_hi", [P, 2, T], F32R), sb("oh_lo", [P, 2, T], F32R)
    consts = sb("consts", [P, NCOLS])
    vcol = sb("vcol", [P, 2, P])
    eps = sb("eps", [P, 3])
    alpha = sb("alpha", [P, 1])
    zero8, spare = sb("zero8", [P, KD]), sb("spare", [P, 1])
    col8 = sb("col8", [P, 2, KD])
    val = sb("val", [P, 4, T])
    stat = sb("stat", [P, NT, 24])

    def const(name, lo=0, n=None):
        at, size = COLS[name]
        return consts[:, at + lo:at + lo + (size - lo if n is None else n)]

    ident, ones = const("ident"), const("ones")

    PE = Progress(k, "pe", nc.tensor, credit=CREDIT)
    SC = Progress(k, "act", nc.scalar, credit=CREDIT)
    VE = Progress(k, "dve", nc.vector, credit=CREDIT)
    PO = Progress(k, "pool", nc.gpsimd, credit=CREDIT)
    SP = Progress(k, "sp", nc.sync)
    for e in (PE, SC, VE, PO):
        e.eng.sem_inc(e.sem, CREDIT)
    W = k.weights = Weights(k, w_raw, w_hi, w_lo)

    def do(e, ins, note=None):
        ins.then_inc(e.sem, e.inc)
        e.n += e.inc
        t = Token(e, e.n, k.loop)
        if note:
            k.noted[note] = [t]
        return t

    def note(name, *tokens):
        k.noted[name] = [t for t in tokens if t is not None]

    queues = {}

    def dma(name, out, in_, eng=None):
        if name not in queues:
            queues[name] = Progress(k, "dma_" + name, eng or nc.gpsimd, inc=16)
        q = queues[name]
        return do(q, q.eng.dma_start(out, in_))

    def act(out, in_, func, *waits, **kw):
        SC.wait(*waits)
        return do(SC, nc.scalar.activation(out, in_, func, **kw))

    def tt(out, x, y, op, *waits, e=VE):
        e.wait(*waits)
        return do(e, e.eng.tensor_tensor(out, x, y, op))

    def ts(out, x, s1, s2, op0, op1, *waits, e=VE):
        e.wait(*waits)
        if s2 is None:
            return do(e, e.eng.tensor_scalar(out, x, s1, None, op0))
        return do(e, e.eng.tensor_scalar(out, x, s1, s2, op0, op1))

    def stt(out, x, s, y, op0, op1, *waits):
        VE.wait(*waits)
        return do(VE, nc.vector.scalar_tensor_tensor(out, x, s, y, op0, op1))

    def recip(out, x, *waits):
        VE.wait(*waits)
        return do(VE, nc.vector.reciprocal(out, x))

    def enter_scratch():
        for e in (SC, VE, PO):
            e.wait("scratch")

    def wait_apart(*tokens):
        VE.wait(*tokens, "spare")
        do(VE, nc.vector.memset(spare[:], 0.0), "spare")

    mult, add, sub = ALU.mult, ALU.add, ALU.subtract

    def three(out, ws, wl, xs, xl, first, last):
        nc.tensor.matmul(out, ws, xs, start=first, stop=False)
        nc.tensor.matmul(out, ws, xl, start=False, stop=False)
        return nc.tensor.matmul(out, wl, xs, start=False, stop=last)

    def project(s, c, b, last=True):
        PE.wait(f"bank{b}", "h7")
        for kk in range(KD):
            w = slice(kk * 256 + c * P, kk * 256 + (c + 1) * P)
            ins = three(bank[b][:], w_hi[:, s, w], w_lo[:, s, w], h_hi[:, kk, :], h_lo[:, kk, :],
                        kk == 0, kk == KD - 1)
        if last:
            return do(PE, ins, f"used{s}")
        return do(PE, ins)

    def project_steps(s, b0, b1):
        PE.wait(f"bank{b0}", f"bank{b1}")
        for kk in range(KD):
            PE.wait(f"h{kk}")
            for c, b in enumerate((b0, b1)):
                w = slice(kk * 256 + c * P, kk * 256 + (c + 1) * P)
                ins = three(bank[b][:], w_hi[:, s, w], w_lo[:, s, w], h_hi[:, kk, :], h_lo[:, kk, :],
                            kk == 0, kk == KD - 1)
            if kk < KD - 1:
                yield
        done = do(PE, ins, f"used{s}")
        k.noted["project"] = [done]
        yield

    def project_pair(s, b0, b1):
        for _ in project_steps(s, b0, b1):
            pass
        return k.noted["project"][0]

    def project_tokens(s, banks, c0=0, n=256, last=True):
        per = T // n
        done = []
        for t in range(NT):
            b = banks[t // per]
            if t % per == 0:
                PE.wait(f"bank{b}", "h7")
            o = bank[b][:, (t % per) * n:(t % per + 1) * n]
            for kk in range(KD):
                w = slice(kk * 256 + c0, kk * 256 + c0 + n)
                x = slice(t * P, (t + 1) * P)
                nc.tensor.matmul(o, h_hi[:, kk, x], w_hi[:, s, w], start=kk == 0, stop=False)
                nc.tensor.matmul(o, h_lo[:, kk, x], w_hi[:, s, w], start=False, stop=False)
                ins = nc.tensor.matmul(o, h_hi[:, kk, x], w_lo[:, s, w], start=False, stop=kk == KD - 1)
            if t == NT - 1 and last:
                done.append(do(PE, ins, f"used{s}"))
            elif t % per == per - 1:
                done.append(do(PE, ins))
        return done

    def split_oh(c, value, *waits, hi=oh_hi, lo=oh_lo, free="oh"):
        t1 = act(hi[:, c, :], value, ACT.Copy, free, *waits)
        t2 = tt(lo[:, c, :], value, hi[:, c, :].bitcast(F32), sub, t1)
        return t2

    def out_step(s, ready, scale=1.0, order=(0, 1), hi=oh_hi, lo=oh_lo, free="oh", then=None):
        outs = [(t, n) for t in range(NT) for n in range(2)]

        def part(j, c, first, last):
            t, n = outs[j]
            b = 4 + j % 4
            x, w = slice(t * P, (t + 1) * P), slice(c * D + n * T, c * D + (n + 1) * T)
            nc.tensor.matmul(bank[b][:], hi[:, c, x], w_hi[:, s, w], start=first, stop=False)
            nc.tensor.matmul(bank[b][:], lo[:, c, x], w_hi[:, s, w], start=False, stop=False)
            return nc.tensor.matmul(bank[b][:], hi[:, c, x], w_lo[:, s, w], start=False, stop=last)

        def evacuate(j, done):
            t, n = outs[j]
            b = 4 + j % 4
            dst = acc[:, t, n * T:(n + 1) * T]
            e = stt(dst, bank[b][:], scale, dst, mult, add, done, "acc")
            note(f"bank{b}", e)
            return e

        if then:
            nc.scalar.preload_act_table_set("natural_log_exp_and_others")
        PE.wait(ready[0])
        for j in range(4):
            PE.wait(f"bank{4 + j}")
            part(j, order[0], True, False)
        PE.wait(ready[1])
        last = None
        for j in range(8):
            if j >= 4:
                PE.wait(f"bank{4 + j % 4}")
                part(j, order[0], True, False)
            ins = part(j, order[1], False, True)
            if j == 7:
                done = do(PE, ins, f"used{s}")
                note(free, done)
            else:
                done = do(PE, ins)
            last = evacuate(j, done)
            if then and j % 2 == 1:
                then.tile(j // 2, last)
        note("acc", last)
        if then:
            then.features()

    def wview(s, n=256):
        return w_raw[:, s, :].rearrange("p (k n) -> p k n", n=n)

    def load_columns(s, m, cols):
        v = m.rearrange("(k p) n -> p k n", p=P)
        W.load(s, [(wview(s)[:, :, c * P:(c + 1) * P], v[:, :, bass.ds(cols[c], P)]) for c in range(2)])

    def load_wide(s, m, col):
        v = m.rearrange("(k p) n -> p k n", p=P)
        W.load(s, [(wview(s)[:, c * 4:c * 4 + 4, :], v[:, c * 4:c * 4 + 4, bass.ds(col, 256)]) for c in range(2)])

    def load_rows(s, m, rows):
        W.load(s, [(w_raw[:, s, c * D:(c + 1) * D], m[bass.ds(rows[c], P), :]) for c in range(2)])

    def sigmoid_part(tmp, x, *waits):
        t = act(tmp, x, ACT.Exp, *waits, scale=-1.0)
        t = ts(tmp, tmp, 1.0, None, add, None, t)
        return recip(tmp, tmp, t)

    t_x = dma("x", acc[:], a["x"].rearrange("b (t p) d -> p (b t) d", p=P))
    k.noted["acc"] = [t_x]

    vrow = val[:, 0, 0:2 * P].rearrange("p (g n) -> p g n", n=P)
    ve_t = do(VE, nc.vector.memset(vrow, 0.0))
    do(PO, nc.gpsimd.memset(eps[:, 0:1], EPS))
    do(PO, nc.gpsimd.memset(eps[:, 1:2], LN_EPS))
    do(PO, nc.gpsimd.memset(zero8[:], 0.0))
    do(PO, nc.gpsimd.memset(alpha[:], ALPHA))
    t_eps = do(PO, nc.gpsimd.memset(eps[:, 2:3], 1.0))
    for e in (SC, VE, PE):
        e.wait(t_eps)
    vec, at = {}, 0
    SP.wait(ve_t)
    for name, src, n in (
            ("c", a["c"].rearrange("b (j p) -> (b j) p", p=P), 8),
            ("ada_b", a["ada_b"].rearrange("l (j p) -> (l j) p", p=P), 48),
            ("norm_g", a["norm_g"].rearrange("l (j p) -> (l j) p", p=P), 16),
            ("lb", a["hgrn_lb"].rearrange("l (j p) -> (l j) p", p=P), 12),
            ("onorm", a["hgrn_onorm_g"].rearrange("l (j p) -> (l j) p", p=P), 4),
            ("pool_scale", a["pool_scale"].rearrange("l (j p) -> (l j) p", p=P), 4),
            ("b_gate", a["gla_b_gate_2"].rearrange("l (j p) -> (l j) p", p=P), 4),
            ("gla_g", a["gla_norm_g_2"].rearrange("l (j p) -> (l j) p", p=P), 2)):
        t_v = dma("vec", vrow[at:at + n, 0, :], src, nc.sync)
        vec[name] = at
        at += n
    for name, src in (("qnorm", a["fox_qnorm_g"]), ("knorm", a["fox_knorm_g"])):
        for half in range(2):
            t_v = dma("vec", vrow[at:at + 1, 0, half * DH:(half + 1) * DH], src, nc.sync)
        vec[name] = at
        at += 1
    assert at <= P
    t_v = dma("vec", vrow[0:48, 1, :], a["ln_g_2"].rearrange("l m (j p) -> (l m j) p", p=P), nc.sync)
    t_v = dma("vec", vrow[48:96, 1, :], a["ln_b_2"].rearrange("l m (j p) -> (l m j) p", p=P), nc.sync)
    fb = sb("fox_b", [FOX_H, 1])
    t_fb = dma("vec", fb[:], a["fox_b_f"].rearrange("a h -> h a"), nc.sync)
    narrow_raw = sb("narrow_raw", [P, 2, KD, 16])
    for n, m in enumerate((a["odd_w_in"][0][:, 4096:4112], a["gla_w_in_2"][0][:, 3072:3088])):
        t_narrow = dma("narrow", narrow_raw[:, n, :, :], m.rearrange("(k p) n -> p k n", p=P), nc.sync)
    t_consts = dma("consts", consts[:], a["consts"], nc.scalar)
    for e in (SC, VE, PE):
        e.wait(t_fb, t_consts)
    for g in range(2):
        t_tr = do(PE, nc.tensor.transpose(bank[0][:, g * P:(g + 1) * P], vrow[:, g, :], ident))
    SC.wait(t_tr)
    t_vc = act(vcol[:].rearrange("p g n -> p (g n)"), bank[0][:, 0:2 * P], ACT.Copy)
    note("bank0", t_vc)

    def vc(name, j, n=1, g=0):
        return vcol[:, g, bass.ds(vec[name] + j, n)]

    lbt = sb("lbt", [P, 12])
    lb, oml, noml = (sb(n, [P, 4]) for n in ("lb", "oml", "noml"))
    x = [vcol[:, 0, vec["lb"] + 4 * r:vec["lb"] + 4 * r + 4] for r in range(3)]
    t = tt(lb[:], x[0], x[1], ALU.max, t_vc)
    t = tt(lb[:], lb[:], x[2], ALU.max, t)
    for r in range(3):
        t = tt(lbt[:, 4 * r:4 * r + 4], x[r], lb[:], sub, t)
    t = act(lbt[:], lbt[:], ACT.Exp, t)
    t = tt(lb[:], lbt[:, 0:4], lbt[:, 4:8], add, t)
    t = tt(lb[:], lb[:], lbt[:, 8:12], add, t)
    t = recip(lb[:], lb[:], t)
    t = tt(lb[:], lb[:], lbt[:, 0:4], mult, t)
    t_lb = ts(noml[:], lb[:], 1.0, None, sub, None, t)
    t_lb = ts(oml[:], lb[:], -1.0, 1.0, mult, add, t)

    cond = sb("cond", [P, 8])
    sg = sb("sg", [P, 8])
    t = sigmoid_part(sg[:], vc("c", 0, 8))
    t_cond = tt(cond[:], vc("c", 0, 8), sg[:], mult, t)

    mod = sb("mod", [P, 2, 24])
    first = ctx.enter_context(ExitStack())
    gate = sb("gate", [P, D], c=first)
    AR = 3
    ada_buf = ctx.enter_context(ExitStack())
    ada_loaded = [k.sem(f"s_ada_loaded{r}") for r in range(AR)]

    ada_sum = val[:, 2:4, :].rearrange("p a (j n) -> p (a j) n", n=P)

    def ada_load(i, j):
        r = j % AR
        SP.wait(f"ada{r}")
        nc.sync.dma_start(ada_raw[:, r, :].rearrange("p (k n) -> p k n", n=P),
                          a["ada_w"][1].rearrange("(k p) n -> p k n", p=P)[:, :, bass.ds(i * 768 + j * P, P)]
                          ).then_inc(ada_loaded[r], 16)

    def ada_piece(i, j):
        r = j % AR
        nc.gpsimd.wait_ge(ada_loaded[r], i * 32 + 16 * (j // AR + 1))
        w = ada_raw[:, r, :]
        t = tt(w.rearrange("p (k n) -> p k n", n=P), w.rearrange("p (k n) -> p k n", n=P),
               cond[:].unsqueeze(2).broadcast_to((P, KD, P)), mult, "ada_sum", e=PO)
        t = tt(w[:, 0:512], w[:, 0:512], w[:, 512:1024], add, t, e=PO)
        t = tt(w[:, 0:256], w[:, 0:256], w[:, 256:512], add, t, e=PO)
        t = tt(ada_sum[:, j, :], w[:, 0:P], w[:, P:2 * P], add, t, e=PO)
        note(f"ada{r}", t)
        if j + AR < 6:
            ada_load(i, j + AR)
        return t

    def ada_columns(i, b, ready):
        PE.wait(ready, f"bank{b}")
        for j in range(6):
            ins = nc.tensor.matmul(bank[b][:, j:j + 1], ada_sum[:, j, :], ones[:, 0:1], start=True, stop=True)
        t = do(PE, ins, "ada_sum")
        t = tt(mod[:, 1, bass.ds(i * 6, 6)], bank[b][:, 0:6], vc("ada_b", 24 + i * 6, 6), add, t)
        note(f"bank{b}", t)
        note("mod", t)

    even_w, odd_w = a["even_w_in"][0], a["odd_w_in"][0]

    diag4 = val[:, 3, :].rearrange("p (t n) -> p t n", n=P)

    class Boundary:

        def __init__(self, gain, shift, by_diag=False):
            self.gain, self.shift, self.by_diag = gain, shift, by_diag
            self.ready = [None] * NT

        def tile(self, t, ready):
            self.ready[t] = ready

        def features(self):
            lo4, hi4 = range(4), range(4, KD)
            order = ((0, lo4), (1, lo4), (0, hi4), (1, hi4), (2, lo4), (2, hi4), (3, lo4), (3, hi4))
            for t, chunks in order:
                PE.wait(self.ready[t])
                rhs = diag4[:, t, :] if self.by_diag else ident
                for j in chunks:
                    if t == 0:
                        PE.wait(f"bank{j}")
                    o, x = bank[j][:, t * P:(t + 1) * P], acc[:, t, j * P:(j + 1) * P]
                    if self.by_diag:
                        ins = nc.tensor.matmul(o, x, rhs, start=True, stop=True)
                    else:
                        ins = nc.tensor.transpose(o, x, rhs)
                done = do(PE, ins)
                if t == 3 and chunks is lo4:
                    done4 = done
            note("transposed", done)
            if self.by_diag:
                note("val3", done)
            g, b = self.gain, self.shift

            def parts(j):
                d = done4 if j < 4 else done
                x, v = bank[j][:], val[:, j % 4, :]
                if j % 2 == 0:
                    hi = act(h_hi[:, j, :], x, ACT.Identity, d, scale=g[:, j:j + 1], bias=b[:, j:j + 1])
                    f = act(v, x, ACT.Identity, f"val{j % 4}", scale=g[:, j:j + 1], bias=b[:, j:j + 1])
                else:
                    f = ts(v, x, g[:, j:j + 1], b[:, j:j + 1], mult, add, d, f"val{j % 4}")
                    hi = act(h_hi[:, j, :], v, ACT.Copy, f)
                note(f"bank{j}", f)
                return hi, f

            made = [parts(0)]
            for j in range(KD):
                if j + 1 < KD:
                    made.append(parts(j + 1))
                hi, f = made[j]
                t = tt(h_lo[:, j, :], val[:, j % 4, :], h_hi[:, j, :].bitcast(F32), sub, hi, f)
                note(f"val{j % 4}", t)
                note(f"h{j}", t)
            self.rest()

        def rest(self):
            pass

    class Modulated(Boundary):

        def __init__(self, l):
            t = ts(col8[:, 0, :], mod[:, l, 8:16], 1.0, None, add, None, "mod", "col8")
            self.cols = tt(col8[:, 0, :], col8[:, 0, :], vc("norm_g", l * 8, 8), mult, t)
            SC.wait(self.cols)
            super().__init__(col8[:, 0, :], mod[:, l, 0:8], by_diag=True)

        def tile(self, t, ready):
            x = stat[:, t, 0:1]
            r = act(val[:, 0:2, :], acc[:, t, :].rearrange("p (a b) -> p a b", a=2), ACT.Square, ready,
                    "val0", "val1", accum_out=x)
            note("val0", r)
            note("val1", r)
            r = act(x, x, ACT.Ln, r, scale=1.0 / D, bias=eps[:, 0:1])
            r = act(x, x, ACT.Exp, r, scale=-0.5)
            self.ready[t] = ts(diag4[:, t, :], ident, x, None, mult, None, r, "transposed")

    def spread_gate(l, banks=(0, 1)):
        v = val[:, 0:2, :].rearrange("p a (j n) -> p (a j) n", n=P)
        t = tt(v, ident.unsqueeze(1).broadcast_to((P, KD, P)),
               mod[:, l, 16:24].unsqueeze(2).broadcast_to((P, KD, P)), mult, "mod", "val0", "val1", "val2", "val3")
        for c in range(2):
            b = banks[c]
            PE.wait(t, f"bank{b}")
            tp = do(PE, nc.tensor.matmul(bank[b][:], ones, val[:, c, :], start=True, stop=True))
            note(f"val{c}", tp)
            t_g = act(gate[:, c * T:(c + 1) * T], bank[b][:], ACT.Copy, tp, "gate")
            note(f"bank{b}", t_g)
        note("gate", t_g)

    with ExitStack() as c2:
        NP = 3 * D // 256
        RING = 5
        first_w, first_sum = sb("ada_first", [P, RING, KD * 256], c=c2), sb("first_sum", [P, RING, 256], c=c2)
        w0 = a["ada_w"][0].rearrange("(k p) n -> p k n", p=P)

        def fetch(n):
            SP.wait(f"ada_free{n % RING}")
            note(f"arrived{n}", dma(f"ada_first{n % RING}", first_w[:, n % RING, :].rearrange("p (k n) -> p k n", n=256),
                                    w0[:, :, n * 256:(n + 1) * 256], nc.sync))

        for n in range(RING):
            fetch(n)

        def sum_rows(n, e):
            x, w, c0 = first_sum[:, n % RING, :], first_w[:, n % RING, :], 2 * n
            e.wait(f"arrived{n}", t_cond)
            if e is VE:
                t = ts(x, w[:, 0:256], cond[:, 0:1], None, mult, None, f"first_sum{n % RING}")
                for kk in range(1, KD):
                    t = stt(x, w[:, kk * 256:(kk + 1) * 256], cond[:, kk:kk + 1], x, mult, add, t)
            elif e is PO:
                w3 = w.rearrange("p (k n) -> p k n", n=256)
                t = tt(w3, w3, cond[:].unsqueeze(2).broadcast_to((P, KD, 256)), mult, e=PO)
                for half in (1024, 512):
                    t = tt(w[:, 0:half], w[:, 0:half], w[:, half:2 * half], add, t, e=PO)
                t = tt(x, w[:, 0:256], w[:, 256:512], add, t, f"first_sum{n % RING}", e=PO)
            else:
                for c in range(2):
                    for kk in range(KD):
                        ins = nc.tensor.matmul(bank[7][:, c0 + c:c0 + c + 1], w[:, kk * 256 + c * P:kk * 256 + (c + 1) * P],
                                               cond[:, kk:kk + 1], start=kk == 0, stop=kk == KD - 1)
                t = do(PE, ins)
            note(f"ada_free{n % RING}", t)
            if n + RING < NP:
                fetch(n + RING)
            return t

        def sum_partitions(n, t, b=7):
            PE.wait(t, f"bank{b}")
            for c in range(2):
                ins = nc.tensor.matmul(bank[b][:, 2 * n + c:2 * n + c + 1],
                                       first_sum[:, n % RING, c * P:(c + 1) * P], ones[:, 0:1], start=True, stop=True)
            return do(PE, ins, f"first_sum{n % RING}")

        def add_bias(n0, n1, t, b=7):
            cols = slice(2 * n0, 2 * n1)
            t = tt(mod[:, 0, cols], bank[b][:, cols], vc("ada_b", 2 * n0, 2 * (n1 - n0)), add, t)
            note(f"bank{b}", t)
            note("mod", t)

        for e in (SC, VE, PE):
            e.wait(t_x)
        for n in range(2 * NP // 3):
            t = sum_rows(n, PE if n % 3 == 1 else VE)
            if n % 3 != 1:
                t = sum_partitions(n, t)
        add_bias(0, 2 * NP // 3, t)
        nc.scalar.preload_act_table_set("natural_log_exp_and_others")
        start = Modulated(0)
        for t in range(NT):
            start.tile(t, None)
        sums = [sum_rows(n, VE if n < NP - 2 else PO) for n in range(2 * NP // 3, NP)]
        load_columns(0, even_w, (0, 512))
        W.convert(0)
        start.features()
        for n in range(2 * NP // 3, NP):
            t = sum_partitions(n, sums[n - 2 * NP // 3], 0)
        add_bias(2 * NP // 3, NP, t, 0)
        spread_gate(0)
    note("scratch", *k.noted["h7"], *k.noted["gate"])

    ada_raw = sb("ada_raw", [P, AR, 1024], c=ada_buf)
    PO.wait(t_cond)

    def cross_tiles(q0, kend, edge, ex, ST, vw, b0, b1, *waits):
        t1 = ts(ex[:, 0, :], q0[:, 2 * P:3 * P], edge[:, 1:2], None, mult, None, *waits)
        t2 = ts(ex[:, 1, :], q0[:, 3 * P:4 * P], edge[:, 2:3], None, mult, None)
        t3 = ts(ex[:, 2, :], ex[:, 1, :], edge[:, 1:2], None, mult, None, t2)
        PE.wait(t3, f"bank{b0}", f"bank{b1}")
        for n, (b, o, j, rhs) in enumerate(((b0, 0, 0, q0[:, P:2 * P]), (b0, 1, 0, ex[:, 0, :]), (b0, 2, 0, ex[:, 2, :]),
                             (b1, 0, 1, q0[:, 2 * P:3 * P]), (b1, 1, 1, ex[:, 1, :]),
                             (b1, 2, 2, q0[:, 3 * P:4 * P]))):
            t = do(PE, nc.tensor.matmul(bank[b][:, o * P:(o + 1) * P], kend[:, j * P:(j + 1) * P],
                                        rhs, start=True, stop=True))
        note("cross", t)
        u1 = act(ST[:, P:T], bank[b0][:, 0:3 * P], ACT.Copy, t, "pv")
        u2 = act(ST[:, 640 + P:640 + 3 * P], bank[b1][:, 0:2 * P], ACT.Copy)
        u3 = act(ST[:, 1280 + P:1280 + 2 * P], bank[b1][:, 2 * P:3 * P], ACT.Copy)
        note(f"bank{b0}", u1)
        note(f"bank{b1}", u3)
        return u3

    def diag_scores(kk, qq, b, *waits):
        PE.wait(f"bank{b}", *waits)
        for j in range(NT):
            t = nc.tensor.matmul(bank[b][:, j * P:(j + 1) * P], kk[:, j * P:(j + 1) * P],
                                 qq[:, j * P:(j + 1) * P], start=True, stop=True)
        return do(PE, t)

    def keep_diag(ST, mask, b, t):
        diag = ST.rearrange("p (j x) -> p j x", x=640)[:, :, 0:P]
        m = mask.bitcast(I32).unsqueeze(1).broadcast_to((P, NT, P))
        wait_apart(t, "diag")
        u = do(VE, nc.vector.copy_predicated(diag, m, bank[b][:].rearrange("p (j x) -> p j x", x=P)))
        note(f"bank{b}", u)
        note("diag", u)
        return u

    def masked_diag(ST, mask, kk, qq, b, *waits):
        t = diag_scores(kk, qq, b, *waits)
        return t, keep_diag(ST, mask, b, t)

    def head_values(b, v, c, ST, *waits):
        PE.wait(f"bank{b}", *waits)
        for j in range(NT):
            ins = nc.tensor.matmul(bank[b][:, j * P:T], v[:, j, c * P:(c + 1) * P],
                                   ST[:, j * 640:j * 640 + T - j * P], start=j == 0, stop=j == NT - 1)
        return do(PE, ins)

    def tile_view(x, n=P):
        return x.rearrange("p (j n) -> p j n", n=n)

    with ExitStack() as c2:
        enter_scratch()
        s_q, s_key, s_cum = (sb(n, [P, T], c=c2) for n in ("e_q", "e_key", "e_cum"))
        s_v = sb("e_v", [P, NT, P], c=c2)
        s_ga, s_ex = val[:, 1, :], val[:, 0, 0:3 * P].rearrange("p (a n) -> p a n", n=P)
        s_u = sb("e_u", [P, 2, 16 + T], c=c2)
        s_d, s_E = sb("e_d", [P, 2, T], c=c2), sb("e_E", [P, 2, T], c=c2)
        s_qs, s_ks = sb("e_qs", [P, 2, T], c=c2), sb("e_ks", [P, 2, T], c=c2)
        s_q0, s_kend = sb("e_q0", [P, T], c=c2), sb("e_kend", [P, T], c=c2)
        s_gb = s_ks[:, 0, :]
        s_f = s_kend
        s_edge = sb("e_edge", [P, NT], c=c2)
        ST = sb("e_ST", [P, NT * 640], c=c2)
        s_sq, s_rs = s_qs[:, 1, :], s_ks[:, 1, :]
        s_pw = val[:, 0, 3 * P:T]
        for x in (ST, s_qs, s_ks, s_u):
            t_z = do(PO, nc.gpsimd.memset(x[:], 0.0))
        for name in ("pv", "diag", "e_qs0", "e_qs1", "e_u"):
            note(name, t_z)

        def even_rows(i, s=2):
            load_rows(s, a["even_w_out"][0], (i * P, i * P + 512))

        def even_out(s=2, then=None):
            W.use(s)
            out_step(s, ("e_r1", "e_r0"), order=(1, 0), then=then)

        def even_body(i, more=True, late=False):
            if more:
                load_columns(0, even_w, (i * P, i * P + 512))
            load_columns(1, even_w, (i * P + 1024, i * P + 1536))
            if more:
                even_rows(i + -1)
            load_columns(1, even_w, (i * P + 2048, i * P + 2560))
            PO.wait("e_pw")
            t_pw = dma("pool_w", s_pw, a["pool_w"][0][bass.ds(i, 1)].rearrange("g c d -> (g c) d"))
            for j in range(AR):
                ada_load(i, j)
            W.convert(1)
            if more:
                W.convert(2, gate[:])
            for j in range(6):
                t_ada = ada_piece(i, j)
            W.use(0)
            tq = tf = project_pair(0, 0, 1)
            t = act(s_f[:], bank[1][:], ACT.Exp, tf, "cross", scale=-1.0)
            note("bank1", t)
            t = act(s_f[:], s_f[:], ACT.Ln, t, bias=eps[:, 2:3])
            t = act(s_f[:], s_f[:], ACT.Exp, t, scale=-1.0)
            t_key = ts(s_key[:], s_f[:], noml[:, bass.ds(i, 1)], oml[:, bass.ds(i, 1)], mult, add, t, "e_key")
            t = act(s_f[:], s_f[:], ACT.Ln, t_key, scale=oml[:, bass.ds(i, 1)], bias=lb[:, bass.ds(i, 1)])
            t_q = act(s_q[:], bank[0][:], ACT.Copy, tq, "e_q")
            note("bank0", t_q)
            VE.wait(t)
            t_cum = do(VE, nc.vector.tensor_tensor_scan(s_cum[:], const("reset128"), s_f[:], 0.0, mult, add))
            W.use(1)
            (tv,) = project_tokens(1, [2], 0, P, last=False)
            tga = project(1, 1, 3)
            t_v = act(s_v[:].rearrange("p t n -> p (t n)"), bank[2][:], ACT.Copy, tv, "e_v")
            note("bank2", t_v)
            cum4 = tile_view(s_cum[:])
            t_E = act(s_E[:, 0, :], s_cum[:], ACT.Exp, t_cum, "e_E0")
            t_q0 = tt(s_q0[:], s_q[:], s_E[:, 0, :], mult, t_E, t_q, "cross")
            t_ed = act(s_edge[:], cum4[:, :, P - 1], ACT.Exp)
            t = tt(tile_view(s_d[:, 0, :]), cum4[:, :, P - 1:P].broadcast_to((P, NT, P)), cum4, sub, "e_d0")
            t = act(s_d[:, 0, :], s_d[:, 0, :], ACT.Exp, t)
            t_kend = tt(s_kend[:], s_key[:], s_d[:, 0, :], mult, t)
            note("e_d0", t_kend)
            note("e_E0", t_kend)
            t_cr = cross_tiles(s_q0, s_kend, s_edge, s_ex, ST[:], s_v, 6, 7, t_kend, t_ed)
            W.convert(1)
            if more and not late:
                even_out()
            W.convert(0)

            def level_operands(n):
                h, z = LEVELS[n], n % 2
                nb = T // (2 * h)
                q3, k3, c3, d3, E3, qs3, ks3 = (x.rearrange("p (b n) -> p b n", n=2 * h) for x in (
                    s_q[:], s_key[:], s_cum[:], s_d[:, z, :], s_E[:, z, :], s_qs[:, z, :], s_ks[:, z, :]))
                lo_, hi_ = slice(0, h), slice(h, 2 * h)
                t = tt(d3, c3, c3[:, :, h - 1:h].broadcast_to((P, nb, 2 * h)), sub, f"e_d{z}", t_cum, e=PO)
                t1 = act(E3[:, :, hi_], d3[:, :, hi_], ACT.Exp, t, f"e_E{z}")
                t2 = act(E3[:, :, lo_], d3[:, :, lo_], ACT.Exp, scale=-1.0)
                note(f"e_d{z}", t2)
                tt(qs3[:, :, hi_], q3[:, :, hi_], E3[:, :, hi_], mult, t1, t_q, f"e_qs{z}")
                t = tt(ks3[:, :, lo_], k3[:, :, lo_], E3[:, :, lo_], mult, t2)
                note(f"e_E{z}", t)
                return t

            W.use(1)
            steps = project_steps(1, 0, 1)
            ready = level_operands(0)
            td = diag_scores(s_key[:], s_q[:], 6, t_key, t_q)
            next(steps)
            for n in range(len(LEVELS)):
                z = n % 2
                after = level_operands(n + 1) if n + 1 < len(LEVELS) else None
                u = keep_diag(ST[:], ident if n == 0 else const("level", (n - 1) * P, P), 6 + z, td)
                td = diag_scores(s_ks[:, z, :], s_qs[:, z, :], 7 - z, ready)
                note(f"e_qs{z}", td)
                ready = after
                next(steps)
            u = keep_diag(ST[:], const("level", (len(LEVELS) - 1) * P, P), 6 + len(LEVELS) % 2, td)
            tu = tgb = k.noted["project"][0]
            note("e_key", td)
            note("e_q", td)
            t = act(s_u[:, 0, 16:16 + T], bank[0][:], ACT.Copy, tu, "e_u")
            t_u = act(s_E[:, 0, :], bank[0][:], ACT.Copy, "e_E0")
            note("bank0", t_u)
            t_ga = act(s_ga, bank[3][:], ACT.Silu, tga, "e_ga")
            note("bank3", t_ga)
            t_gb = act(s_gb, bank[1][:], ACT.Silu, tgb, "e_qs0")
            note("bank1", t_gb)
            nc.scalar.preload_act_table_set("natural_log_exp_and_others")
            tp = head_values(2, s_v[:], 0, ST[:], u, t_v, t_cr)
            note("pv", tp)
            note("e_v", tp)
            tsq = act(s_sq, bank[2][:], ACT.Square, tp, "e_qs1")
            VE.wait(t_u)
            for n in range(4):
                sh = 2 ** n
                src, dst = s_u[:, n % 2, :], s_u[:, (n + 1) % 2, :]
                t = stt(dst[:, 16:16 + T], src[:, 16 - sh:16 - sh + T],
                        const("pool_on")[:, bass.ds(i * 4 + n, 1)], src[:, 16:16 + T], mult, add, t)
            pooled = s_u[:, 0, 16:16 + T]
            t = tt(s_u[:, 0, 16:32], s_u[:, 0, 16:32], const("pool_head")[:, bass.ds(i * 16, 16)], mult, t)
            t = stt(s_qs[:, 0, :], pooled, const("pool_w")[:, bass.ds(i, 1)], s_E[:, 0, :], mult, sub, t)
            note("e_E0", t)
            note("e_u", t)
            PE.wait(t, "bank0", t_pw)
            t = do(PE, nc.tensor.matmul(bank[0][:], s_pw, s_qs[:, 0, :], start=True, stop=True))
            note("e_pw", t)
            t = stt(s_gb, bank[0][:], vc("pool_scale", i), s_gb, mult, mult, t, t_gb)
            note("bank0", t)
            t_gb = t
            PE.wait(tsq, "bank3")
            t = do(PE, nc.tensor.matmul(bank[3][:], ones, s_sq, start=True, stop=True))
            if late:
                even_rows(i, 1)
                W.convert(1, gate[:])
                even_out()
            t = act(s_rs, bank[3][:], ACT.Ln, t, scale=1.0 / P, bias=eps[:, 0:1])
            note("bank3", t)
            t = act(s_rs, s_rs, ACT.Exp, t, scale=-0.5)
            t = stt(s_rs, bank[2][:], vc("onorm", i), s_rs, mult, mult, t)
            note("bank2", t)
            t = tt(s_ga, s_ga, s_rs, mult, t, t_ga)
            note("e_qs1", t)
            r1 = split_oh(1, s_gb, t_gb)
            note("e_qs0", r1)
            note("e_r1", r1)
            r0 = split_oh(0, s_ga, t)
            note("e_ga", r0)
            note("e_r0", r0)
            ada_columns(i, 7, t_ada)

        nc.scalar.preload_act_table_set("natural_log_exp_and_others")
        even_body(0, more=False)
        with k.rounds("even", NH - 2, [0, 1, 2, 1]) as i:
            even_body(i + 1)
        even_body(NH - 1, late=True)
        even_out(1, then=Modulated(1))
    note("scratch", *k.noted["h7"])

    ada_buf.close()

    def narrow(n, b):
        hi, lo = (x[:].rearrange("p c (j n) -> p (c j) n", n=P) for x in (oh_hi, oh_lo))
        VE.wait("oh")
        t1 = do(VE, nc.vector.memset(oh_hi[:].bitcast(F32), 0.0))
        t2 = do(VE, nc.vector.memset(oh_lo[:].bitcast(F32), 0.0))
        t3 = act(hi[:, :, 0:16], narrow_raw[:, n, :, :], ACT.Copy, t_narrow, t1, t2)
        t4 = tt(lo[:, :, 0:16], narrow_raw[:, n, :, :], hi[:, :, 0:16].bitcast(F32), sub, t2, t3)
        PE.wait(t4, "h7", f"bank{b}")
        for kk in range(KD):
            ins = three(bank[b][:], hi[:, kk, :], lo[:, kk, :], h_hi[:, kk, :], h_lo[:, kk, :],
                        kk == 0, kk == KD - 1)
        return do(PE, ins, "oh")

    def log_sigmoid(out, tmp, xb, *waits):
        t = act(tmp, xb, ACT.Abs, *waits)
        t = act(tmp, tmp, ACT.Exp, t, scale=-1.0)
        t = act(tmp, tmp, ACT.Ln, t, bias=eps[0:tmp.shape[0], 2:3])
        return stt(out, xb, 0.0, tmp, ALU.min, sub, t)

    with ExitStack() as c2:
        enter_scratch()
        cum = sb("o_cum", [FOX_H, T], c=c2)
        gq8 = sb("o_gq8", [P, 1], c=c2)
        t_gq = ts(gq8[:], vc("qnorm", 0), DH ** -0.5, None, mult, None)
        o_qn, o_kn = sb("o_qn", [P, 2, T], c=c2), sb("o_kn", [P, 2, T], c=c2)
        o_v, o_g = sb("o_v", [P, NT, 256], c=c2), sb("o_g", [P, NT, 256], c=c2)
        o_S, o_PT = sb("o_S", [P, 3, 2, T], c=c2), sb("o_PT", [P, 2, T], c=c2)
        o_sq, o_rs = o_S[:, 0, :, :], o_PT
        o_row, o_bias = sb("o_row", [FOX_H, 2, T], c=c2), sb("o_bias", [P, 4, T], c=c2)
        o_m, o_l = sb("o_m", [P, 16], c=c2), sb("o_l", [P, 16], c=c2)

        def forget_gates():
            xb, tmp, lf = o_S[0:FOX_H, 1, 0, :], o_S[0:FOX_H, 1, 1, :], o_S[0:FOX_H, 2, 0, :]
            t = narrow(0, 7)
            t = act(xb, bank[7][0:FOX_H, :], ACT.Identity, t, bias=fb[:, 0:1])
            note("bank7", t)
            t = log_sigmoid(lf, tmp, xb, t)
            VE.wait(t)
            t1 = do(VE, nc.vector.memset(tmp, 1.0))
            VE.wait(t1, t)
            t = do(VE, nc.vector.tensor_tensor_scan(cum[:], tmp, lf, 0.0, mult, add))
            for name in ("o_cum", "o_S1", "o_S2"):
                note(name, t)

        def head_norm(dst, g, src, b, *waits):
            tb = []
            for c in range(2):
                t = act(o_sq[:, c, :], bank[src + c][:], ACT.Square, waits[c], "o_S0")
                PE.wait(t, f"bank{b + c}")
                tb.append(do(PE, nc.tensor.matmul(bank[b + c][:], const("block_ones"), o_sq[:, c, :],
                                                  start=True, stop=True)))
            note("o_S0", *tb)
            for c in range(2):
                t = act(o_rs[:, c, :], bank[b + c][:], ACT.Ln, tb[c], f"o_PT{c}", scale=1.0 / DH, bias=eps[:, 0:1])
                note(f"bank{b + c}", t)
                t = act(o_rs[:, c, :], o_rs[:, c, :], ACT.Exp, t, scale=-0.5)
                t = stt(dst[:, c, :], bank[src + c][:], g, o_rs[:, c, :], mult, mult, t, "o_qk")
                note(f"bank{src + c}", t)
                note(f"o_PT{c}", t)
            return t

        def odd_body(i, first=False, then=None):
            for s, col in ((0, 0), (1, 1024), (2, 2048), (0, 3072)):
                load_wide(s, odd_w, i * 256 + col)
            load_rows(1, a["odd_w_out"][0], (i * 256, i * 256 + P))
            W.convert(1)
            W.use(0)
            tq = project_pair(0, 0, 1)
            if first:
                spread_gate(1, banks=(4, 5))
                forget_gates()
            W.convert(2)
            W.use(1)
            tk = project_pair(1, 2, 3)
            for hh in range(4):
                z = hh % 2
                t = ts(o_row[:, z, :], cum[:], ident[0:FOX_H, bass.ds(i * 4 + hh, 1)], -1.0, mult, mult,
                       f"o_row{z}", "o_cum")
                PE.wait(t, f"bank{4 + z}")
                t = do(PE, nc.tensor.matmul(bank[4 + z][:], ones[0:FOX_H, :], o_row[:, z, :], start=True, stop=True),
                       f"o_row{z}")
                t_bias = act(o_bias[:, hh, :], bank[4 + z][:], ACT.Copy, t, "o_bias")
                note(f"bank{4 + z}", t_bias)
            t_qn = head_norm(o_qn, gq8[:, 0:1], 0, 4, tq, tq)
            W.convert(0)
            W.use(2)
            tv = project_tokens(2, (6, 7))
            t_kn = head_norm(o_kn, vc("knorm", 0), 2, 4, tk, tk)
            for c in range(2):
                t_v = act(o_v[:, 2 * c:2 * c + 2, :].rearrange("p t n -> p (t n)"), bank[6 + c][:], ACT.Copy,
                          tv[c], "o_v")
                note(f"bank{6 + c}", t_v)
            W.convert(1, gate[:])
            W.use(0)
            tg = project_tokens(0, (0, 1))
            for c in range(2):
                t_g = act(o_g[:, 2 * c:2 * c + 2, :].rearrange("p t n -> p (t n)"), bank[c][:], ACT.Silu,
                          tg[c], "o_g")
                note(f"bank{c}", t_g)
            nc.scalar.preload_act_table_set("natural_log_exp_and_others")

            def scores(n):
                t, pair = n // 2, n % 2
                w, z, b = (t + 1) * P, n % 3, 4 + 2 * (n % 2)
                PE.wait(f"bank{b}", f"bank{b + 1}", t_qn, t_kn)
                for e in range(2):
                    rows = slice(e * DH, (e + 1) * DH)
                    x = nc.tensor.matmul(bank[b + e][:, 0:w], o_qn[rows, pair, t * P:w],
                                         o_kn[rows, pair, 0:w], start=True, stop=True)
                x = do(PE, x)
                S = o_S[:, z, :, 0:w]
                y = tt(S, psum[:, b:b + 2, 0:w], o_bias[:, 2 * pair:2 * pair + 2, 0:w], add, x, f"o_S{z}", t_bias)
                note(f"bank{b}", y)
                note(f"bank{b + 1}", y)
                d = o_S[:, z, :, t * P:w]
                y = tt(d, d, const("causal_add").unsqueeze(1).broadcast_to((P, 2, P)), add, y)
                VE.wait(y)
                m = o_m[:, 2 * n:2 * n + 2]
                y = do(VE, nc.vector.tensor_reduce(m, S, AX, ALU.max))
                return ts(m, m, -1.0, None, mult, None, y)

            def exps(n, y):
                w, z, m = (n // 2 + 1) * P, n % 3, o_m[:, 2 * n:2 * n + 2]
                for e in range(2):
                    y = act(o_S[:, z, e, 0:w], o_S[:, z, e, 0:w], ACT.Exp, y, bias=m[:, e:e + 1],
                            accum_out=o_l[:, 2 * n + e:2 * n + e + 1])
                return y

            def turn(n, e_done):
                t, z = n // 2, n % 3
                w = (t + 1) * P
                PE.wait(e_done)
                xs = []
                for e in range(2):
                    PE.wait(f"bank{e}")
                    for j in range(t + 1):
                        x = nc.tensor.transpose(bank[e][:, j * P:(j + 1) * P],
                                                o_S[:, z, e, j * P:(j + 1) * P], ident)
                    xs.append(do(PE, x))
                note(f"o_S{z}", xs[1])
                for e in range(2):
                    xs[e] = act(o_PT[:, e, 0:w], bank[e][:, 0:w], ACT.Copy, xs[e], f"o_PT{e}")
                    note(f"bank{e}", xs[e])
                return xs

            def values(n, xs):
                t, pair = n // 2, n % 2
                ob = 2 + t % 2
                if pair == 0:
                    PE.wait(f"bank{ob}")
                for e in range(2):
                    PE.wait(xs[e], t_v)
                    col = (2 * pair + e) * DH
                    for j in range(t + 1):
                        x = nc.tensor.matmul(bank[ob][:, col:col + DH], o_PT[:, e, j * P:(j + 1) * P],
                                             o_v[:, j, (2 * pair + e) * DH:(2 * pair + e + 1) * DH],
                                             start=j == 0, stop=j == t)
                    x = do(PE, x, f"o_PT{e}")
                if pair == 1:
                    o3 = bank[ob][:, 0:256].rearrange("p (h d) -> p h d", d=DH)
                    l4 = o_l[:, t * 4:t * 4 + 4]
                    r = recip(l4, l4, ahead[n])
                    g3 = o_g[:, t, :].rearrange("p (h d) -> p h d", d=DH)
                    q = tt(g3, g3, l4.unsqueeze(2).broadcast_to((P, 4, DH)), mult, r, t_g)
                    q = tt(g3, o3, g3, mult, x, q)
                    note(f"bank{ob}", q)
                    ready.append(q)

            ahead, ready = [], []
            for n in range(8 + 2):
                if n >= 2:
                    turned = turn(n - 2, ahead[n - 2])
                if n < 8:
                    largest = scores(n)
                if n >= 2:
                    values(n - 2, turned)
                if n < 8:
                    ahead.append(exps(n, largest))
            note("o_bias", ahead[-1])
            note("o_qk", k.noted["o_PT1"][0])
            note("o_v", k.noted["o_PT1"][0])
            PE.wait("bank4", "bank5", ready[-1])
            for c in range(2):
                for t in range(NT):
                    x = do(PE, nc.tensor.transpose(bank[4 + c][:, t * P:(t + 1) * P],
                                                   o_g[:, t, c * P:(c + 1) * P], ident))
                r = split_oh(c, bank[4 + c][:], x)
                note(f"bank{4 + c}", r)
                if c == 0:
                    r0 = r
            note("o_g", x)
            W.convert(0)
            W.use(1)
            out_step(1, (r0, r), then=then)

        class Plain(Boundary):

            def rest(self):
                PO.wait("transposed")
                note("acc", do(PO, nc.gpsimd.tensor_tensor(
                    acc[:], acc[:], alpha[:, 0:1].unsqueeze(2).broadcast_to((P, NT, D)), mult)))

        odd_body(0, first=True)
        with k.rounds("odd", 2, [0, 1, 2, 0, 1]) as i:
            odd_body(i + 1)
        odd_body(3, then=Plain(const("ones"), zero8))
        note("scratch", *k.noted["h7"])
    first.close()

    lng, lnb = sb("lng", [P, D]), sb("lnb", [P, D])

    class LayerNorm(Boundary):

        def __init__(self, l, m, final=False):
            at = (l * 3 + m) * KD
            self.final, self.out = final, []
            PO.wait("ln_vec")
            dma("ln_vec", lng[:], a["ln_g_2"][l, m].partition_broadcast(P))
            self.vec = dma("ln_vec", lnb[:], a["ln_b_2"][l, m].partition_broadcast(P))
            super().__init__(vcol[:, 1, at:at + 8], vcol[:, 1, 48 + at:56 + at])

        def begin(self):
            if not self.final:
                act(lng[:], lng[:], ACT.Copy, self.vec, scale=ALPHA)
                self.vec = act(lnb[:], lnb[:], ACT.Copy, scale=ALPHA)
            return self

        def tile(self, t, ready):
            s = stat[:, t, :]
            VE.wait(ready)
            for n in range(2):
                r = do(VE, nc.vector.bn_stats(s[:, 6 * n:6 * n + 6], acc[:, t, n * T:(n + 1) * T]))
            VE.wait(r)
            r = do(VE, nc.vector.bn_aggr(s[:, 12:14], s[:, 0:12]))
            mean, rstd, shift = s[:, 12:13], s[:, 14:15], s[:, 15:16]
            r = act(rstd, s[:, 13:14], ACT.Ln, r, bias=eps[:, 1:2])
            r = act(rstd, rstd, ACT.Exp, r, scale=-0.5)
            if not self.final:
                r = stt(shift, mean, -1.0, rstd, mult, mult, r)
                self.ready[t] = act(acc[:, t, :], acc[:, t, :], ACT.Identity, r, scale=rstd, bias=shift)
                return
            r = stt(acc[:, t, :], acc[:, t, :], mean, lng[:], sub, mult, r, self.vec)
            r = stt(acc[:, t, :], acc[:, t, :], rstd, lnb[:], mult, add, r)
            SP.wait(r)
            self.out.append(dma("out", a["out"].rearrange("b (t p) d -> t p (b d)", p=P)[t], acc[:, t, :], nc.sync))

        def features(self):
            if self.final:
                SP.wait(self.out[-1])
            else:
                super().features()

        def rest(self):
            for t in range(NT):
                g = tt(acc[:, t, :], acc[:, t, :], lng[:], mult, "transposed", self.vec, e=PO)
                g = tt(acc[:, t, :], acc[:, t, :], lnb[:], add, g, e=PO)
            note("acc", g)
            note("ln_vec", g)

    def ffn(l, w):
        with ExitStack() as c2:
            enter_scratch()
            f_s, f_h = sb(f"f_s{l}{w}", [P, 2, T], c=c2), sb(f"f_h{l}{w}", [P, 2, T], c=c2)
            ffn_rounds(f_s, f_h, l, w)
            note("scratch", *k.noted["h7"])

    def ffn_rounds(f_s, f_h, l, w):
        w_in, w_out = a["ffn_w_in_2"][l, w], a["ffn_w_out_2"][l, w]

        def hidden(s):
            tg = tu = project_pair(s, 2 * s, 2 * s + 1)
            t = act(f_s[:, s, :], bank[2 * s][:], ACT.Silu, tg, f"f_h{s}")
            note(f"bank{2 * s}", t)
            t = tt(f_h[:, s, :], f_s[:, s, :], bank[2 * s + 1][:], mult, t, tu)
            note(f"bank{2 * s + 1}", t)
            r = split_oh(s, f_h[:, s, :], t)
            note(f"f_h{s}", r)
            return r

        def body(i, more=True, then=None):
            load_columns(0, w_in, (i * 256, i * 256 + DFF))
            load_columns(1, w_in, (i * 256 + P, i * 256 + P + DFF))
            load_rows(2, w_out, (i * 256, i * 256 + P))
            W.convert(1)
            W.convert(2)
            W.use(0)
            r0 = hidden(0)
            if more:
                W.convert(0)
            W.use(1)
            r1 = hidden(1)
            W.use(2)
            out_step(2, (r0, r1), scale=0.5, then=then)

        n = DFF // 256
        final = (l, w) == (1, 1)
        nc.scalar.preload_act_table(ACT.Silu)
        then = LayerNorm(l, 2 * w, final)
        body(0)
        with k.rounds(f"ffn{l}{w}", n - 2, [0, 1, 2]) as i:
            body(i + 1)
        body(n - 1, more=not final, then=then.begin())

    def gla():
        m = a["gla_w_in_2"][0]
        with ExitStack() as c2:
            enter_scratch()
            low = sb("g_low", [16, T], c=c2)
            g_wg = sb("g_wg", [16, P], c=c2)
            g_q, g_k, g_x, g_l, g_c64, g_c128 = (sb("g_" + n, [P, T], c=c2)
                                                for n in ("q", "k", "x", "l", "c64", "c128"))
            g_v, g_r = sb("g_v", [P, NT, 256], c=c2), val[:, 1:3, :]
            g_E, g_d = sb("g_E", [P, 3, T], c=c2), sb("g_d", [P, 2, T], c=c2)
            g_qd, g_kinv, g_k64, g_q0, g_kend = (sb("g_" + n, [P, T], c=c2)
                                                for n in ("qd", "kinv", "k64", "q0", "kend"))
            g_ex, g_edge = val[:, 0, 0:3 * P].rearrange("p (a n) -> p a n", n=P), sb("g_edge", [P, NT], c=c2)
            ST = sb("g_ST", [P, NT * 640], c=c2)
            g_sq, g_rs = g_d, g_x
            t_z = do(VE, nc.vector.memset(ST[:], 0.0))
            SC.wait(t_z); VE.wait(t_z)
            nc.scalar.preload_act_table_set("natural_log_exp_and_others")

            def rows(i, s=2):
                load_rows(s, a["gla_w_out_2"][0], (i * 256, i * 256 + P))

            def body(i, more=True, late=False):
                b_o = 2 if late else 6
                load_columns(0, m, (i * P, i * P + 512))
                load_wide(1, m, i * 256 + 1024)
                if more:
                    rows(i + -1)
                load_wide(1, m, i * 256 + 2048)
                PO.wait("g_wg")
                t_wg = dma("w_gate", g_wg[:], a["gla_w_gate_2"][0][:, bass.ds(i * P, P)])
                W.convert(1)
                if more:
                    W.convert(2)
                W.use(0)
                tq = tk = project_pair(0, 0, 1)
                if not more:
                    note("g_low", act(low[:], bank[3][0:16, :], ACT.Copy, narrow(1, 3)))
                    note("bank3", *k.noted["g_low"])
                PE.wait("g_low", t_wg, "bank2")
                t = do(PE, nc.tensor.matmul(bank[2][:], g_wg[:], low[:], start=True, stop=True), "g_wg")
                t = act(g_x[:], bank[2][:], ACT.Identity, t, "g_x", bias=vc("b_gate", i))
                note("bank2", t)
                t = log_sigmoid(g_l[:], g_E[:, 0, :], g_x[:], t, "g_E")
                note("g_x", t)
                VE.wait(t, "g_c")
                do(VE, nc.vector.tensor_tensor_scan(g_c64[:], const("reset64"), g_l[:], 0.0, mult, add))
                t_c = do(VE, nc.vector.tensor_tensor_scan(g_c128[:], const("reset128"), g_l[:], 0.0, mult, add))
                t_q = act(g_q[:], bank[0][:], ACT.Copy, tq, "g_q", scale=P ** -0.5)
                note("bank0", t_q)
                t_k = act(g_k[:], bank[1][:], ACT.Copy, tk, "g_k")
                note("bank1", t_k)
                W.use(1)
                tv = project_tokens(1, (4, 5))
                s16 = 1.0 / 16.0
                te = act(g_E[:, 0, :], g_c64[:], ACT.Exp, t_c, scale=s16)
                t_qd = tt(g_qd[:], g_q[:], g_E[:, 0, :], mult, te, t_q, "g_diag")
                te = act(g_E[:, 1, :], g_c64[:], ACT.Exp, scale=-s16)
                t_ki = tt(g_kinv[:], g_k[:], g_E[:, 1, :], mult, te, t_k)
                te = act(g_E[:, 2, :], g_c128[:], ACT.Exp, scale=s16)
                t_q0 = tt(g_q0[:], g_q[:], g_E[:, 2, :], mult, te, "cross")
                c8, c4 = tile_view(g_c64[:], 64), tile_view(g_c128[:])
                t = tt(tile_view(g_d[:, 0, :], 64), c8[:, :, 63:64].broadcast_to((P, 8, 64)), c8, sub, "g_sq")
                t = act(g_d[:, 0, :], g_d[:, 0, :], ACT.Exp, t, scale=s16)
                t_k64 = tt(g_k64[:], g_k[:], g_d[:, 0, :], mult, t)
                t = tt(tile_view(g_d[:, 1, :]), c4[:, :, P - 1:P].broadcast_to((P, NT, P)), c4, sub)
                t = act(g_d[:, 1, :], g_d[:, 1, :], ACT.Exp, t, scale=s16)
                t_ed = act(g_edge[:], c4[:, :, P - 1], ACT.Exp, scale=s16)
                note("g_c", t_ed)
                t_kend = tt(g_kend[:], g_k[:], g_d[:, 1, :], mult, t)
                note("g_E", t_kend)
                note("g_q", t_kend)
                note("g_k", t_kend)
                for c in range(2):
                    t_v = act(g_v[:, 2 * c:2 * c + 2, :].rearrange("p t n -> p (t n)"), bank[4 + c][:],
                              ACT.Copy, tv[c], "pv")
                    note(f"bank{4 + c}", t_v)
                W.convert(1)
                if more and not late:
                    W.use(2)
                    out_step(2, ("g_r0", "g_r1"))
                W.convert(0)
                W.use(1)
                tr = project_pair(1, 2, 3)
                cross_tiles(g_q0, g_kend, g_edge, g_ex, ST[:], g_v, 4, 5, t_kend, t_ed)
                masked_diag(ST[:], const("chunk_causal"), g_kinv[:], g_qd[:], 6, t_ki)
                tp, u = masked_diag(ST[:], const("level", 6 * P, P), g_k64[:], g_qd[:], 7, t_k64)
                note("g_diag", tp)
                for c in range(2):
                    t_r = act(g_r[:, c, :], bank[2 + c][:], ACT.Silu, tr, "g_r")
                    note(f"bank{2 + c}", t_r)
                nc.scalar.preload_act_table_set("natural_log_exp_and_others")
                tsq = []
                PE.wait(t_v, *k.noted["bank5"], *k.noted["bank4"])
                for c in range(2):
                    tp = head_values(b_o + c, g_v[:], c, ST[:], u)
                    tsq.append(act(g_sq[:, c, :], bank[b_o + c][:], ACT.Square, tp, "g_E", "g_sq"))
                note("pv", tp)
                PE.wait("bank0")
                for c in range(2):
                    PE.wait(tsq[c])
                    ins = nc.tensor.matmul(bank[0][:], ones, g_sq[:, c, :], start=c == 0, stop=c == 1)
                t = do(PE, ins, "g_sq")
                if late:
                    rows(i, 1)
                    W.convert(1)
                    W.use(2)
                    out_step(2, ("g_r0", "g_r1"))
                t = act(g_rs[:], bank[0][:], ACT.Ln, t, scale=1.0 / 256, bias=eps[:, 0:1])
                note("bank0", t)
                t = act(g_rs[:], g_rs[:], ACT.Exp, t, scale=-0.5)
                r = []
                for c in range(2):
                    u = stt(g_sq[:, c, :], bank[b_o + c][:], vc("gla_g", c), g_rs[:], mult, mult, t, "g_sq")
                    note(f"bank{b_o + c}", u)
                    u = tt(g_r[:, c, :], g_r[:, c, :], g_sq[:, c, :], mult, u, t_r)
                    r.append(split_oh(c, g_r[:, c, :], u))
                note("g_x", u)
                note("g_sq", u)
                note("g_r", r[1])
                note("g_r0", r[0])
                note("g_r1", r[1])

            then = LayerNorm(0, 1)
            body(0, more=False)
            with k.rounds("gla", NH - 2, [0, 1, 2, 1]) as i:
                body(i + 1)
            body(NH - 1, late=True)
            W.use(1)
            out_step(1, ("g_r0", "g_r1"), then=then.begin())
            note("scratch", *k.noted["h7"])

    def retention():
        m = a["ret_w_in_2"][0]
        with ExitStack() as c2:
            enter_scratch()
            cos, dec = sb("r_cos", [P, T], c=c2), sb("r_dec", [P, NH, T], c=c2)
            sin, ng = val[:, 3, :], val[:, 2, :]
            dma("rope", cos[:], a["rope"][:, 0, :], nc.scalar)
            t1 = dma("rope", sin, a["rope"][:, 1, :], nc.scalar)
            t2 = dma("decay", dec[:], a["ret_decay"], nc.scalar)
            t3 = dma("ret_g", ng, a["ret_norm_g_2"][0].partition_broadcast(P), nc.scalar)
            VE.wait(t1, t2, t3)
            qr, kr = sb("r_q", [P, 2, T], c=c2), sb("r_k", [P, 2, T], c=c2)
            r_t = val
            r_v, r_g = sb("r_v", [P, NT, T], c=c2), sb("r_g", [P, NT, T], c=c2)
            ST = sb("r_ST", [P, NT, T], c=c2)
            o2_hi, o2_lo = sb("o2_hi", [P, 2, T], F32R, c2), sb("o2_lo", [P, 2, T], F32R, c2)
            nc.scalar.preload_act_table_set("natural_log_exp_and_others")

            def rotate(dst, b, tks, *waits):
                x1, x2 = bank[b][:], bank[b + 1][:]
                t = tt(dst[:, 0, :], x1, cos[:], mult, *tks, *waits)
                u = tt(r_t[:, 0, :], x2, sin, mult)
                t = tt(dst[:, 0, :], dst[:, 0, :], r_t[:, 0, :], sub, u)
                t = tt(dst[:, 1, :], x1, sin, mult)
                note(f"bank{b}", t)
                u = tt(r_t[:, 1, :], x2, cos[:], mult)
                note(f"bank{b + 1}", u)
                return tt(dst[:, 1, :], dst[:, 1, :], r_t[:, 1, :], add, u)

            def rows(i, s, half):
                load_rows(s, a["ret_w_out_2"][0], (i * 512 + half * 256, i * 512 + half * 256 + P))

            def turn_out():
                PE.wait("r_values")
                for c in range(4):
                    PE.wait(f"bank{4 + c}")
                    for q in range(NT):
                        x = do(PE, nc.tensor.transpose(bank[4 + c][:, q * P:(q + 1) * P],
                                                       r_g[:, q, c * P:(c + 1) * P], ident))
                    own = {} if c < 2 else {"hi": o2_hi, "lo": o2_lo, "free": "o2"}
                    r = split_oh(c % 2, bank[4 + c][:], x, **own)
                    note(f"bank{4 + c}", r)
                    note(f"r_o{c}", r)
                note("r_g", x)

            def out_half(s, half, then=None):
                W.use(s)
                if half == 0:
                    out_step(s, ("r_o0", "r_o1"))
                else:
                    out_step(s, ("r_o2", "r_o3"), hi=o2_hi, lo=o2_lo, free="o2", then=then)

            def body(i, more=True):
                load_wide(0, m, i * 256)
                load_wide(1, m, i * 256 + 1024)
                if more:
                    rows(i + -1, 2, 0)
                    rows(i + -1, 0, 1)
                for s, col in ((1, 2048), (2, 2304), (0, 4096), (1, 4352)):
                    load_wide(s, m, i * 512 + col)
                W.convert(1)
                W.use(0)
                tq = [project_pair(0, 0, 1)]
                t_q = rotate(qr, 0, tq, "r_qk")
                if more:
                    W.convert(2)
                    turn_out()
                W.use(1)
                tk = [project_pair(1, 2, 3)]
                t_k = rotate(kr, 2, tk)
                if more:
                    W.convert(0)
                    out_half(2, 0)
                    W.convert(1)
                    out_half(0, 1)
                else:
                    W.convert(1)
                for half in range(2):
                    W.convert((2, 0)[half])
                    W.use(1 + half)
                    tv = project_tokens(1 + half, (4 + 2 * half, 5 + 2 * half))
                    for c in range(2):
                        b = 4 + 2 * half + c
                        t_v = act(r_v[:, 2 * c:2 * c + 2, half * 256:half * 256 + 256],
                                  bank[b][:].rearrange("p (t n) -> p t n", n=256), ACT.Copy, tv[c], "pv")
                        note(f"bank{b}", t_v)
                for half in range(2):
                    W.convert((1, 0)[half])
                    W.use(half)
                    tg = project_tokens(half, (0 + 2 * half, 1 + 2 * half))
                    for c in range(2):
                        b = 2 * half + c
                        g = r_g[:, 2 * c:2 * c + 2, half * 256:half * 256 + 256]
                        x = bank[b][:].rearrange("p (t n) -> p t n", n=256)
                        t_g = act(g, x, ACT.Silu, tg[c], "r_g")
                        note(f"bank{b}", t_g)
                nc.scalar.preload_act_table_set("natural_log_exp_and_others")
                for j in range(NT):
                    PE.wait(f"bank{4 + j}", t_q, t_k)
                    w = T - j * P
                    for c in range(2):
                        ins = nc.tensor.matmul(bank[4 + j][:, 0:w], kr[:, c, j * P:(j + 1) * P],
                                               qr[:, c, j * P:T], start=c == 0, stop=c == 1)
                    t = do(PE, ins)
                    t_S = tt(ST[:, j, 0:w], bank[4 + j][:, 0:w],
                             dec[:, bass.ds(i, 1), 0:w].rearrange("p a w -> p (a w)"), mult, t, "pv")
                    note(f"bank{4 + j}", t_S)
                note("r_qk", t)
                PE.wait(t_S, t_v)
                for q in range(NT):
                    PE.wait(f"bank{q}")
                    for j in range(q + 1):
                        ins = nc.tensor.matmul(bank[q][:], ST[:, j, (q - j) * P:(q - j + 1) * P], r_v[:, j, :],
                                               start=j == 0, stop=j == q)
                    tp = do(PE, ins)
                    VE.wait(tp)
                    t = do(VE, nc.vector.bn_stats(stat[:, q, 0:6], bank[q][:]))
                    wait_apart(t)
                    t = do(VE, nc.vector.bn_aggr(stat[:, q, 12:14], stat[:, q, 0:6]))
                    t = act(stat[:, q, 14:15], stat[:, q, 13:14], ACT.Ln, t, bias=eps[:, 0:1])
                    t = act(stat[:, q, 14:15], stat[:, q, 14:15], ACT.Exp, t, scale=-0.5)
                    t = ts(r_t[:, q % 2, :], bank[q][:], stat[:, q, 12:13], stat[:, q, 14:15], sub, mult, t)
                    note(f"bank{q}", t)
                    t = tt(r_t[:, q % 2, :], r_t[:, q % 2, :], ng, mult, t)
                    t = tt(r_g[:, q, :], r_g[:, q, :], r_t[:, q % 2, :], mult, t, t_g)
                note("pv", tp)
                note("r_values", t)

            then = LayerNorm(1, 1)
            body(0, more=False)
            with k.rounds("ret", NH - 1, [0, 1, 2, 0, 1, 2, 0, 1]) as i:
                body(i + 1)
            rows(NH - 1, 2, 0)
            rows(NH - 1, 1, 1)
            W.convert(2)
            W.convert(1)
            turn_out()
            out_half(2, 0)
            then.begin()
            out_half(1, 1, then=then)
            note("scratch", *k.noted["h7"])

    ffn(0, 0)
    gla()
    ffn(0, 1)
    ffn(1, 0)
    retention()
    ffn(1, 1)


_INS = ["x", "c", "norm_g", "ada_w", "ada_b", "hgrn_lb", "even_w_in", "hgrn_onorm_g", "pool_w", "pool_scale",
        "even_w_out", "odd_w_in", "fox_b_f", "fox_qnorm_g", "fox_knorm_g", "odd_w_out", "ffn_w_in_2",
        "ffn_w_out_2", "ln_g_2", "ln_b_2", "gla_w_in_2", "gla_w_gate_2", "gla_b_gate_2", "gla_norm_g_2",
        "gla_w_out_2", "ret_w_in_2", "ret_norm_g_2", "ret_w_out_2"]


def kernel(**inputs):
    import numpy as _np
    import concourse.bacc as _bacc
    from concourse import mybir as _mybir
    from concourse.bass_utils import run_bass_kernel_spmd as _run

    arrays = {n: _np.ascontiguousarray(inputs[n]) for n in _INS}
    arrays.update(constant_tables())
    counts = {}
    for _ in range(2):
        nc = _bacc.Bacc("TRN2", target_bir_lowering=False, num_devices=1)
        dt = _mybir.dt.float32
        a = {n: nc.dram_tensor(f"in_{n}", v.shape, dt, kind="ExternalInput").ap() for n, v in arrays.items()}
        a["out"] = nc.dram_tensor("out", (1, T, D), dt, kind="ExternalOutput").ap()
        counts = build(nc, a, counts)
    r = _run(nc, [{f"in_{n}": v for n, v in arrays.items()}], core_ids=[0])
    return r.results[0]["out"]
```
